# Optimizing a Trainium2 kernel written in Bass

```python
import jax, jax.numpy as jnp
from jax import lax
import numpy as np

D_MODEL = 1024
BATCH = 1
SEQ = 1024
DEPTH = 1

GRID_W = 64
D_MIX = D_MODEL
D_ATTN = D_MIX // 2
D_FOUR = D_MIX - D_ATTN
N_HEADS_A = 8
HEAD_DIM = D_ATTN // N_HEADS_A
WIN_H = 8
WIN_W = 16
N_FOUR_GROUPS = 8
FOUR_GROUP_DIM = D_FOUR // N_FOUR_GROUPS
D_PROJ = 3 * D_ATTN + D_FOUR
N_EXPERT_GROUPS = 4
EXPERTS_PER_GROUP = 8
N_EXPERTS = N_EXPERT_GROUPS * EXPERTS_PER_GROUP
TOP_K_FINE = 2
D_EXPERT = D_MODEL // 4
RMS_EPS = 1e-6

kernel_name = "hymba_natten_fnet_hiermoe_encoder"

def rmsnorm(x, g):
    xf = x.astype(jnp.float32)
    y = xf * lax.rsqrt(jnp.mean(xf * xf, axis=-1, keepdims=True) + RMS_EPS)
    return (y * g.astype(jnp.float32)).astype(x.dtype)

def neighbourhood_attention(q, k, v, rpb):
    b, t, h, dh = q.shape
    rows = t // GRID_W
    kh = min(WIN_H, rows)
    q = q.reshape(b, rows, GRID_W, h, dh)
    k = k.reshape(b, rows, GRID_W, h, dh)
    v = v.reshape(b, rows, GRID_W, h, dh)
    cols = jnp.arange(GRID_W)
    col_start = jnp.clip(cols - WIN_W // 2, 0, GRID_W - WIN_W)
    col_idx = col_start[:, None] + jnp.arange(WIN_W)[None, :]
    dc = col_idx - cols[:, None] + (WIN_W - 1)
    scale = HEAD_DIM ** -0.5

    def row_block(r):
        rs = jnp.clip(r - kh // 2, 0, rows - kh)
        k_rows = lax.dynamic_slice_in_dim(k, rs, kh, axis=1)
        v_rows = lax.dynamic_slice_in_dim(v, rs, kh, axis=1)
        k_win = k_rows[:, :, col_idx]
        v_win = v_rows[:, :, col_idx]
        q_row = lax.dynamic_index_in_dim(q, r, axis=1, keepdims=False)
        s = jnp.einsum('bchd,bicjhd->bhcij', q_row, k_win).astype(jnp.float32) * scale
        dr = rs + jnp.arange(kh) - r + (WIN_H - 1)
        bias = rpb[:, dr[None, :, None], dc[:, None, :]]
        s = s + bias.astype(jnp.float32)[None]
        p = jax.nn.softmax(s.reshape(b, h, GRID_W, kh * WIN_W), axis=-1)
        p = p.reshape(b, h, GRID_W, kh, WIN_W).astype(v.dtype)
        return jnp.einsum('bhcij,bicjhd->bchd', p, v_win)

    o = lax.map(row_block, jnp.arange(rows))
    return jnp.moveaxis(o, 0, 1).reshape(b, t, h * dh)

def fourier_mix(u, w_four, b_four):
    b, t, _ = u.shape
    ug = u.reshape(b, t, N_FOUR_GROUPS, FOUR_GROUP_DIM).astype(jnp.float32)
    f = jnp.fft.fft2(ug, axes=(1, 3), norm="ortho").real
    y = jnp.einsum('btgc,gcd->btgd', f, w_four.astype(jnp.float32)).reshape(b, t, D_FOUR)
    return (y + b_four.astype(jnp.float32)).astype(u.dtype)

def hybrid_mixer(xn, w_in, rpb, w_four, b_four, g_attn_out, g_four_out, w_out):
    b, t, _ = xn.shape
    proj = xn @ w_in
    q, k, v, u = jnp.split(proj, [D_ATTN, 2 * D_ATTN, 3 * D_ATTN], axis=-1)
    q = q.reshape(b, t, N_HEADS_A, HEAD_DIM)
    k = k.reshape(b, t, N_HEADS_A, HEAD_DIM)
    v = v.reshape(b, t, N_HEADS_A, HEAD_DIM)
    o_a = neighbourhood_attention(q, k, v, rpb)
    o_f = fourier_mix(u, w_four, b_four)
    merged = jnp.concatenate([rmsnorm(o_a, g_attn_out), rmsnorm(o_f, g_four_out)], axis=-1)
    return merged @ w_out

def hierarchical_moe(x, w_rc, b_rc, w_rf, b_rf, w_gate, w_up, w_down):
    b, t, d = x.shape
    n = b * t
    xt = x.reshape(n, d)
    coarse = (xt @ w_rc).astype(jnp.float32) + b_rc.astype(jnp.float32)
    coarse_p = jax.nn.softmax(coarse, axis=-1)
    g_w, g_idx = lax.top_k(coarse_p, 1)
    fine = ((xt @ w_rf).astype(jnp.float32) + b_rf.astype(jnp.float32))
    fine = fine.reshape(n, N_EXPERT_GROUPS, EXPERTS_PER_GROUP)
    fine_sel = jnp.take_along_axis(fine, g_idx[:, :, None], axis=1)[:, 0]
    f_val, f_idx = lax.top_k(fine_sel, TOP_K_FINE)
    f_w = jax.nn.softmax(f_val, axis=-1) * g_w
    expert_id = g_idx * EXPERTS_PER_GROUP + f_idx
    combine = jnp.sum(jax.nn.one_hot(expert_id, N_EXPERTS, dtype=jnp.float32)
                      * f_w[..., None], axis=1)
    y = jnp.zeros((n, d), jnp.float32)
    for e in range(N_EXPERTS):
        hdn = jax.nn.silu(xt @ w_gate[e]) * (xt @ w_up[e])
        y = y + combine[:, e:e + 1] * (hdn @ w_down[e]).astype(jnp.float32)
    return y.astype(x.dtype).reshape(b, t, d)

def setup_inputs(seed: int = 0) -> dict:
    key = jax.random.key(seed)
    ks = jax.random.split(key, 18)
    f32 = jnp.float32
    nrm = lambda k, shape, s: jax.random.normal(k, shape, f32) * s
    gain = lambda k, shape: 1.0 + 0.05 * jax.random.normal(k, shape, f32)
    return {
        "x": jax.random.normal(ks[0], (BATCH, SEQ, D_MODEL), f32),
        "norm_mix": gain(ks[1], (DEPTH, D_MODEL)),
        "w_in": nrm(ks[2], (DEPTH, D_MODEL, D_PROJ), D_MODEL ** -0.5),
        "rpb": nrm(ks[3], (DEPTH, N_HEADS_A, 2 * WIN_H - 1, 2 * WIN_W - 1), 0.5),
        "w_four": nrm(ks[4], (DEPTH, N_FOUR_GROUPS, FOUR_GROUP_DIM, FOUR_GROUP_DIM), FOUR_GROUP_DIM ** -0.5),
        "b_four": nrm(ks[5], (DEPTH, D_FOUR), 0.02),
        "g_attn_out": gain(ks[6], (DEPTH, D_ATTN)),
        "g_four_out": gain(ks[7], (DEPTH, D_FOUR)),
        "w_out": nrm(ks[8], (DEPTH, D_MIX, D_MODEL), D_MIX ** -0.5),
        "norm_moe": gain(ks[9], (DEPTH, D_MODEL)),
        "w_router_coarse": nrm(ks[10], (DEPTH, D_MODEL, N_EXPERT_GROUPS), D_MODEL ** -0.5),
        "b_router_coarse": nrm(ks[11], (DEPTH, N_EXPERT_GROUPS), 0.01),
        "w_router_fine": nrm(ks[12], (DEPTH, D_MODEL, N_EXPERTS), D_MODEL ** -0.5),
        "b_router_fine": nrm(ks[13], (DEPTH, N_EXPERTS), 0.01),
        "w_gate": nrm(ks[14], (DEPTH, N_EXPERTS, D_MODEL, D_EXPERT), D_MODEL ** -0.5),
        "w_up": nrm(ks[15], (DEPTH, N_EXPERTS, D_MODEL, D_EXPERT), D_MODEL ** -0.5),
        "w_down": nrm(ks[16], (DEPTH, N_EXPERTS, D_EXPERT, D_MODEL), D_EXPERT ** -0.5),
        "norm_final": gain(ks[17], (D_MODEL,)),
    }

def reference(x, norm_mix, w_in, rpb, w_four, b_four, g_attn_out, g_four_out, w_out,
              norm_moe, w_router_coarse, b_router_coarse, w_router_fine, b_router_fine,
              w_gate, w_up, w_down, norm_final):
    h = x
    for layer in range(DEPTH):
        xn = rmsnorm(h, norm_mix[layer])
        h = h + hybrid_mixer(xn, w_in[layer], rpb[layer], w_four[layer], b_four[layer],
                             g_attn_out[layer], g_four_out[layer], w_out[layer])
        hn = rmsnorm(h, norm_moe[layer])
        h = h + hierarchical_moe(hn, w_router_coarse[layer], b_router_coarse[layer],
                                 w_router_fine[layer], b_router_fine[layer],
                                 w_gate[layer], w_up[layer], w_down[layer])
    return rmsnorm(h, norm_final)


_drawn_inputs = setup_inputs


def setup_inputs(seed=0):
    import zlib

    import numpy as np

    out = dict(_drawn_inputs(seed))
    spreads = {}
    factors = {'b_router_coarse': 13.188, 'b_router_fine': 4.128}
    for name, (base, spread) in spreads.items():
        noise = np.random.default_rng([zlib.crc32(name.encode()), seed]).standard_normal(out[name].shape)
        drawn = base * np.exp(spread * noise) if base else spread * noise
        out[name] = __import__('jax').numpy.asarray(drawn.astype(out[name].dtype))
    for name, factor in factors.items():
        out[name] = (out[name] * factor).astype(out[name].dtype)
    return out
```

```python
import concourse.bass as bass
import concourse.mybir as mybir
import numpy as np
from contextlib import ExitStack

P = 128
T, D = 1024, 1024
NT, KD = T // P, D // P
GRID_W, ROWS = 64, 16
HEADS, DH = 8, 64
WIN_H, WIN_W = 8, 16
DM = 512
NC = DM // P
QR, QC = 8, 16
KR, KC = 12, 32
NK = KR * KC
COL_BASE = (0, 8, 24, 32)
RPB_R, RPB_C = 2 * WIN_H - 1, 2 * WIN_W - 1
FG = 8
HALF = T // 2
NG, NF = 4, 32
EPG = NF // NG
FE = 256
CAP = P
BLOCKS = T // CAP
SLOTS = BLOCKS * NF * CAP
SKIP = 1 << 20
EPS = 1e-6
BIG = 1e30

RPB_PAD = 160
RPB_N = HEADS * RPB_R * RPB_C
Z0 = (RPB_R // 2 - 4) * RPB_C - 1
G_LEN = (HEADS - 1) * RPB_R * RPB_C + (KR - 1 + RPB_R // 2) * RPB_C + (KC - 1) + RPB_C // 2 - Z0 + 1

C_ID, C_TRI, C_CC, C_SC = 0, 128, 256, 384
C_IOTA, C_IOTAM, C_GRP, C_SLOT, C_IOTA4, C_ALT = 512, 544, 576, 608, 640, 644
C_N = 648


def constants():
    k = np.arange(HALF)
    ang = 2 * np.pi * ((k[:, None] * k[None, :]) % T) / T
    dft = np.stack([np.cos(ang), np.sin(ang)], 0).reshape(2, 4, P, HALF).transpose(2, 0, 1, 3)
    c = np.arange(FG * 8)
    small = np.zeros((P, C_N))
    small[:, C_ID:C_ID + P] = np.eye(P)
    small[:, C_TRI:C_TRI + P] = np.arange(P)[:, None] < np.arange(P)[None, :]
    a2 = 2 * np.pi * ((c[:, None] * c[None, :]) % 64) / 64
    for i in range(2):
        s = slice(64 * i, 64 * i + 64)
        small[s, C_CC + 64 * i:C_CC + 64 * i + 64] = np.cos(a2) / 256
        small[s, C_SC + 64 * i:C_SC + 64 * i + 64] = np.sin(a2) / 256
    e = np.arange(NF)
    small[:, C_IOTA:C_IOTA + NF] = e
    small[:, C_IOTAM:C_IOTAM + NF] = e - 100
    small[:, C_GRP:C_GRP + NF] = e // EPG - 100
    small[:, C_SLOT:C_SLOT + NF] = e * CAP
    small[:, C_IOTA4:C_IOTA4 + NG] = np.arange(NG)
    small[:, C_ALT] = 1 - 2 * (np.arange(P) % 2)
    altrow = (1 - 2 * (np.arange(HALF) % 2))[None]
    mask = np.full((P, 8, KR, KC), BIG)
    for a in range(2):
        for b in range(4):
            for i in range(QR):
                for cc in range(QC):
                    r, col = QR * a + i, QC * b + cc
                    rs = min(max(r - WIN_H // 2, 0), ROWS - WIN_H)
                    cs = min(max(col - WIN_W // 2, 0), GRID_W - WIN_W)
                    j0, k0 = rs - 4 * a, cs - COL_BASE[b]
                    mask[QC * i + QC - 1 - cc, 4 * a + b, j0:j0 + WIN_H, k0:k0 + WIN_W] = 0
    f = np.float32
    return {"c_dft": np.ascontiguousarray(dft.reshape(P, -1)).astype(f), "c_small": small.astype(f),
            "c_alt": altrow.astype(f), "c_mask": mask.reshape(P, -1).astype(f)}


def build(nc, io, out):
    f32, f32r, bf16 = mybir.dt.float32, mybir.dt.float32r, mybir.dt.bfloat16
    i32, u32 = mybir.dt.int32, mybir.dt.uint32
    ALU, ACT, AX = mybir.AluOpType, mybir.ActivationFunctionType, mybir.AxisListType

    v_dram = nc.dram_tensor("v_rows", (T, DM), f32).ap()
    rpb_dram = nc.dram_tensor("rpb_padded", (1, RPB_N + 2 * RPB_PAD), f32)
    hn_dram = nc.dram_tensor("hn_rows", (T, D), f32).ap()
    slot_dram = nc.dram_tensor("slot_table", (SLOTS, 2), u32).ap()
    y_dram = nc.dram_tensor("y_rows", (2 * T, D), f32).ap()

    w_in = io["w_in"].rearrange("o (k p) n -> p (o k) n", p=P)
    w_out = io["w_out"].rearrange("o (k p) n -> p (o k) n", p=P)
    w_gate = io["w_gate"].rearrange("o e (k p) n -> p (o e) k n", p=P)
    w_up = io["w_up"].rearrange("o e (k p) n -> p (o e) k n", p=P)
    w_down = io["w_down"].rearrange("o e (k p) n -> p (o e) k n", p=P)
    x_rows = io["x"].rearrange("o (t p) n -> p (o t) n", p=P)
    out_rows = out.rearrange("o (t p) n -> p (o t) n", p=P)
    hn_rows = hn_dram.rearrange("(t p) n -> p t n", p=P)
    y_rows = y_dram.rearrange("(t p k) n -> p t (k n)", p=P, k=2)

    ctx = ExitStack()
    BASE = 16512

    def at(name, kb, shape, dtype=f32):
        return nc.alloc_sbuf_tensor_at(name, shape, dtype, offset=BASE + int(kb * 32) * 32)

    def sem(name):
        return ctx.enter_context(nc.semaphore(name))

    with ctx:
        small = at("small", 0, [P, C_N])
        ident = small[:, C_ID:C_ID + P]
        tri_ones = at("tri_ones", 2.6, [P, 2, P], bf16)
        rows20 = at("rows20", 3.15, [20, P])
        cols = at("cols", 3.7, [P, 20])
        g_mix, g_merged, b_four = cols[:, 0:8], cols[:, 8:16], cols[:, 16:20]
        half_neg = at("half_neg", 3.8, [P, 1])
        ss_x = at("ss_x", 3.82, [P, 8])
        ss_h = at("ss_h", 3.86, [P, 8])
        ss_f = at("ss_f", 3.9, [P, 8])
        xT_hi = at("xT_hi", 4, [P, KD, T], f32r)
        xT_lo = at("xT_lo", 36, [P, KD, T], f32r)
        x_in = at("x_in", 68, [P, NT, D])
        qT = at("qT", 68, [P, NC, T])
        kT = at("kT", 84, [P, NC, T])
        w_raw = at("w_raw", 100, [P, 2, KD, 256])
        w_hi = at("w_hi", 116, [P, 2, KD, 256], f32r)
        w_lo = at("w_lo", 132, [P, 2, KD, 256], f32r)
        u_even = at("u_even", 148, [P, NC, HALF + 1])
        u_odd = at("u_odd", 156.5, [P, NC, HALF])
        u_top = at("u_top", 165, [P, 2, HALF])
        v_out = at("v_out", 177, [P, 4, 256])
        dft = at("dft", 181, [P, 2, 4, HALF])
        m_chan = at("m_chan", 197, [P, 2, NC, P])
        w_bd = at("w_bd", 201, [P, NC, P])
        altrow = at("altrow", 203, [1, HALF])
        zeros = at("zeros", 205, [P, 512], u32)
        junk_x = at("junk_x", 165, [P, D])
        ones_col = at("ones_col", 3.98, [P, 1])
        a_even = at("a_even", 128, [P, 4, DM])
        b_odd = at("b_odd", 136, [P, 4, DM])
        a_mid = at("a_mid", 144, [1, DM])
        y_tmp = at("y_tmp", 165, [P, 2, HALF])
        y_sq = at("y_sq", 128, [P, NC, T])
        yT = at("yT", 52, [P, NC, T])
        vk = at("vk", 4, [P, 16, DM])
        bias_g = at("bias_g", 100, [P, G_LEN])
        mask = at("mask", 116, [P, 8, NK])
        bm = at("bm", 36, [P, 3, NK])
        s_sb = at("s_sb", 40.5, [P, 2, NK])
        p_sb = at("p_sb", 43.5, [P, 2, NK])
        pT = at("pT", 46.5, [P, 2, NK])
        s_min = at("s_min", 49.5, [P, 4])
        r_sum = at("r_sum", 49.6, [P, 2, 8])
        r_inv = at("r_inv", 49.7, [P, 2, 8])
        ss_o = at("ss_o", 49.8, [P, 8])
        junk_o = at("junk_o", 50, [P, DM])
        oT = at("oT", 148, [P, NC, T])
        o_sb = at("o_sb", 197, [P, 2, DM])
        wo_raw = at("wo_raw", 201, [P, 3, 512])
        wo_hi = [at("wo_hi0", 181, [P, KD, 512], f32r), at("wo_hi1", 4, [P, KD, 512], f32r)]
        wo_lo = [at("wo_lo0", 165, [P, KD, 512], f32r), at("wo_lo1", 20, [P, KD, 512], f32r)]
        mT_hi = at("mT_hi", 68, [P, KD, T], f32r)
        mT_lo = at("mT_lo", 100, [P, KD, T], f32r)
        h = at("h", 36, [P, NT, D])
        x_res = at("x_res", 132, [P, 4, 512])
        hn = at("hn", 140, [P, 2, D])
        junk_h = at("junk_h", 148, [P, D])
        g_moe = at("g_moe", 152, [P, D])
        w_r = at("w_r", 156, [P, KD, NG + NF])
        b_r = at("b_r", 157.2, [P, NG + NF])
        fill = at("fill", 158, [P, 512], u32)
        hT = at("hT", 165, [P, 2, KD, P])
        lg = at("lg", 173, [P, NT, NG + NF])
        c_d = at("c_d", 174.2, [P, NT, NG])
        c_e = at("c_e", 174.4, [P, NT, NG])
        c_eq = at("c_eq", 174.6, [P, NT, NG])
        c_cand = at("c_cand", 174.8, [P, NT, NG])
        r8 = at("r8", 175, [P, 12, NT])
        f_m = at("f_m", 176, [P, NT, NF])
        f_eq = at("f_eq", 177, [P, NT, NF])
        f_cand = at("f_cand", 178, [P, NT, NF])
        oh1 = at("oh1", 179, [P, NT, NF])
        oh2 = at("oh2", 180, [P, NT, NF])
        oh = at("oh", 181, [P, NT, NF], bf16)
        rank = at("rank", 182, [P, NT, NF])
        rank_i = at("rank_i", 183, [P, NT, NF], i32)
        rank_b = at("rank_b", 184, [P, NT, NF])
        pick = at("pick", 185, [P, 2, NT, NF])
        gu_raw = at("gu_raw", 68, [P, 2, KD, 2, FE])
        dn_raw = at("dn_raw", 100, [P, 2, 2, D])
        gu_hi = at("gu_hi", 4, [P, KD, 2 * FE], f32r)
        gu_lo = at("gu_lo", 20, [P, KD, 2 * FE], f32r)
        dn_hi = at("dn_hi", 116, [P, 2, D], f32r)
        dn_lo = at("dn_lo", 124, [P, 2, D], f32r)
        xg = at("xg", 132, [P, 2, D])
        xgT_hi = at("xgT_hi", 140, [P, KD, P], f32r)
        xgT_lo = at("xgT_lo", 144, [P, KD, P], f32r)
        act_g = at("act_g", 148, [P, FE])
        hid = at("hid", 149, [P, FE])
        hidT_hi = at("hidT_hi", 150, [P, 2, P], f32r)
        hidT_lo = at("hidT_lo", 151, [P, 2, P], f32r)
        y_sb = at("y_sb", 187, [P, 2, D])
        slot_all = at("slot_all", 195, [P, NF, 2], u32)
        slot_val = at("slot_val", 195.3, [P, NT, 2, 2], u32)
        slot_of = at("slot_of", 195.5, [P, 2, NT], u32)
        mix_w = at("mix_w", 195.6, [P, 2, NT])
        idx_x = at("idx_x", 195.7, [P, 2, 1], u32)
        idx_y = at("idx_y", 195.72, [P, 2, 1], u32)
        zero_i = at("zero_i", 195.75, [P, 1], u32)
        most = at("most", 195.8, [P, 2], f32)
        most_i = at("most_i", 195.9, [P, 2], i32)
        y_pair = at("y_pair", 68, [P, 3, 2 * D])
        g_fin = at("g_fin", 100, [P, D])
        fin = at("fin", 104, [P, 2, D])
        o_fin = at("o_fin", 112, [P, 2, D])
        junk_f = at("junk_f", 120, [P, D])
        ss_e = at("ss_e", 124, [P, 8])

        bank = [ctx.enter_context(nc.psum_tensor(f"bank{i}", [P, 512], f32)) for i in range(8)]

        consts_in, wbd_in, dft_in = (sem(n) for n in ("consts_in", "wbd_in", "dft_in"))
        x_loaded = [sem(f"x_loaded{t}") for t in range(NT)]
        w_loaded = [sem(f"w_loaded{i}") for i in range(2)]
        init_set, fill_set, rms_mid = (sem(n) for n in ("init_set", "fill_set", "rms_mid"))
        HALVES, ONES, WBD_ZERO, ZEROS, ODD_ZERO, TRI = 1, 2, 3, 4, 5, 7
        cols_tr, cols_set, m_done, m_set = (sem(n) for n in ("cols_tr", "cols_set", "m_done", "m_set"))
        x_sq, x_rs, x_scaled, x_tr, x_hi, x_lo = (sem(n) for n in ("x_sq", "x_rs", "x_scaled", "x_tr", "x_hi", "x_lo"))
        w_gained, w_hi_set, w_lo_set, proj_done, evac_act, evac_dve = (
            sem(n) for n in ("w_gained", "w_hi_set", "w_lo_set", "proj_done", "evac_act", "evac_dve"))
        v_stored = [sem(f"v_stored{i}") for i in range(4)]
        vk_in, rpb_mid, bias_in = (sem(n) for n in ("vk_in", "rpb_mid", "bias_in"))
        f1_done, f1_act, f1_dve, f2_done, f2_tmp, f2_dve, f_mid, f_mid_set, y_squared, f_moved, f_rs = (
            sem(n) for n in ("f1_done", "f1_act", "f1_dve", "f2_done", "f2_tmp", "f2_dve", "f_mid", "f_mid_set", "y_squared", "f_moved", "f_rs"))
        bm_set, s_done, s_shift, p_set, p_tr, pT_act, pT_dve, pv_done = (
            sem(n) for n in ("bm_set", "s_done", "s_shift", "p_set", "p_tr", "pT_act", "pT_dve", "pv_done"))
        o_inv, o_normed, o_sq, o_rs, o_scaled, o_tr, oT_set = (
            sem(n) for n in ("o_inv", "o_normed", "o_sq", "o_rs", "o_scaled", "o_tr", "oT_set"))
        wo_loaded = [sem(f"wo_loaded{i}") for i in range(3)]
        wo_gained, wo_hi_set, wo_lo_set, m_hi_set, m_lo_set, wo_done, h_part, h_set = (
            sem(n) for n in ("wo_gained", "wo_hi_set", "wo_lo_set", "m_hi_set", "m_lo_set", "wo_done", "h_part", "h_set"))
        xr_loaded = [sem(f"xr_loaded{i}") for i in range(4)]
        gmoe_in, router_in, filled = (sem(n) for n in ("gmoe_in", "router_in", "filled"))
        h_sq, h_rs, hn_set, h_tr, hT_set, r_done = (sem(n) for n in ("h_sq", "h_rs", "hn_set", "h_tr", "hT_set", "r_done"))
        hn_stored = [sem(f"hn_stored{i}") for i in range(2)]
        rt, c_sub, c_exp, d_sub, d_exp, oh_set, rank_done, slots_set, vals_set, slots_scattered = (
            sem(n) for n in ("rt", "c_sub", "c_exp", "d_sub", "d_exp", "oh_set", "rank_done", "slots_set", "vals_set", "slots_scattered"))
        slots_loaded, xg_zero, most_set, gu_half, amid_done, amid_set = (
            sem(n) for n in ("slots_loaded", "xg_zero", "most_set", "gu_half", "amid_done", "amid_set"))
        f_ssum, hT_set_act = (sem(n) for n in ("f_ssum", "hT_set_act"))
        gu_loaded = [sem(f"gu_loaded{i}") for i in range(2)]
        dn_loaded = [sem(f"dn_loaded{i}") for i in range(2)]
        gu_hi_set, gu_lo_set, dn_hi_set, dn_lo_set = (sem(n) for n in ("gu_hi_set", "gu_lo_set", "dn_hi_set", "dn_lo_set"))
        idxx_set, idxy_set, idx_seen = sem("idxx_set"), sem("idxy_set"), sem("idx_seen")
        xg_in = [sem(f"xg_in{i}") for i in range(2)]
        y_out = [sem(f"y_out{i}") for i in range(2)]
        xg_tr, xgT_hi_set, xgT_lo_set, gu_done, silu_set, hid_set, hid_tr, hidT_hi_set, hidT_lo_set, dn_done, y_set = (
            sem(n) for n in ("xg_tr", "xgT_hi_set", "xgT_lo_set", "gu_done", "silu_set", "hid_set", "hid_tr",
                             "hidT_hi_set", "hidT_lo_set", "dn_done", "y_set"))
        yp_loaded = [sem(f"yp_loaded{i}") for i in range(3)]
        gfin_in, e_one, e_two, e_sq, e_rs, e_set = (sem(n) for n in ("gfin_in", "e_one", "e_two", "e_sq", "e_rs", "e_set"))
        out_stored = [sem(f"out_stored{i}") for i in range(2)]

        block = ctx.enter_context(nc.Block())

        CHUNKS = [("u", 3 * DM), ("u", 3 * DM + 256), ("q", 0), ("q", 256), ("k", DM), ("k", DM + 256),
                  ("v", 2 * DM), ("v", 2 * DM + 256)]
        GROUPS = []
        for w, (kind, _) in enumerate(CHUNKS):
            if kind == "v":
                GROUPS += [(w, kind, None, t) for t in range(NT)]
            else:
                GROUPS += [(w, kind, s, half) for s in range(2) for half in (1, 0)]
        CHUNK_END = [sum(x[0] <= w for x in GROUPS) for w in range(len(CHUNKS))]
        BY_ACT = [g for g, (_, kind, _, half) in enumerate(GROUPS) if kind in "qk" or (kind == "u" and half == 1)]
        BY_DVE = [g for g in range(len(GROUPS)) if g not in BY_ACT]

        def wait_evacuated(eng, g):
            if g in BY_ACT:
                eng.wait_ge(evac_act, BY_ACT.index(g) + 1)
            else:
                eng.wait_ge(evac_dve, BY_DVE.index(g) + 1)

        QT = [(a, b) for a in range(2) for b in range(4)]
        M = len(QT) * HEADS

        def wait_pT(eng, m):
            eng.wait_ge(pT_dve if m % 2 else pT_act, m // 2 + 1)

        def three(pe, dst, hi, lo, rhi, rlo, first, last):
            pe.matmul(dst, hi, rhi, start=first, stop=False)
            pe.matmul(dst, hi, rlo, start=False, stop=False)
            return pe.matmul(dst, lo, rhi, start=False, stop=last)

        def chunk_c(w):
            return CHUNKS[w][1]

        def slot(p, k, d):
            return (p + d) % 2, k + (p + d) // 2

        def ge(eng, which, value):
            if not isinstance(value, int) or value > 0:
                eng.wait_ge(which, value)

        def expert_pass(eng, step, b):
            def peeled(l):
                step(l, l, NF * b + l, NF // 2 * b + l // 2, l % 2)
            for l in range(4):
                peeled(l)
            with eng.Fori(2, NF // 2 - 1) as i:
                for p in range(2):
                    step(None, 2 * i + p, NF * b + 2 * i + p, NF // 2 * b + i, p)
            for l in (NF - 2, NF - 1, NF):
                peeled(l)

        def all_blocks(eng, step):
            expert_pass(eng, step, 0)
            eng.wait_ge(most_set, 1)
            over = eng.value_load(most_i[0:1, 0:1])
            with eng.If(over > CAP):
                with eng.Fori(1, BLOCKS) as b:
                    expert_pass(eng, step, b)
            with eng.Else():
                eng.nop()
            eng.nop()

        @block.sync
        def _(sp):
            sp.dma_start(small[:], io["c_small"]).then_inc(consts_in, 16)
            for t in range(NT):
                sp.dma_start(x_in[:, t, :], x_rows[:, t, :]).then_inc(x_loaded[t], 16)
                if t in (2, 5):
                    w = 0 if t == 2 else 1
                    sp.dma_start(w_raw[:, w, :, :], w_in[:, :, chunk_c(w):chunk_c(w) + 256]).then_inc(w_loaded[w], 16)
                if t == 0:
                    for k, name in ((0, "norm_mix"), (8, "g_attn_out"), (12, "g_four_out"), (16, "b_four")):
                        src = io[name].rearrange("o (k p) -> (o k) p", p=P)
                        sp.dma_start(rows20[k:k + src.shape[0], :], src).then_inc(consts_in, 16)
            sp.wait_ge(init_set, WBD_ZERO)
            for g in range(FG):
                o = 64 * (g % 2)
                sp.dma_start(w_bd[o:o + 64, g // 2, o:o + 64], io["w_four"][0, g]).then_inc(wbd_in, 16)
            sp.dma_start(dft[:].rearrange("p a b c -> p (a b c)"), io["c_dft"]).then_inc(dft_in, 16)
            sp.dma_start(altrow[:], io["c_alt"]).then_inc(dft_in, 16)
            sp.wait_ge(init_set, ZEROS)
            rp = rpb_dram.ap()
            sp.dma_start(rp[:, RPB_PAD:RPB_PAD + RPB_N], io["rpb"].rearrange("o h a b -> o (h a b)")).then_inc(rpb_mid, 16)
            for o in (0, RPB_PAD + RPB_N):
                sp.dma_start(rp[:, o:o + RPB_PAD], zeros[0:1, 0:RPB_PAD].bitcast(f32)).then_inc(rpb_mid, 16)
            for w in range(2, len(CHUNKS)):
                sp.wait_ge(w_lo_set, w - 1)
                sp.dma_start(w_raw[:, w % 2, :, :], w_in[:, :, chunk_c(w):chunk_c(w) + 256]).then_inc(w_loaded[w % 2], 16)
            v_at = 0
            for w in (6, 7):
                for t in range(NT):
                    g = 24 + v_at
                    wait_evacuated(sp, g)
                    sp.dma_start(v_dram[t * P:(t + 1) * P, 256 * (w - 6):256 * (w - 5)], v_out[:, v_at % 4, :])\
                      .then_inc(v_stored[v_at % 4], 16)
                    v_at += 1
            for i in range(4):
                sp.wait_ge(v_stored[i], 64)
            sp.wait_ge(proj_done, len(GROUPS))
            for g in range(4):
                for j in range(4):
                    for lo_b, hi_b in ((0, 3), (1, 2)):
                        row = (4 * g + j) * GRID_W + COL_BASE[lo_b]
                        gap = COL_BASE[hi_b] - COL_BASE[lo_b]
                        src = bass.AP(v_dram.tensor, row * DM, [[DM, KC], [gap * DM, 2], [1, DM]])
                        dst = vk[32 * j:32 * j + 32, 4 * g + lo_b:4 * g + hi_b + 1:hi_b - lo_b, :]
                        sp.dma_start(dst, src).then_inc(vk_in, 16)
            sp.wait_ge(rpb_mid, 48)
            for i in range(QR):
                src = bass.AP(rpb_dram, RPB_PAD + Z0 - RPB_C * i - (QC - 1), [[1, QC], [1, G_LEN]])
                sp.dma_start(bias_g[QC * i:QC * i + QC, :], src).then_inc(bias_in, 16)
            sp.dma_start(mask[:].rearrange("p a b -> p (a b)"), io["c_mask"]).then_inc(bias_in, 16)
            sp.wait_ge(f_rs, 1)
            def load_wo(i):
                n, c = i // KD, i % KD
                if i >= 3:
                    sp.wait_ge(wo_lo_set, i - 2)
                sp.dma_start(wo_raw[:, i % 3, :], w_out[:, c, 512 * n:512 * n + 512]).then_inc(wo_loaded[i % 3], 16)

            def load_xr(i):
                n, t = i // NT, i % NT
                if i >= 4:
                    sp.wait_ge(h_part, i - 3)
                sp.dma_start(x_res[:, i % 4, :], x_rows[:, t, 512 * n:512 * n + 512]).then_inc(xr_loaded[i % 4], 16)

            for i in range(KD + 3):
                load_wo(i)
            for i in range(4):
                load_xr(i)
            for i in range(KD + 3, 2 * KD):
                load_xr(i - KD + 1)
                load_wo(i)
            sp.wait_ge(m_lo_set, NT)
            sp.dma_start(g_moe[:], io["norm_moe"].partition_broadcast(P).rearrange("p o n -> p (o n)")).then_inc(gmoe_in, 16)
            sp.dma_start(w_r[:, :, 0:NG], io["w_router_coarse"].rearrange("o (k p) n -> p (o k) n", p=P)).then_inc(router_in, 16)
            sp.dma_start(w_r[:, :, NG:], io["w_router_fine"].rearrange("o (k p) n -> p (o k) n", p=P)).then_inc(router_in, 16)
            sp.dma_start(b_r[:, 0:NG], io["b_router_coarse"].partition_broadcast(P).rearrange("p o n -> p (o n)")).then_inc(router_in, 16)
            sp.dma_start(b_r[:, NG:], io["b_router_fine"].partition_broadcast(P).rearrange("p o n -> p (o n)")).then_inc(router_in, 16)
            def store_hn(t):
                sp.wait_ge(hn_set, t + 1)
                sp.dma_start(hn_rows[:, t, :], hn[:, t % 2, :]).then_inc(hn_stored[t % 2], 16)

            for i in range(9, 2 * NT):
                load_xr(i)
                if i == 9:
                    sp.wait_ge(fill_set, 1)
                    sp.dma_start(slot_dram.rearrange("(p a) b -> p (a b)", p=P), fill[:]).then_inc(filled, 16)
                if i >= 12:
                    store_hn(i - 12)
            for t in range(4, NT):
                store_hn(t)
            sp.wait_ge(wo_done, 4 * NT)

            def load_gu(n, e, p, reuse):
                if reuse:
                    sp.wait_ge(gu_hi_set, 2 * (n - 1))
                    sp.wait_ge(gu_lo_set, 2 * (n - 1))
                sp.dma_start(gu_raw[:, p, :, 0, :], w_gate[:, e, :, :]).then_inc(gu_loaded[p], 16)
                sp.dma_start(gu_raw[:, p, :, 1, :], w_up[:, e, :, :]).then_inc(gu_loaded[p], 16)

            def load_dn(n, e, p, reuse):
                if reuse:
                    sp.wait_ge(dn_hi_set, n - 1)
                    sp.wait_ge(dn_lo_set, n - 1)
                sp.dma_start(dn_raw[:, p, :, :], w_down[:, e, :, :]).then_inc(dn_loaded[p], 16)

            def one(e):
                return bass.ds(e, 1)

            def load_expert(n, e, p, reuse):
                if isinstance(e, int):
                    load_gu(n, e, p, reuse)
                    load_dn(n, e, p, reuse)
                    return
                if reuse:
                    sp.wait_ge(gu_hi_set, 2 * (n - 1))
                    sp.wait_ge(gu_lo_set, 2 * (n - 1))
                sp.dma_start(gu_raw[:, p, :, 0, :], w_gate[:, one(e), :, :].rearrange("p o k n -> p (o k) n")).then_inc(gu_loaded[p], 16)
                sp.dma_start(gu_raw[:, p, :, 1, :], w_up[:, one(e), :, :].rearrange("p o k n -> p (o k) n")).then_inc(gu_loaded[p], 16)
                if reuse:
                    sp.wait_ge(dn_hi_set, n - 1)
                    sp.wait_ge(dn_lo_set, n - 1)
                sp.dma_start(dn_raw[:, p, :, :], w_down[:, one(e), :, :].rearrange("p o k n -> p (o k) n")).then_inc(dn_loaded[p], 16)

            load_expert(0, 0, 0, False)
            load_expert(1, 1, 1, False)
            sp.wait_ge(slots_scattered, 16 * 2 * NT)
            sp.dma_start(slot_all[:], slot_dram[0:NF * CAP, :].rearrange("(e s) b -> s e b", s=CAP)).then_inc(slots_loaded, 16)
            with sp.Fori(1, NF // 2) as i:
                for p in range(2):
                    load_expert(2 * i + p, 2 * i + p, p, True)
            sp.wait_ge(most_set, 1)
            over = sp.value_load(most_i[0:1, 0:1])
            with sp.If(over > CAP):
                with sp.Fori(1, BLOCKS) as b:
                    sp.wait_ge(idxx_set, NF * b)
                    sp.wait_ge(idxy_set, NF * b)
                    sp.dma_start(slot_all[:], slot_dram[bass.ds(b * NF * CAP, NF * CAP), :].rearrange("(e s) b -> s e b", s=CAP))\
                      .then_inc(slots_loaded, 16)
                    with sp.Fori(0, NF // 2) as i:
                        for p in range(2):
                            load_expert(NF * b + 2 * i + p, 2 * i + p, p, True)
                sp.wait_ge(y_out[0], 16 * NF // 2 * BLOCKS)
                sp.wait_ge(y_out[1], 16 * NF // 2 * BLOCKS)
            with sp.Else():
                sp.wait_ge(y_out[0], 16 * NF // 2)
                sp.wait_ge(y_out[1], 16 * NF // 2)
            sp.dma_start(g_fin[:], io["norm_final"].rearrange("(o n) -> o n", o=1).partition_broadcast(P).rearrange("p o n -> p (o n)")).then_inc(gfin_in, 16)
            for t in range(NT):
                if t >= 3:
                    sp.wait_ge(e_two, t - 2)
                sp.dma_start(y_pair[:, t % 3, :], y_rows[:, t, :]).then_inc(yp_loaded[t % 3], 16)
                if t >= 1:
                    sp.wait_ge(e_set, t)
                    sp.dma_start(out_rows[:, t - 1, :], o_fin[:, (t - 1) % 2, :]).then_inc(out_stored[(t - 1) % 2], 16)
            sp.wait_ge(e_set, NT)
            sp.dma_start(out_rows[:, NT - 1, :], o_fin[:, (NT - 1) % 2, :]).then_inc(out_stored[(NT - 1) % 2], 16)
            for i in range(2):
                sp.wait_ge(out_stored[i], 64)
                sp.wait_ge(hn_stored[i], 64)
            sp.wait_ge(filled, 16)

        @block.scalar
        def _(act):
            def split_w_hi(w):
                act.wait_ge(w_gained, w + 1)
                if w >= 2:
                    act.wait_ge(proj_done, CHUNK_END[w - 2])
                act.activation(w_hi[:, w % 2, :, :], w_raw[:, w % 2, :, :], ACT.Copy).then_inc(w_hi_set, 1)

            def x_square(t):
                act.wait_ge(x_loaded[t], 16)
                if t:
                    act.wait_ge(x_sq, t)
                act.activation(junk_x[:],
                               x_in[:, t, :], ACT.Square, accum_out=ss_x[:, t:t + 1]).then_inc(x_sq, 1)

            act.wait_ge(consts_in, 80)
            x_square(0)
            for t in range(NT):
                if t + 1 < NT:
                    x_square(t + 1)
                for j in range(2):
                    act.wait_ge(x_tr, 2 * t + j + 1)
                    act.activation(xT_hi[:, 4 * j:4 * j + 4, t * P:(t + 1) * P], bank[4 + j][:, :].rearrange("p (k n) -> p k n", n=P),
                                   ACT.Copy).then_inc(x_hi, 1)
                if t == 5:
                    split_w_hi(0)
            split_w_hi(1)
            act.wait_ge(m_done, 2)
            for i in range(2):
                act.activation(m_chan[:, i, :, :].rearrange("p c n -> p (c n)"), bank[6 + i][:, :], ACT.Copy).then_inc(m_set, 1)
            for g, (w, kind, s, half) in enumerate(GROUPS):
                if g in BY_ACT:
                    act.wait_ge(proj_done, g + 1)
                    src = bank[g % 4][:, :]
                    c = 2 * (w % 2) + (s or 0)
                    if kind == "u":
                        if c >= 2:
                            wait_evacuated(act, 2 * (c - 2) + 1)
                        act.activation(u_top[:, c % 2, :], src, ACT.Copy).then_inc(evac_act, 1)
                    elif kind == "q":
                        dst = qT[:, c, 512 * half:512 * half + 512].rearrange("p (b i w) -> p i b w", b=4, i=QR)[:, :, :, ::-1]
                        act.activation(dst, src.rearrange("p (i b w) -> p i b w", i=QR, b=4), ACT.Copy, scale=-DH ** -0.5).then_inc(evac_act, 1)
                    else:
                        act.activation(kT[:, c, 512 * half:512 * half + 512], src, ACT.Copy).then_inc(evac_act, 1)
                last_of_chunk = g + 1 == len(GROUPS) or GROUPS[g + 1][0] != w
                if last_of_chunk and w + 2 < len(CHUNKS):
                    split_w_hi(w + 2)
            for i in range(4):
                act.wait_ge(f1_done, i + 1)
                act.activation(a_even[:, i, :], bank[4 + i][:, :], ACT.Copy).then_inc(f1_act, 1)
            act.wait_ge(amid_done, 1)
            act.activation(a_mid[:], bank[0][0:1, :], ACT.Copy).then_inc(amid_set, 1)
            for c in range(NC):
                act.wait_ge(f2_done, 2 * c + 1)
                if c >= 2:
                    act.wait_ge(f2_dve, c - 1)
                act.activation(y_tmp[:, c % 2, :], bank[2 * (c % 2)][:, :], ACT.Identity, bias=b_four[:, c:c + 1]).then_inc(f2_tmp, 1)
            act.wait_ge(f2_dve, NC)
            act.wait_ge(f_mid_set, 1)
            act.activation(y_sq[:].rearrange("p c n -> p (c n)"), yT[:].rearrange("p c n -> p (c n)"), ACT.Square).then_inc(y_squared, 1)

            def o_square(q):
                act.wait_ge(o_normed, q + 1)
                if q:
                    act.wait_ge(o_scaled, q)
                act.activation(junk_o[:], o_sb[:, q % 2, :], ACT.Square, accum_out=ss_o[:, q:q + 1]).then_inc(o_sq, 1)

            def o_scale(q):
                act.wait_ge(o_rs, q + 1)
                act.wait_ge(o_sq, q + 1)
                act.activation(o_sb[:, q % 2, :], o_sb[:, q % 2, :], ACT.Copy, scale=ss_o[:, q:q + 1]).then_inc(o_scaled, 1)

            def o_place(q):
                a, b = QT[q]
                act.wait_ge(o_tr, q + 1)
                dst = oT[:].rearrange("p c (r w) -> p c r w", w=GRID_W)[:, :, QR * a:QR * a + QR, QC * b:QC * b + QC]
                act.activation(dst, bank[7][:, :].rearrange("p (c r w) -> p c r w", c=NC, w=QC)[:, :, :, ::-1], ACT.Copy).then_inc(oT_set, 1)

            def split_wo_hi(i):
                n, c = i // KD, i % KD
                act.wait_ge(wo_gained, i + 1)
                act.activation(wo_hi[n][:, c, :], wo_raw[:, i % 3, :], ACT.Copy).then_inc(wo_hi_set, 1)

            def pT_copy(m):
                act.wait_ge(p_tr, m + 1)
                if m >= 2:
                    act.wait_ge(pv_done, m - 1)
                act.activation(pT[:, m % 2, :], bank[3 + m % 2][:, 0:NK], ACT.Copy).then_inc(pT_act, 1)

            for m in range(M):
                q, hd = m // HEADS, m % HEADS
                act.wait_ge(s_shift, m + 1)
                if m >= 2:
                    act.wait_ge(p_tr, m - 1)
                if q >= 2 and hd == 0:
                    act.wait_ge(o_inv, q - 1)
                act.activation(p_sb[:, m % 2, :], s_sb[:, m % 2, :], ACT.Exp, bias=s_min[:, m % 4:m % 4 + 1], scale=-1.0,
                               accum_out=r_sum[:, q % 2, hd:hd + 1]).then_inc(p_set, 1)
                if m >= 1 and (m - 1) % 2 == 0:
                    pT_copy(m - 1)
                if q:
                    if hd == 3:
                        o_square(q - 1)
                    if hd == 4:
                        o_scale(q - 1)
                    if hd == 7:
                        o_place(q - 1)
                if m >= 14 and m % 6 == 2 and (m - 14) // 6 < KD:
                    split_wo_hi((m - 14) // 6)
            o_square(7)
            o_scale(7)
            o_place(7)
            for t in range(NT):
                for j, src in ((0, oT), (1, yT)):
                    act.wait_ge(oT_set, 8)
                    act.activation(mT_hi[:, 4 * j:4 * j + 4, t * P:(t + 1) * P], src[:, :, t * P:(t + 1) * P], ACT.Copy).then_inc(m_hi_set, 1)
            for i in range(KD, 2 * KD):
                split_wo_hi(i)
            for t in range(NT + 1):
                if t < NT:
                    act.wait_ge(h_set, NT + t + 1)
                    act.activation(junk_h[:], h[:, t, :], ACT.Square, accum_out=ss_h[:, t:t + 1]).then_inc(h_sq, 1)
                if t >= 1:
                    u = t - 1
                    act.wait_ge(h_tr, 2 * u + 1)
                    if u >= 2:
                        act.wait_ge(r_done, u - 1)
                    act.activation(hT[:, u % 2, 0:4, :].rearrange("p k n -> p (k n)"), bank[4][:, :], ACT.Copy).then_inc(hT_set_act, 1)
            act.wait_ge(c_sub, 1)
            act.activation(c_e[:], c_d[:], ACT.Exp).then_inc(c_exp, 1)
            act.wait_ge(d_sub, 1)
            act.activation(r8[:, 6, :], r8[:, 5, :], ACT.Exp).then_inc(d_exp, 1)

            def gu_hi_half(n1, p1, k1, j):
                act.activation(gu_hi[:, 4 * j:4 * j + 4, :], gu_raw[:, p1, 4 * j:4 * j + 4, :, :].rearrange("p k a n -> p k (a n)"),
                               ACT.Copy).then_inc(gu_hi_set, 1)

            def xgT_high(n1):
                act.wait_ge(xg_tr, n1 + 1)
                act.wait_ge(gu_done, n1) if not isinstance(n1, int) or n1 > 0 else None
                act.activation(xgT_hi[:, 0:4, :].rearrange("p k n -> p (k n)"), bank[2][:, :], ACT.Copy).then_inc(xgT_hi_set, 1)
                act.activation(xgT_hi[:, 4:8, :].rearrange("p k n -> p (k n)"), bank[3][:, :], ACT.Copy).then_inc(xgT_hi_set, 1)

            def step(l, e, n, k, p):
                if l == 0:
                    act.wait_ge(gu_loaded[p], 32 * (k + 1))
                    ge(act, gu_done, n)
                    gu_hi_half(n, p, k, 0)
                    gu_hi_half(n, p, k, 1)
                    xgT_high(n)
                if l != 0:
                    pp, kp = slot(p, k, -1)
                    act.wait_ge(gu_done, n)
                    ge(act, hid_set, n - 1)
                    act.activation(act_g[:], bank[pp][:, 0:FE], ACT.Silu).then_inc(silu_set, 1)
                    act.wait_ge(dn_loaded[pp], 16 * (kp + 1))
                    ge(act, dn_done, n - 1)
                    act.activation(dn_hi[:], dn_raw[:, pp, :, :], ACT.Copy).then_inc(dn_hi_set, 1)
                    act.wait_ge(hid_tr, n)
                    act.activation(hidT_hi[:].rearrange("p k n -> p (k n)"), bank[4][:, 0:2 * P], ACT.Copy).then_inc(hidT_hi_set, 1)
                if l is None or l < NF - 1:
                    pn, kn = slot(p, k, 1)
                    act.wait_ge(gu_loaded[pn], 32 * (kn + 1))
                    act.wait_ge(gu_half, n + 1)
                    gu_hi_half(n + 1, pn, kn, 0)
                    xgT_high(n + 1)
                    gu_hi_half(n + 1, pn, kn, 1)

            act.wait_ge(wo_done, 4 * NT)
            all_blocks(act, step)
            for t in range(NT):
                act.wait_ge(e_two, t + 1)
                if t:
                    act.wait_ge(e_sq, t)
                act.activation(junk_f[:], fin[:, t % 2, :], ACT.Square, accum_out=ss_e[:, t:t + 1]).then_inc(e_sq, 1)

        @block.vector
        def _(dve):
            def split_w_lo(w):
                dve.wait_ge(w_hi_set, w + 1)
                dve.tensor_tensor(w_lo[:, w % 2, :, :], w_raw[:, w % 2, :, :], w_hi[:, w % 2, :, :].bitcast(f32), ALU.subtract)\
                   .then_inc(w_lo_set, 1)

            dve.memset(half_neg[:], -0.5).then_inc(init_set, 1)
            dve.memset(ones_col[:], 1.0).then_inc(init_set, 1)
            dve.memset(w_bd[:], 0.0).then_inc(init_set, 1)
            dve.memset(zeros[:], 0).then_inc(init_set, 1)
            dve.memset(u_odd[:, :, 0:1], 0.0).then_inc(init_set, 1)
            dve.wait_ge(consts_in, 80)
            dve.tensor_copy(tri_ones[:, 0, :], small[:, C_TRI:C_TRI + P]).then_inc(init_set, 1)
            dve.memset(tri_ones[:, 1, :], 1.0).then_inc(init_set, 1)
            dve.wait_ge(cols_tr, 1)
            dve.tensor_copy(cols[:], bank[7][:, 0:20]).then_inc(cols_set, 1)
            for t in range(NT + 1):
                if t < NT:
                    dve.wait_ge(x_rs, t + 1)
                    dve.tensor_scalar(x_in[:, t, :], x_in[:, t, :], ss_x[:, t:t + 1], None, ALU.mult).then_inc(x_scaled, 1)
                if t:
                    u = t - 1
                    for j in range(2):
                        dve.wait_ge(x_hi, 2 * u + j + 1)
                        part = (slice(None), slice(4 * j, 4 * j + 4), slice(u * P, (u + 1) * P))
                        dve.tensor_tensor(xT_lo[part], bank[4 + j][:, :].rearrange("p (k n) -> p k n", n=P), xT_hi[part].bitcast(f32),
                                          ALU.subtract).then_inc(x_lo, 1)
            split_w_lo(0)
            split_w_lo(1)
            for g, (w, kind, s, half) in enumerate(GROUPS):
                if g in BY_DVE:
                    dve.wait_ge(proj_done, g + 1)
                    src = bank[g % 4][:, :]
                    if kind == "u":
                        c = 2 * (w % 2) + s
                        wait_evacuated(dve, g - 1)
                        top = u_top[:, c % 2, :]
                        rev = u_top[:, c % 2, HALF - 1:0:-1]
                        dve.tensor_copy(u_even[:, c, 0:1], src[:, 0:1])
                        dve.tensor_copy(u_even[:, c, HALF:HALF + 1], top[:, 0:1])
                        dve.tensor_tensor(u_even[:, c, 1:HALF], src[:, 1:HALF], rev, ALU.add)
                        dve.tensor_tensor(u_odd[:, c, 1:HALF], src[:, 1:HALF], rev, ALU.subtract).then_inc(evac_dve, 1)
                    else:
                        i = g - 24
                        if i >= 4:
                            dve.wait_ge(v_stored[i % 4], 16 * (i // 4))
                        dve.tensor_copy(v_out[:, i % 4, :], src[:, 0:256]).then_inc(evac_dve, 1)
                last_of_chunk = g + 1 == len(GROUPS) or GROUPS[g + 1][0] != w
                if last_of_chunk and w + 2 < len(CHUNKS):
                    split_w_lo(w + 2)
            for i in range(4):
                dve.wait_ge(f1_done, 5 + i)
                dve.tensor_copy(b_odd[:, i, :], bank[4 + i][:, :]).then_inc(f1_dve, 1)
            for c in range(NC):
                dve.wait_ge(f2_tmp, c + 1)
                dve.wait_ge(f2_done, 2 * c + 2)
                yo = bank[2 * (c % 2) + 1]
                dve.tensor_tensor(yT[:, c, 0:HALF], y_tmp[:, c % 2, :], yo[:, :], ALU.subtract)
                dve.tensor_tensor(yT[:, c, T - 1:HALF:-1], y_tmp[:, c % 2, 1:HALF], yo[:, 1:HALF], ALU.add).then_inc(f2_dve, 1)
            dve.wait_ge(f_mid, 1)
            dve.tensor_tensor(yT[:, :, HALF:HALF + 1].rearrange("p c o -> p (c o)"), bank[4][:, 0:NC], b_four, ALU.add).then_inc(f_mid_set, 1)

            def score(m):
                dve.wait_ge(s_done, m + 1)
                dve.wait_ge(bm_set, m + 1)
                if m >= 2:
                    dve.wait_ge(p_set, m - 1)
                dve.tensor_tensor_reduce(out=s_sb[:, m % 2, :], in0=bank[m % 3][:, 0:NK], in1=bm[:, m % 3, :], scale=1.0, scalar=3e38,
                                         op0=ALU.add, op1=ALU.min, accum_out=s_min[:, m % 4:m % 4 + 1]).then_inc(s_shift, 1)

            def pT_copy(m):
                dve.wait_ge(p_tr, m + 1)
                if m >= 2:
                    dve.wait_ge(pv_done, m - 1)
                dve.tensor_copy(pT[:, m % 2, :], bank[3 + m % 2][:, 0:NK]).then_inc(pT_dve, 1)

            def o_norm(q):
                dve.wait_ge(p_set, 8 * (q + 1))
                dve.reciprocal(r_inv[:, q % 2, :], r_sum[:, q % 2, :]).then_inc(o_inv, 1)
                dve.wait_ge(o_inv, q + 1)
                dve.wait_ge(pv_done, 8 * (q + 1))
                if q >= 2:
                    dve.wait_ge(o_tr, q - 1)
                dve.tensor_tensor(o_sb[:, q % 2, :].rearrange("p (h d) -> p h d", d=DH), bank[5 + q % 2][:, :].rearrange("p (h d) -> p h d", d=DH),
                                  r_inv[:, q % 2, :].unsqueeze(2).broadcast_to([P, HEADS, DH]), ALU.mult).then_inc(o_normed, 1)

            def split_wo_lo(i):
                n, c = i // KD, i % KD
                dve.wait_ge(wo_hi_set, i + 1)
                dve.tensor_tensor(wo_lo[n][:, c, :], wo_raw[:, i % 3, :], wo_hi[n][:, c, :].bitcast(f32), ALU.subtract).then_inc(wo_lo_set, 1)

            for m in range(M + 2):
                if m < M:
                    score(m)
                if m >= 2 and m % 2 == 1:
                    pT_copy(m - 2)
                if m == 1:
                    dve.wait_ge(f_ssum, 1)
                    dve.tensor_copy(ss_f[:], bank[7][:, 0:NT]).then_inc(f_moved, 1)
                if m >= 8 and m % 8 == 2 and m // 8 - 1 < 7:
                    o_norm(m // 8 - 1)
                if m >= 16 and m % 6 == 4 and (m - 16) // 6 < KD:
                    split_wo_lo((m - 16) // 6)
            o_norm(7)

            def m_low(t):
                for j, src in ((0, oT), (1, yT)):
                    dve.wait_ge(m_hi_set, 2 * t + j + 1)
                    part = (slice(None), slice(4 * j, 4 * j + 4), slice(t * P, (t + 1) * P))
                    last = dve.tensor_tensor(mT_lo[part], src[:, :, t * P:(t + 1) * P], mT_hi[part].bitcast(f32), ALU.subtract)
                last.then_inc(m_lo_set, 1)

            def h_rows(i):
                n, t = i // NT, i % NT
                part = h[:, t, 512 * n:512 * n + 512]
                dve.wait_ge(wo_done, 2 * i + 2)
                dve.wait_ge(xr_loaded[i % 4], 16 * (i // 4 + 1))
                dve.scalar_tensor_tensor(part, bank[2 * (i % 2) + 1][:, :], ss_f[:, t:t + 1], x_res[:, i % 4, :], ALU.mult, ALU.add).then_inc(h_part, 1)
                dve.wait_ge(h_part, i + 1)
                dve.tensor_tensor(part, bank[2 * (i % 2)][:, :], part, ALU.add).then_inc(h_set, 1)

            for t in range(4):
                m_low(t)
            dve.wait_ge(f_rs, 1)
            h_rows(0)
            m_low(4)
            m_low(5)
            h_rows(1)
            m_low(6)
            m_low(7)
            for i in range(2, NT):
                split_wo_lo(KD + i - 2)
                h_rows(i)
            split_wo_lo(2 * KD - 2)
            split_wo_lo(2 * KD - 1)
            dve.wait_ge(gmoe_in, 16)

            dve.memset(fill[:], SKIP).then_inc(fill_set, 1)
            for t in range(NT + 1):
                if t < NT:
                    h_rows(NT + t)
                    dve.wait_ge(h_rs, t + 1)
                    if t >= 2:
                        dve.wait_ge(hn_stored[t % 2], 16 * (t // 2))
                        dve.wait_ge(h_tr, 2 * (t - 1))
                    dve.scalar_tensor_tensor(hn[:, t % 2, :], h[:, t, :], ss_h[:, t:t + 1], g_moe[:], ALU.mult, ALU.mult).then_inc(hn_set, 1)
                if t:
                    u = t - 1
                    dve.wait_ge(h_tr, 2 * u + 2)
                    if u >= 2:
                        dve.wait_ge(r_done, u - 1)
                    dve.tensor_copy(hT[:, u % 2, 4:8, :].rearrange("p k n -> p (k n)"), bank[5][:, :]).then_inc(hT_set, 1)
            dve.memset(xg[:].rearrange("p a n -> p (a n)"), 0.0).then_inc(xg_zero, 1)

            links = [0]

            def link(instruction):
                links[0] += 1
                instruction.then_inc(rt, 1)
                dve.wait_ge(rt, links[0])

            def over_tiles(ap, n):
                return ap.unsqueeze(1).broadcast_to([P, NT, n])

            def over_last(ap, n):
                return ap.unsqueeze(2).broadcast_to([P, NT, n])

            iota, iotam, grp = (small[:, c:c + NF] for c in (C_IOTA, C_IOTAM, C_GRP))
            c_max, gi, m1, e1, m2, dm, ex, gsum, den, den_r, tmp, e2 = (r8[:, i, :] for i in range(12))
            dve.wait_ge(r_done, NT)
            dve.wait_ge(router_in, 64)
            link(dve.tensor_tensor(lg[:], bank[6][:, 0:NT * (NG + NF)].rearrange("p (t n) -> p t n", n=NG + NF),
                                   over_tiles(b_r[:], NG + NF), ALU.add))
            link(dve.tensor_reduce(c_max, lg[:, :, 0:NG], AX.X, ALU.max))
            dve.tensor_tensor(c_d[:], lg[:, :, 0:NG], over_last(c_max, NG), ALU.subtract).then_inc(c_sub, 1)
            dve.wait_ge(c_sub, 1)
            link(dve.tensor_scalar(c_eq[:], c_d[:], 0.0, None, ALU.is_equal))
            link(dve.scalar_tensor_tensor(c_cand[:], c_eq[:], -100.0, over_tiles(small[:, C_IOTA4:C_IOTA4 + NG], NG), ALU.mult, ALU.add))
            link(dve.tensor_reduce(gi, c_cand[:], AX.X, ALU.min))
            link(dve.tensor_tensor(f_eq[:], over_tiles(grp, NF), over_last(gi, NF), ALU.is_equal))
            link(dve.tensor_scalar(f_eq[:], f_eq[:], -1.0, BIG, ALU.add, ALU.mult))
            link(dve.tensor_tensor(f_m[:], lg[:, :, NG:], f_eq[:], ALU.add))

            def best(value, index, one_hot):
                link(dve.tensor_reduce(value, f_m[:], AX.X, ALU.max))
                link(dve.tensor_tensor(f_eq[:], f_m[:], over_last(value, NF), ALU.is_equal))
                link(dve.scalar_tensor_tensor(f_cand[:], f_eq[:], -100.0, over_tiles(iota, NF), ALU.mult, ALU.add))
                link(dve.tensor_reduce(index, f_cand[:], AX.X, ALU.min))
                link(dve.tensor_tensor(one_hot, over_tiles(iotam, NF), over_last(index, NF), ALU.is_equal))

            best(m1, e1, oh1[:])
            link(dve.scalar_tensor_tensor(f_m[:], oh1[:], -2 * BIG, f_m[:], ALU.mult, ALU.add))
            best(m2, e2, oh2[:])
            dve.tensor_tensor(oh[:], oh1[:], oh2[:], ALU.add).then_inc(oh_set, 1)
            dve.tensor_tensor(dm, m2, m1, ALU.subtract).then_inc(d_sub, 1)
            dve.wait_ge(c_exp, 1)
            link(dve.tensor_reduce(gsum, c_e[:], AX.X, ALU.add))
            dve.wait_ge(d_exp, 1)
            link(dve.tensor_scalar(den, ex, 1.0, None, ALU.add))
            link(dve.tensor_tensor(den, den, gsum, ALU.mult))
            link(dve.reciprocal(mix_w[:, 0, :], den))
            link(dve.tensor_tensor(mix_w[:, 1, :], mix_w[:, 0, :], ex, ALU.mult))
            dve.wait_ge(rank_done, 1)
            link(dve.tensor_copy(rank_i[:], bank[7][:, 0:NT * NF].rearrange("p (t n) -> p t n", n=NF)))
            link(dve.tensor_single_scalar(rank_i[:], rank_i[:], 7, ALU.arith_shift_right))
            link(dve.tensor_copy(rank_b[:], rank_i[:]))
            link(dve.scalar_tensor_tensor(rank[:], rank_b[:], float(NF * CAP - CAP), bank[7][:, 0:NT * NF].rearrange("p (t n) -> p t n", n=NF),
                                          ALU.mult, ALU.add))
            link(dve.tensor_tensor(rank[:], rank[:], over_tiles(small[:, C_SLOT:C_SLOT + NF], NF), ALU.add))
            dve.tensor_tensor(pick[:, 0, :, :], rank[:], oh1[:], ALU.mult)
            link(dve.tensor_tensor(pick[:, 1, :, :], rank[:], oh2[:], ALU.mult))
            link(dve.tensor_reduce(tmp, pick[:, 0, :, :], AX.X, ALU.add))
            link(dve.tensor_reduce(e1, pick[:, 1, :, :], AX.X, ALU.add))
            dve.tensor_copy(slot_of[:, 0, :], tmp).then_inc(slots_set, 1)
            dve.tensor_copy(slot_of[:, 1, :], e1).then_inc(slots_set, 1)
            link(dve.tensor_reduce(most[:, 0:1], bank[7][:, NT * NF:(NT + 1) * NF], AX.X, ALU.max))
            dve.tensor_copy(most_i[:, 0:1], most[:, 0:1]).then_inc(most_set, 1)

            def gu_lo_half(p1, j, n1):
                dve.wait_ge(gu_hi_set, 2 * n1 + j + 1)
                dve.tensor_tensor(gu_lo[:, 4 * j:4 * j + 4, :], gu_raw[:, p1, 4 * j:4 * j + 4, :, :].rearrange("p k a n -> p k (a n)"),
                                  gu_hi[:, 4 * j:4 * j + 4, :].bitcast(f32), ALU.subtract).then_inc(gu_lo_set, 1)

            def xgT_low(n1):
                for j in range(2):
                    dve.wait_ge(xgT_hi_set, 2 * n1 + j + 1)
                    dve.tensor_tensor(xgT_lo[:, 4 * j:4 * j + 4, :].rearrange("p k n -> p (k n)"), bank[2 + j][:, :],
                                      xgT_hi[:, 4 * j:4 * j + 4, :].rearrange("p k n -> p (k n)").bitcast(f32), ALU.subtract).then_inc(xgT_lo_set, 1)

            def y_rows_out(n2, p2, k2):
                dve.wait_ge(dn_done, n2 + 1)
                ge(dve, y_out[p2], 16 * k2)
                dve.tensor_copy(y_sb[:, p2, 0:512], bank[5][:, :])
                dve.tensor_copy(y_sb[:, p2, 512:], bank[6][:, :]).then_inc(y_set, 1)

            def step(l, e, n, k, p):
                if l == 0:
                    gu_lo_half(p, 0, n)
                    gu_lo_half(p, 1, n)
                    xgT_low(n)
                if l != 0:
                    pp, kp = slot(p, k, -1)
                    dve.wait_ge(silu_set, n)
                    ge(dve, hid_tr, n - 1)
                    dve.tensor_tensor(hid[:], act_g[:], bank[pp][:, FE:2 * FE], ALU.mult).then_inc(hid_set, 1)
                    dve.wait_ge(hidT_hi_set, n)
                    dve.tensor_tensor(hidT_lo[:].rearrange("p k n -> p (k n)"), bank[4][:, 0:2 * P],
                                      hidT_hi[:].rearrange("p k n -> p (k n)").bitcast(f32), ALU.subtract).then_inc(hidT_lo_set, 1)
                if l is None or l < NF - 1:
                    gu_lo_half(slot(p, k, 1)[0], 0, n + 1)
                if l is None or l >= 2:
                    y_rows_out(n - 2, p, k - 1)
                if l is None or l < NF - 1:
                    xgT_low(n + 1)
                    gu_lo_half(slot(p, k, 1)[0], 1, n + 1)
                if l == NF:
                    pp, kp = slot(p, k, -1)
                    y_rows_out(n - 1, pp, kp)

            all_blocks(dve, step)
            dve.wait_ge(gfin_in, 16)
            for t in range(NT + 1):
                if t < NT:
                    if t >= 2:
                        dve.wait_ge(e_sq, t - 1)
                    dve.wait_ge(yp_loaded[t % 3], 16 * (t // 3 + 1))
                    dve.scalar_tensor_tensor(fin[:, t % 2, :], y_pair[:, t % 3, 0:D], mix_w[:, 0, t:t + 1], h[:, t, :], ALU.mult, ALU.add).then_inc(e_one, 1)
                    dve.wait_ge(e_one, t + 1)
                    dve.scalar_tensor_tensor(fin[:, t % 2, :], y_pair[:, t % 3, D:], mix_w[:, 1, t:t + 1], fin[:, t % 2, :], ALU.mult, ALU.add).then_inc(e_two, 1)
                if t:
                    u = t - 1
                    dve.wait_ge(e_rs, u + 1)
                    if u >= 2:
                        dve.wait_ge(out_stored[u % 2], 16 * (u // 2))
                    dve.scalar_tensor_tensor(o_fin[:, u % 2, :], fin[:, u % 2, :], ss_e[:, u:u + 1], g_fin[:], ALU.mult, ALU.mult).then_inc(e_set, 1)

        @block.gpsimd
        def _(pool):
            rms_count = [0]

            def rms(ss, ready, value, done, n):
                pool.wait_ge(ready, value)
                pool.tensor_scalar(ss, ss, 1.0 / n, EPS, ALU.mult, ALU.add).then_inc(rms_mid, 1)
                rms_count[0] += 1
                pool.wait_ge(rms_mid, rms_count[0])
                e = half_neg[:, 0:1] if ss.shape[1] == 1 else half_neg[:, 0:1].broadcast_to(list(ss.shape))
                pool.tensor_tensor(ss, ss, e, ALU.pow).then_inc(done, 1)

            def gain_w(w):
                pool.wait_ge(w_loaded[w % 2], 16 * (w // 2 + 1))
                pool.tensor_tensor(w_raw[:, w % 2, :, :], w_raw[:, w % 2, :, :], g_mix.unsqueeze(2).broadcast_to([P, KD, 256]), ALU.mult)\
                    .then_inc(w_gained, 1)

            pool.wait_ge(init_set, HALVES)
            for t in range(NT):
                rms(ss_x[:, t:t + 1], x_sq, t + 1, x_rs, D)
                if t == 3:
                    pool.wait_ge(cols_set, 1)
                    gain_w(0)
            for w in range(1, len(CHUNKS)):
                gain_w(w)

            def gain_wo(i):
                n, c = i // KD, i % KD
                pool.wait_ge(wo_loaded[i % 3], 16 * (i // 3 + 1))
                pool.tensor_scalar(wo_raw[:, i % 3, :], wo_raw[:, i % 3, :], g_merged[:, c:c + 1], None, ALU.mult).then_inc(wo_gained, 1)

            pool.wait_ge(bias_in, 16 * (QR + 1))
            for m in range(M):
                q, hd = m // HEADS, m % HEADS
                a, b = QT[q]
                if m >= 3:
                    pool.wait_ge(s_shift, m - 2)
                z = hd * RPB_R * RPB_C + (RPB_R // 2 - 4 * a) * RPB_C + (COL_BASE[b] - QC * b) + RPB_C // 2 - Z0
                view = bass.AP(bias_g, z, [[G_LEN, P], [RPB_C, KR], [1, KC]])
                pool.tensor_tensor(bm[:, m % 3, :].rearrange("p (r w) -> p r w", w=KC), mask[:, q, :].rearrange("p (r w) -> p r w", w=KC),
                                   view, ALU.subtract).then_inc(bm_set, 1)
                if m == 2:
                    rms(ss_f[:], f_moved, 1, f_rs, DM)
                if q and hd == 6:
                    rms(ss_o[:, q - 1:q], o_sq, q, o_rs, DM)
                if m >= 12 and m % 6 == 0 and (m - 12) // 6 < KD:
                    gain_wo((m - 12) // 6)
            rms(ss_o[:, 7:8], o_sq, 8, o_rs, DM)
            for i in range(KD, 2 * KD):
                gain_wo(i)
            pool.wait_ge(wo_done, 2 * NT)
            pool.memset(zero_i[:], 0).then_inc(vals_set, 1)
            pool.iota(slot_val[:, :, :, 0], pattern=[[P, NT], [0, 2]], base=0, channel_multiplier=1).then_inc(vals_set, 1)
            pool.iota(slot_val[:, :, :, 1], pattern=[[2 * P, NT], [1, 2]], base=0, channel_multiplier=2).then_inc(vals_set, 1)
            for t in range(NT):
                rms(ss_h[:, t:t + 1], h_sq, t + 1, h_rs, D)
            pool.wait_ge(filled, 16)
            pool.wait_ge(slots_set, 2)
            pool.wait_ge(vals_set, 3)
            for t in range(NT):
                for c in range(2):
                    pool.indirect_dma_start(slot_dram, bass.IndirectOffsetOnAxis(ap=slot_of[:, c, t:t + 1], axis=0), slot_val[:, t, c, :], None)\
                        .then_inc(slots_scattered, 16)

            def gather(e2, n2, p2, k2):
                pool.tensor_tensor(idx_x[:, p2, :], slot_all[:, e2, 0:1], zero_i[:], ALU.add).then_inc(idxx_set, 1)
                pool.wait_ge(idxx_set, n2 + 1)
                pool.sem_inc(idx_seen, 1)
                pool.indirect_dma_start(xg[:, p2, :], None, hn_dram, bass.IndirectOffsetOnAxis(ap=idx_x[:, p2, :], axis=0),
                                        bounds_check=T - 1, oob_is_err=False).then_inc(xg_in[p2], 16)

            def scatter(e2, n2, p2, k2):
                pool.wait_ge(y_set, n2 + 1)
                ge(pool, y_out[p2], 16 * k2)
                pool.tensor_tensor(idx_y[:, p2, :], slot_all[:, e2, 1:2], zero_i[:], ALU.add).then_inc(idxy_set, 1)
                pool.wait_ge(idxy_set, n2 + 1)
                pool.sem_inc(idx_seen, 1)
                pool.indirect_dma_start(y_dram, bass.IndirectOffsetOnAxis(ap=idx_y[:, p2, :], axis=0), y_sb[:, p2, :], None,
                                        bounds_check=2 * T - 1, oob_is_err=False).then_inc(y_out[p2], 16)

            def step(l, e, n, k, p):
                if l == 0:
                    pool.wait_ge(slots_loaded, 16 * (n // NF + 1) if isinstance(n, int) else 16 + n // NF * 16)
                    gather(e, n, p, k)
                    pn, kn = slot(p, k, 1)
                    gather(e + 1, n + 1, pn, kn)
                if l is None or l + 2 < NF:
                    pool.wait_ge(xg_tr, n + 1)
                    gather(e + 2, n + 2, p, k + 1)
                if l != 0:
                    pp, kp = slot(p, k, -1)
                    pool.wait_ge(dn_hi_set, n)
                    pool.tensor_tensor(dn_lo[:], dn_raw[:, pp, :, :], dn_hi[:].bitcast(f32), ALU.subtract).then_inc(dn_lo_set, 1)
                if l is None or l >= 2:
                    scatter(e - 2, n - 2, p, k - 1)
                if l == NF:
                    pp, kp = slot(p, k, -1)
                    scatter(e - 1, n - 1, pp, kp)

            pool.wait_ge(xg_zero, 1)
            for i in range(2):
                pool.wait_ge(hn_stored[i], 64)
            all_blocks(pool, step)
            for t in range(NT):
                rms(ss_e[:, t:t + 1], e_sq, t + 1, e_rs, D)

        @block.tensor
        def _(pe):
            pe.wait_ge(consts_in, 80)
            pe.transpose(bank[7][:, 0:20], rows20[:], ident[0:20, 0:20]).then_inc(cols_tr, 1)
            for t in range(NT):
                pe.wait_ge(x_scaled, t + 1)
                for j in range(2):
                    if t:
                        pe.wait_ge(x_lo, 2 * (t - 1) + j + 1)
                    for k in range(4):
                        d = 4 * j + k
                        last = pe.transpose(bank[4 + j][:, k * P:(k + 1) * P], x_in[:, t, d * P:(d + 1) * P], ident)
                    last.then_inc(x_tr, 1)
            pe.wait_ge(wbd_in, 16 * FG)
            pe.wait_ge(cols_set, 1)
            for i, c in enumerate((C_CC, C_SC)):
                pe.matmul(bank[6 + i][:, :], small[:, c:c + P], w_bd[:].rearrange("p c n -> p (c n)"), start=True, stop=True).then_inc(m_done, 1)
            pe.wait_ge(x_lo, 2 * NT)
            seen = -1
            for g, (w, kind, s, half) in enumerate(GROUPS):
                if w != seen:
                    pe.wait_ge(w_lo_set, w + 1)
                    seen = w
                if g >= 4:
                    wait_evacuated(pe, g - 4)
                for k in range(KD):
                    first, last = k == 0, k == KD - 1
                    if kind == "v":
                        tok = slice(half * P, (half + 1) * P)
                        done = three(pe, bank[g % 4][:, 0:256], xT_hi[:, k, tok], xT_lo[:, k, tok],
                                     w_hi[:, w % 2, k, :], w_lo[:, w % 2, k, :], first, last)
                    else:
                        tok, col = slice(512 * half, 512 * half + 512), slice(P * s, P * s + P)
                        done = three(pe, bank[g % 4][:, :], w_hi[:, w % 2, k, col], w_lo[:, w % 2, k, col],
                                     xT_hi[:, k, tok], xT_lo[:, k, tok], first, last)
                done.then_inc(proj_done, 1)
            pe.wait_ge(m_set, 2)
            pe.wait_ge(init_set, ODD_ZERO)
            wait_evacuated(pe, 7)
            for i in range(8):
                odd, r = i // 4, i % 4
                if odd:
                    pe.wait_ge(f1_act, r + 1)
                src = u_odd if odd else u_even
                for c in range(NC):
                    last = pe.matmul(bank[4 + r][:, c * P:(c + 1) * P], src[:, c, r * P:(r + 1) * P], m_chan[:, odd, c, :], start=True, stop=True)
                last.then_inc(f1_done, 1)
            wait_evacuated(pe, 36)
            for c in range(NC):
                last = pe.matmul(bank[0][0:1, c * P:(c + 1) * P], u_even[:, c, HALF:HALF + 1], m_chan[:, 0, c, :], start=True, stop=True)
            last.then_inc(amid_done, 1)
            pe.wait_ge(dft_in, 32)
            pe.wait_ge(amid_set, 1)
            for g in (37, 38, 39):
                wait_evacuated(pe, g)
            pe.wait_ge(f1_act, 4)
            for c in range(NC):
                col = slice(c * P, (c + 1) * P)
                if c >= 2:
                    pe.wait_ge(f2_tmp, c - 1)
                for i in range(4):
                    pe.matmul(bank[2 * (c % 2)][:, :], a_even[:, i, col], dft[:, 0, i, :], start=(i == 0), stop=False)
                pe.matmul(bank[2 * (c % 2)][:, :], a_mid[0:1, col], altrow[:], start=False, stop=True).then_inc(f2_done, 1)
                pe.wait_ge(f1_dve, 4)
                if c >= 2:
                    pe.wait_ge(f2_dve, c - 1)
                for i in range(4):
                    last = pe.matmul(bank[2 * (c % 2) + 1][:, :], b_odd[:, i, col], dft[:, 1, i, :], start=(i == 0), stop=(i == 3))
                last.then_inc(f2_done, 1)
            for c in range(NC):
                col = slice(c * P, (c + 1) * P)
                for i in range(4):
                    pe.matmul(bank[4][:, c:c + 1], a_even[:, i, col], small[:, C_ALT:C_ALT + 1], start=(i == 0), stop=False)
                last = pe.matmul(bank[4][:, c:c + 1], a_mid[0:1, col], altrow[0:1, 0:1], start=False, stop=True)
            last.then_inc(f_mid, 1)

            def scores(m):
                q, hd = m // HEADS, m % HEADS
                a, b = QT[q]
                rows = slice(DH * (hd % 2), DH * (hd % 2) + DH)
                if m >= 3:
                    pe.wait_ge(s_shift, m - 2)
                grid_k = kT[rows, hd // 2, :].rearrange("p (r w) -> p r w", w=GRID_W)
                pe.matmul(bank[m % 3][:, 0:NK].rearrange("p (r w) -> p r w", w=KC), qT[rows, hd // 2, q * P:(q + 1) * P],
                          grid_k[:, 4 * a:4 * a + KR, COL_BASE[b]:COL_BASE[b] + KC], start=True, stop=True).then_inc(s_done, 1)

            def probs_T(m):
                pe.wait_ge(p_set, m + 1)
                if m >= 2:
                    wait_pT(pe, m - 2)
                for j in range(3):
                    last = pe.transpose(bank[3 + m % 2][:, j * P:(j + 1) * P], p_sb[:, m % 2, j * P:(j + 1) * P], ident)
                last.then_inc(p_tr, 1)

            def values(m):
                q, hd = m // HEADS, m % HEADS
                a, b = QT[q]
                if m == 0:
                    pe.wait_ge(vk_in, 16 * 32)
                if q >= 2 and hd == 0:
                    pe.wait_ge(o_normed, q - 1)
                wait_pT(pe, m)
                for j in range(3):
                    last = pe.matmul(bank[5 + q % 2][:, hd * DH:(hd + 1) * DH], pT[:, m % 2, j * P:(j + 1) * P],
                                     vk[:, 4 * (a + j) + b, hd * DH:(hd + 1) * DH], start=(j == 0), stop=(j == 2))
                last.then_inc(pv_done, 1)

            def o_T(q):
                pe.wait_ge(o_scaled, q + 1)
                if q:
                    pe.wait_ge(oT_set, q)
                for c in range(NC):
                    last = pe.transpose(bank[7][:, c * P:(c + 1) * P], o_sb[:, q % 2, c * P:(c + 1) * P], ident)
                last.then_inc(o_tr, 1)

            pe.wait_ge(f2_tmp, NC)
            pe.wait_ge(f2_dve, NC)
            for m in range(-2, M + 1):
                if m + 2 < M:
                    scores(m + 2)
                if 0 <= m < M:
                    probs_T(m)
                if m >= 1:
                    values(m - 1)
                if m == 0:
                    pe.wait_ge(y_squared, 1)
                    pe.wait_ge(init_set, ONES)
                    for t in range(NT):
                        for c in range(NC):
                            last = pe.matmul(bank[7][:, t:t + 1], y_sq[:, c, t * P:(t + 1) * P], ones_col[:], start=(c == 0), stop=(c == NC - 1))
                    last.then_inc(f_ssum, 1)
                if m >= 8 and m % 8 == 7 and m < M:
                    o_T(m // 8 - 1)
            o_T(7)
            for i in range(2 * NT):
                n, t = i // NT, i % NT
                tok = slice(t * P, (t + 1) * P)
                if n == 0:
                    pe.wait_ge(m_lo_set, t + 1)
                    if t == 0:
                        pe.wait_ge(wo_lo_set, KD)
                elif t == 0:
                    pe.wait_ge(wo_lo_set, 2 * KD)
                if i >= 2:
                    pe.wait_ge(h_set, i - 1)
                for part in range(2):
                    for k in range(4):
                        c = 4 * part + k
                        last = three(pe, bank[2 * (i % 2) + part][:, :], mT_hi[:, c, tok], mT_lo[:, c, tok],
                                     wo_hi[n][:, c, :], wo_lo[n][:, c, :], k == 0, k == 3)
                    last.then_inc(wo_done, 1)

                def hn_T(u):
                    pe.wait_ge(hn_set, u + 1)
                    for j in range(2):
                        if u and j == 0:
                            pe.wait_ge(hT_set_act, u)
                        if u and j == 1:
                            pe.wait_ge(hT_set, u)
                        for k in range(4):
                            d = 4 * j + k
                            last = pe.transpose(bank[4 + j][:, k * P:(k + 1) * P], hn[:, u % 2, d * P:(d + 1) * P], ident)
                        last.then_inc(h_tr, 1)

                def route(u):
                    pe.wait_ge(hT_set_act, u + 1)
                    pe.wait_ge(hT_set, u + 1)
                    pe.wait_ge(router_in, 64)
                    for k in range(KD):
                        last = pe.matmul(bank[6][:, u * (NG + NF):(u + 1) * (NG + NF)], hT[:, u % 2, k, :], w_r[:, k, :],
                                         start=(k == 0), stop=(k == KD - 1))
                    last.then_inc(r_done, 1)

                if n == 1 and t >= 1:
                    hn_T(t - 1)
                if n == 1 and t >= 2:
                    route(t - 2)
            hn_T(NT - 1)
            route(NT - 2)
            route(NT - 1)
            pe.wait_ge(oh_set, 1)
            pe.wait_ge(init_set, TRI)
            for t in range(NT + 1):
                dst = bank[7][:, t * NF:(t + 1) * NF]
                for u in range(min(t + 1, NT)):
                    last = pe.matmul(dst, tri_ones[:, 0 if u == t else 1, :], oh[:, u, :], start=(u == 0), stop=(u == min(t, NT - 1)))
            last.then_inc(rank_done, 1)

            def x_T(n1, p1, k1):
                pe.wait_ge(xg_in[p1], 16 * (k1 + 1))
                ge(pe, xgT_lo_set, 2 * n1)
                for d in range(KD):
                    last = pe.transpose(bank[2 + d // 4][:, d % 4 * P:(d % 4 + 1) * P], xg[:, p1, d * P:(d + 1) * P], ident)
                last.then_inc(xg_tr, 1)

            def gate_up(n, p, j):
                pe.wait_ge(gu_lo_set, 2 * n + j + 1)
                for k in range(4):
                    d = 4 * j + k
                    last = three(pe, bank[p][:, :], xgT_hi[:, d, :], xgT_lo[:, d, :], gu_hi[:, d, :], gu_lo[:, d, :], d == 0, d == KD - 1)
                last.then_inc(gu_done if j else gu_half, 1)

            def step(l, e, n, k, p):
                if l == 0:
                    x_T(n, p, k)
                more = l is None or l < NF
                if more:
                    pe.wait_ge(xgT_lo_set, 2 * n + 2)
                    ge(pe, hid_set, n - 1)
                    gate_up(n, p, 0)
                if l != 0:
                    pe.wait_ge(hid_set, n)
                    ge(pe, hidT_lo_set, n - 1)
                    for c in range(2):
                        last = pe.transpose(bank[4][:, c * P:(c + 1) * P], hid[:, c * P:(c + 1) * P], ident)
                    last.then_inc(hid_tr, 1)
                if more:
                    gate_up(n, p, 1)
                if l is None or l < NF - 1:
                    pn, kn = slot(p, k, 1)
                    x_T(n + 1, pn, kn)
                if l != 0:
                    pe.wait_ge(hidT_lo_set, n)
                    pe.wait_ge(dn_lo_set, n)
                    ge(pe, y_set, n - 1)
                    for c in range(2):
                        for half in range(2):
                            cols_ = slice(512 * half, 512 * half + 512)
                            last = three(pe, bank[5 + half][:, :], hidT_hi[:, c, :], hidT_lo[:, c, :],
                                         dn_hi[:, c, cols_], dn_lo[:, c, cols_], c == 0, c == 1)
                    last.then_inc(dn_done, 1)

            all_blocks(pe, step)


_INPUTS = ("x", "norm_mix", "w_in", "rpb", "w_four", "b_four", "g_attn_out", "g_four_out", "w_out", "norm_moe",
           "w_router_coarse", "b_router_coarse", "w_router_fine", "b_router_fine", "w_gate", "w_up", "w_down", "norm_final")


def kernel(**inputs):
    import concourse.bacc as bacc
    from concourse.bass_utils import run_bass_kernel_spmd

    nc = bacc.Bacc("TRN2", target_bir_lowering=False, num_devices=1)
    arrays = {name: np.ascontiguousarray(inputs[name]) for name in _INPUTS}
    arrays.update(constants())
    io = {name: nc.dram_tensor(name, a.shape, mybir.dt.float32, kind="ExternalInput").ap() for name, a in arrays.items()}
    out = nc.dram_tensor("out", (1, T, D), mybir.dt.float32, kind="ExternalOutput").ap()
    build(nc, io, out)
    result = run_bass_kernel_spmd(nc, [arrays], core_ids=[0])
    return result.results[0]["out"]
```

```python
import concourse.bass as bass
import concourse.mybir as mybir
import numpy as np
from contextlib import ExitStack

P = 128
T, D = 1024, 1024
NT, KD = T // P, D // P
GRID_W, ROWS = 64, 16
HEADS, DH = 8, 64
WIN_H, WIN_W = 8, 16
DM = 512
NC = DM // P
QR, QC = 8, 16
KR, KC = 12, 32
NK = KR * KC
COL_BASE = (0, 8, 24, 32)
RPB_R, RPB_C = 2 * WIN_H - 1, 2 * WIN_W - 1
FG = 8
HALF = T // 2
NG, NF = 4, 32
EPG = NF // NG
FE = 256
CAP = P
BLOCKS = T // CAP
SLOTS = BLOCKS * NF * CAP
SKIP = 1 << 20
EPS = 1e-6
BIG = 1e30

RPB_PAD = 160
RPB_N = HEADS * RPB_R * RPB_C
Z0 = (RPB_R // 2 - 4) * RPB_C - 1
G_LEN = (HEADS - 1) * RPB_R * RPB_C + (KR - 1 + RPB_R // 2) * RPB_C + (KC - 1) + RPB_C // 2 - Z0 + 1

C_ID, C_TRI, C_CC, C_SC = 0, 128, 256, 384
C_IOTA, C_IOTAM, C_GRP, C_SLOT, C_IOTA4, C_ALT = 512, 544, 576, 608, 640, 644
C_N = 648
S_SLOT, S_ROW, S_TILE = 0, P, P + 1
S_N = P + 1 + 2 * NT


def constants():
    k = np.arange(HALF)
    ang = 2 * np.pi * ((k[:, None] * k[None, :]) % T) / T
    dft = np.stack([np.cos(ang), np.sin(ang)], 0).reshape(2, 4, P, HALF).transpose(2, 0, 1, 3)
    c = np.arange(FG * 8)
    small = np.zeros((P, C_N))
    small[:, C_ID:C_ID + P] = np.eye(P)
    small[:, C_TRI:C_TRI + P] = np.arange(P)[:, None] < np.arange(P)[None, :]
    a2 = 2 * np.pi * ((c[:, None] * c[None, :]) % 64) / 64
    for i in range(2):
        s = slice(64 * i, 64 * i + 64)
        small[s, C_CC + 64 * i:C_CC + 64 * i + 64] = np.cos(a2) / 256
        small[s, C_SC + 64 * i:C_SC + 64 * i + 64] = np.sin(a2) / 256
    e = np.arange(NF)
    small[:, C_IOTA:C_IOTA + NF] = e
    small[:, C_IOTAM:C_IOTAM + NF] = e - 100
    small[:, C_GRP:C_GRP + NF] = e // EPG - 100
    small[:, C_SLOT:C_SLOT + NF] = e * CAP
    small[:, C_IOTA4:C_IOTA4 + NG] = np.arange(NG)
    small[:, C_ALT] = 1 - 2 * (np.arange(P) % 2)
    slots = np.zeros((P, S_N))
    slots[:, S_SLOT:S_SLOT + P] = np.arange(P)
    slots[:, S_ROW] = np.arange(P) + 1
    slots[:, S_TILE:] = P * np.arange(2 * NT)
    altrow = (1 - 2 * (np.arange(HALF) % 2))[None]
    mask = np.full((P, 8, KR, KC), BIG)
    for a in range(2):
        for b in range(4):
            for i in range(QR):
                for cc in range(QC):
                    r, col = QR * a + i, QC * b + cc
                    rs = min(max(r - WIN_H // 2, 0), ROWS - WIN_H)
                    cs = min(max(col - WIN_W // 2, 0), GRID_W - WIN_W)
                    j0, k0 = rs - 4 * a, cs - COL_BASE[b]
                    mask[QC * i + QC - 1 - cc, 4 * a + b, j0:j0 + WIN_H, k0:k0 + WIN_W] = 0
    f = np.float32
    return {"c_dft": np.ascontiguousarray(dft.reshape(P, -1)).astype(f), "c_small": small.astype(f), "c_slots": slots.astype(f),
            "c_alt": altrow.astype(f), "c_mask": mask.reshape(P, -1).astype(f)}


def build(nc, io, out):
    f32, f32r, bf16 = mybir.dt.float32, mybir.dt.float32r, mybir.dt.bfloat16
    i32, u32 = mybir.dt.int32, mybir.dt.uint32
    ALU, ACT, AX = mybir.AluOpType, mybir.ActivationFunctionType, mybir.AxisListType

    v_dram = nc.dram_tensor("v_rows", (T, DM), f32).ap()
    rpb_dram = nc.dram_tensor("rpb_padded", (1, RPB_N + 2 * RPB_PAD), f32)
    hn_dram = nc.dram_tensor("hn_rows", (T, D), f32).ap()
    slot_dram = nc.dram_tensor("slot_table", (SLOTS, 2), u32).ap()
    y_dram = nc.dram_tensor("y_rows", (2 * T, D), f32).ap()

    w_in = io["w_in"].rearrange("o (k p) n -> p (o k) n", p=P)
    w_out = io["w_out"].rearrange("o (k p) n -> p (o k) n", p=P)
    w_gate = io["w_gate"].rearrange("o e (k p) n -> p (o e) k n", p=P)
    w_up = io["w_up"].rearrange("o e (k p) n -> p (o e) k n", p=P)
    w_down = io["w_down"].rearrange("o e (k p) n -> p (o e) k n", p=P)
    x_rows = io["x"].rearrange("o (t p) n -> p (o t) n", p=P)
    out_rows = out.rearrange("o (t p) n -> p (o t) n", p=P)
    hn_rows = hn_dram.rearrange("(t p) n -> p t n", p=P)
    y_rows = y_dram.rearrange("(k t p) n -> p t k n", p=P, k=2)

    ctx = ExitStack()
    BASE = 16512

    def at(name, kb, shape, dtype=f32):
        return nc.alloc_sbuf_tensor_at(name, shape, dtype, offset=BASE + int(kb * 32) * 32)

    def sem(name):
        return ctx.enter_context(nc.semaphore(name))

    with ctx:
        small = at("small", 0, [P, C_N])
        ident = small[:, C_ID:C_ID + P]
        tri_ones = at("tri_ones", 2.6, [P, 2, P], bf16)
        rows20 = at("rows20", 3.15, [20, P])
        cols = at("cols", 3.7, [P, 20])
        g_mix, g_merged, b_four = cols[:, 0:8], cols[:, 8:16], cols[:, 16:20]
        half_neg = at("half_neg", 3.8, [P, 1])
        ss_x = at("ss_x", 3.82, [P, 8])
        ss_h = at("ss_h", 3.86, [P, 8])
        ss_f = at("ss_f", 3.9, [P, 8])
        xT_hi = at("xT_hi", 4, [P, KD, T], f32r)
        xT_lo = at("xT_lo", 36, [P, KD, T], f32r)
        x_in = at("x_in", 68, [P, NT, D])
        qT = at("qT", 68, [P, NC, T])
        kT = at("kT", 84, [P, NC, T])
        w_raw = at("w_raw", 100, [P, 2, KD, 256])
        w_hi = at("w_hi", 116, [P, 2, KD, 256], f32r)
        w_lo = at("w_lo", 132, [P, 2, KD, 256], f32r)
        u_even = at("u_even", 148, [P, NC, HALF + 1])
        u_odd = at("u_odd", 156.5, [P, NC, HALF])
        u_top = at("u_top", 165, [P, 2, HALF])
        v_out = at("v_out", 177, [P, 4, 256])
        dft = at("dft", 181, [P, 2, 4, HALF])
        m_chan = at("m_chan", 197, [P, 2, NC, P])
        w_bd = at("w_bd", 201, [P, NC, P])
        altrow = at("altrow", 203, [1, HALF])
        zeros = at("zeros", 205, [P, 512], u32)
        junk_x = at("junk_x", 165, [P, D])
        slot_c = at("slot_c", 207, [P, S_N])
        ones_col = at("ones_col", 3.98, [P, 1])
        a_even = at("a_even", 128, [P, 4, DM])
        b_odd = at("b_odd", 136, [P, 4, DM])
        a_mid = at("a_mid", 144, [1, DM])
        y_tmp = at("y_tmp", 165, [P, 2, HALF])
        y_sq = at("y_sq", 148, [P, NC, T])
        yT = at("yT", 52, [P, NC, T])
        vk = at("vk", 4, [P, 16, DM])
        bias_g = at("bias_g", 100, [P, G_LEN])
        mask = at("mask", 116, [P, 8, NK])
        bm = at("bm", 36, [P, 3, NK])
        s_sb = at("s_sb", 40.5, [P, 2, NK])
        p_sb = at("p_sb", 43.5, [P, 2, NK])
        pT = at("pT", 46.5, [P, 2, NK])
        s_min = at("s_min", 49.5, [P, 4])
        r_sum = at("r_sum", 49.6, [P, 2, 8])
        r_inv = at("r_inv", 49.7, [P, 2, 8])
        ss_o = at("ss_o", 49.8, [P, 8])
        junk_o = at("junk_o", 50, [P, DM])
        oT = at("oT", 148, [P, NC, T])
        o_sb = at("o_sb", 197, [P, 2, DM])
        wo_raw = at("wo_raw", 201, [P, 3, 512])
        wo_hi = [at("wo_hi0", 181, [P, KD, 512], f32r), at("wo_hi1", 4, [P, KD, 512], f32r)]
        wo_lo = [at("wo_lo0", 165, [P, KD, 512], f32r), at("wo_lo1", 20, [P, KD, 512], f32r)]
        mT_hi = at("mT_hi", 68, [P, KD, T], f32r)
        mT_lo = at("mT_lo", 100, [P, KD, T], f32r)
        h = at("h", 36, [P, NT, D])
        x_res = at("x_res", 132, [P, 4, 512])
        hn = at("hn", 140, [P, 2, D])
        junk_h = at("junk_h", 148, [P, D])
        g_moe = at("g_moe", 152, [P, D])
        w_r = at("w_r", 156, [P, KD, NG + NF])
        b_r = at("b_r", 157.2, [P, NG + NF])
        fill = at("fill", 158, [P, 512], u32)
        hT = at("hT", 165, [P, 2, KD, P])
        lg = at("lg", 173, [P, NT, NG + NF])
        c_d = at("c_d", 174.2, [P, NT, NG])
        c_e = at("c_e", 174.4, [P, NT, NG])
        c_eq = at("c_eq", 174.6, [P, NT, NG])
        c_cand = at("c_cand", 174.8, [P, NT, NG])
        r8 = at("r8", 175, [P, 12, NT])
        f_m = at("f_m", 176, [P, NT, NF])
        f_eq = at("f_eq", 177, [P, NT, NF])
        f_cand = at("f_cand", 178, [P, NT, NF])
        oh1 = at("oh1", 197, [P, NT, NF])
        oh2 = at("oh2", 198, [P, NT, NF])
        oh = at("oh", 181, [P, NT, NF], bf16)
        rank = at("rank", 182, [P, NT, NF])
        rank_i = at("rank_i", 183, [P, NT, NF], i32)
        rank_b = at("rank_b", 184, [P, NT, NF])
        pick = at("pick", 185, [P, 2, NT, NF])
        sel = at("sel", 160, [P, 2, NT, 2, NF], bf16)
        in_slot = at("in_slot", 187, [P, 2, NT, P], bf16)
        table = at("table", 162, [P, 4, NF])
        gu_raw = at("gu_raw", 68, [P, 2, KD, 2, FE])
        dn_raw = at("dn_raw", 100, [P, 2, 2, D])
        gu_hi = at("gu_hi", 4, [P, KD, 2 * FE], f32r)
        gu_lo = at("gu_lo", 20, [P, KD, 2 * FE], f32r)
        dn_hi = at("dn_hi", 116, [P, 2, 2, D], f32r)
        dn_lo = at("dn_lo", 165, [P, 2, 2, D], f32r)
        xg = at("xg", 132, [P, 2, D])
        xgT_hi = at("xgT_hi", 140, [P, KD, P], f32r)
        xgT_lo = at("xgT_lo", 144, [P, KD, P], f32r)
        act_g = at("act_g", 148, [P, FE])
        hid = at("hid", 149, [P, FE])
        hidT_hi = at("hidT_hi", 150, [P, 2, P], f32r)
        hidT_lo = at("hidT_lo", 151, [P, 2, P], f32r)
        y_sb = at("y_sb", 187, [P, 2, D])
        slot_all = at("slot_all", 195, [P, NF, 2], u32)
        slot_val = at("slot_val", 195.3, [P, NT, 2, 2], u32)
        slot_f = at("slot_f", 199, [P, 2, NT])
        slot_of = at("slot_of", 195.5, [P, 2, NT], u32)
        mix_w = at("mix_w", 195.6, [P, 2, NT])
        idx_x = at("idx_x", 195.7, [P, 2, 1], u32)
        idx_y = at("idx_y", 195.72, [P, 2, 1], u32)
        zero_i = at("zero_i", 195.75, [P, 1], u32)
        most = at("most", 195.8, [P, 2], f32)
        most_i = at("most_i", 195.9, [P, 2], i32)
        y_pair = at("y_pair", 68, [P, NT, 2, D])
        g_fin = at("g_fin", 152, [P, D])
        fin = at("fin", 4, [P, 3, D])
        o_fin = at("o_fin", 16, [P, 4, D])
        junk_f = at("junk_f", 32, [P, D])
        ss_e = at("ss_e", 156, [P, 8])

        bank = [ctx.enter_context(nc.psum_tensor(f"bank{i}", [P, 512], f32)) for i in range(8)]

        consts_in, wbd_in, dft_in = (sem(n) for n in ("consts_in", "wbd_in", "dft_in"))
        x_loaded = [sem(f"x_loaded{t}") for t in range(NT)]
        w_loaded = [sem(f"w_loaded{i}") for i in range(2)]
        init_set, fill_set, rms_mid = (sem(n) for n in ("init_set", "fill_set", "rms_mid"))
        HALVES, ONES, WBD_ZERO, ZEROS, ODD_ZERO, TRI = 1, 2, 3, 4, 5, 7
        cols_tr, cols_set, m_done, m_set = (sem(n) for n in ("cols_tr", "cols_set", "m_done", "m_set"))
        x_sq, x_rs, x_scaled, x_tr, x_hi, x_lo = (sem(n) for n in ("x_sq", "x_rs", "x_scaled", "x_tr", "x_hi", "x_lo"))
        w_gained, w_hi_set, w_lo_set, proj_done, evac_act, evac_dve = (
            sem(n) for n in ("w_gained", "w_hi_set", "w_lo_set", "proj_done", "evac_act", "evac_dve"))
        v_stored = [sem(f"v_stored{i}") for i in range(4)]
        vk_in, rpb_mid, bias_in = (sem(n) for n in ("vk_in", "rpb_mid", "bias_in"))
        f1_done, f1_act, f1_dve, f2_done, f2_tmp, f2_dve, f_mid, f_mid_set, y_squared, y_summed, f_moved, f_rs = (
            sem(n) for n in ("f1_done", "f1_act", "f1_dve", "f2_done", "f2_tmp", "f2_dve", "f_mid", "f_mid_set", "y_squared", "y_summed", "f_moved", "f_rs"))
        bm_set, s_done, s_shift, p_set, p_tr, pT_act, pT_dve, pv_done = (
            sem(n) for n in ("bm_set", "s_done", "s_shift", "p_set", "p_tr", "pT_act", "pT_dve", "pv_done"))
        o_inv, o_normed, o_sq, o_rs, o_scaled, o_tr, oT_set = (
            sem(n) for n in ("o_inv", "o_normed", "o_sq", "o_rs", "o_scaled", "o_tr", "oT_set"))
        wo_loaded = [sem(f"wo_loaded{i}") for i in range(3)]
        wo_gained, wo_hi_set, wo_lo_set, m_hi_set, m_lo_set, wo_done, h_part, h_set = (
            sem(n) for n in ("wo_gained", "wo_hi_set", "wo_lo_set", "m_hi_set", "m_lo_set", "wo_done", "h_part", "h_set"))
        xr_loaded = [sem(f"xr_loaded{i}") for i in range(4)]
        gmoe_in, router_in, filled = (sem(n) for n in ("gmoe_in", "router_in", "filled"))
        h_sq, h_rs, hn_set, h_tr, hT_set, r_done = (sem(n) for n in ("h_sq", "h_rs", "hn_set", "h_tr", "hT_set", "r_done"))
        hn_stored = [sem(f"hn_stored{i}") for i in range(2)]
        rt, c_sub, c_exp, d_sub, d_exp, oh_set, rank_done, slots_set, vals_set, slots_scattered = (
            sem(n) for n in ("rt", "c_sub", "c_exp", "d_sub", "d_exp", "oh_set", "rank_done", "slots_set", "vals_set", "slots_scattered"))
        slots_loaded, xg_zero, most_set, gu_half, amid_done, amid_set = (
            sem(n) for n in ("slots_loaded", "xg_zero", "most_set", "gu_half", "amid_done", "amid_set"))
        f_ssum, hT_set_act = (sem(n) for n in ("f_ssum", "hT_set_act"))
        slotc_in, sel_set, in_slot_set, table_done, table_set = (
            sem(n) for n in ("slotc_in", "sel_set", "in_slot_set", "table_done", "table_set"))
        gu_loaded = [sem(f"gu_loaded{i}") for i in range(2)]
        dn_loaded = [sem(f"dn_loaded{i}") for i in range(2)]
        gu_hi_set, gu_lo_set, dn_hi_set, dn_lo_set = (sem(n) for n in ("gu_hi_set", "gu_lo_set", "dn_hi_set", "dn_lo_set"))
        idxx_set, idxy_set, idx_seen = sem("idxx_set"), sem("idxy_set"), sem("idx_seen")
        xg_in = [sem(f"xg_in{i}") for i in range(2)]
        y_out = [sem(f"y_out{i}") for i in range(2)]
        xg_tr, xgT_hi_set, xgT_lo_set, gu_done, silu_set, hid_set, hid_tr, hidT_hi_set, hidT_lo_set, dn_done, y_set = (
            sem(n) for n in ("xg_tr", "xgT_hi_set", "xgT_lo_set", "gu_done", "silu_set", "hid_set", "hid_tr",
                             "hidT_hi_set", "hidT_lo_set", "dn_done", "y_set"))
        yp_loaded = x_loaded
        gfin_in, e_one, e_two, e_sq, e_rs, e_set = (sem(n) for n in ("gfin_in", "e_one", "e_two", "e_sq", "e_rs", "e_set"))
        out_stored = [sem(f"out_stored{i}") for i in range(4)]

        block = ctx.enter_context(nc.Block())

        CHUNKS = [("u", 3 * DM), ("u", 3 * DM + 256), ("q", 0), ("q", 256), ("k", DM), ("k", DM + 256),
                  ("v", 2 * DM), ("v", 2 * DM + 256)]
        GROUPS = []
        for w, (kind, _) in enumerate(CHUNKS):
            if kind == "v":
                GROUPS += [(w, kind, None, t) for t in range(NT)]
            elif w == 0:
                GROUPS += [(w, kind, s, half) for half in (0, 1) for s in range(2)]
            else:
                GROUPS += [(w, kind, s, half) for s in range(2) for half in (1, 0)]
        CHUNK_END = [sum(x[0] <= w for x in GROUPS) for w in range(len(CHUNKS))]
        BY_ACT = [g for g, (_, kind, _, half) in enumerate(GROUPS) if kind in "qk" or (kind == "u" and half == 1)]
        BY_DVE = [g for g in range(len(GROUPS)) if g not in BY_ACT]

        def u_group(c, half):
            return GROUPS.index((c // 2, "u", c % 2, half))

        def x_bank(t, j):
            return bank[4 + 2 * (t % 2) + j]

        def wait_evacuated(eng, g):
            if g in BY_ACT:
                eng.wait_ge(evac_act, BY_ACT.index(g) + 1)
            else:
                eng.wait_ge(evac_dve, BY_DVE.index(g) + 1)

        QT = [(a, b) for a in range(2) for b in range(4)]
        M = len(QT) * HEADS

        def wait_pT(eng, m):
            eng.wait_ge(pT_dve if m % 2 else pT_act, m // 2 + 1)

        def three(pe, dst, hi, lo, rhi, rlo, first, last):
            pe.matmul(dst, hi, rhi, start=first, stop=False)
            pe.matmul(dst, hi, rlo, start=False, stop=False)
            return pe.matmul(dst, lo, rhi, start=False, stop=last)

        def chunk_c(w):
            return CHUNKS[w][1]

        def slot(p, k, d):
            return (p + d) % 2, k + (p + d) // 2

        def ge(eng, which, value):
            if not isinstance(value, int) or value > 0:
                eng.wait_ge(which, value)

        def expert_pass(eng, step, b):
            def peeled(l):
                step(l, l, NF * b + l, NF // 2 * b + l // 2, l % 2)
            for l in range(4):
                peeled(l)
            with eng.Fori(2, NF // 2 - 1) as i:
                for p in range(2):
                    step(None, 2 * i + p, NF * b + 2 * i + p, NF // 2 * b + i, p)
            for l in (NF - 2, NF - 1, NF):
                peeled(l)

        def all_blocks(eng, step, before=None):
            expert_pass(eng, step, 0)
            eng.wait_ge(most_set, 1)
            over = eng.value_load(most_i[0:1, 0:1])
            with eng.If(over > CAP):
                if before:
                    before()
                with eng.Fori(1, BLOCKS) as b:
                    expert_pass(eng, step, b)
            with eng.Else():
                eng.nop()
            eng.nop()

        @block.sync
        def _(sp):
            sp.dma_start(small[:], io["c_small"]).then_inc(consts_in, 16)
            sp.dma_start(slot_c[:], io["c_slots"]).then_inc(slotc_in, 16)
            for t in range(NT):
                sp.dma_start(x_in[:, t, :], x_rows[:, t, :]).then_inc(x_loaded[t], 16)
                if t in (2, 5):
                    w = 0 if t == 2 else 1
                    sp.dma_start(w_raw[:, w, :, :], w_in[:, :, chunk_c(w):chunk_c(w) + 256]).then_inc(w_loaded[w], 16)
                if t == 0:
                    for k, name in ((0, "norm_mix"), (8, "g_attn_out"), (12, "g_four_out"), (16, "b_four")):
                        src = io[name].rearrange("o (k p) -> (o k) p", p=P)
                        sp.dma_start(rows20[k:k + src.shape[0], :], src).then_inc(consts_in, 16)
            sp.wait_ge(init_set, WBD_ZERO)
            for g in range(FG):
                o = 64 * (g % 2)
                sp.dma_start(w_bd[o:o + 64, g // 2, o:o + 64], io["w_four"][0, g]).then_inc(wbd_in, 16)
            sp.dma_start(dft[:].rearrange("p a b c -> p (a b c)"), io["c_dft"]).then_inc(dft_in, 16)
            sp.dma_start(altrow[:], io["c_alt"]).then_inc(dft_in, 16)
            sp.wait_ge(init_set, ZEROS)
            rp = rpb_dram.ap()
            sp.dma_start(rp[:, RPB_PAD:RPB_PAD + RPB_N], io["rpb"].rearrange("o h a b -> o (h a b)")).then_inc(rpb_mid, 16)
            for o in (0, RPB_PAD + RPB_N):
                sp.dma_start(rp[:, o:o + RPB_PAD], zeros[0:1, 0:RPB_PAD].bitcast(f32)).then_inc(rpb_mid, 16)
            for w in range(2, len(CHUNKS)):
                sp.wait_ge(w_lo_set, w - 1)
                sp.dma_start(w_raw[:, w % 2, :, :], w_in[:, :, chunk_c(w):chunk_c(w) + 256]).then_inc(w_loaded[w % 2], 16)
            v_at = 0
            for w in (6, 7):
                for t in range(NT):
                    g = 24 + v_at
                    wait_evacuated(sp, g)
                    sp.dma_start(v_dram[t * P:(t + 1) * P, 256 * (w - 6):256 * (w - 5)], v_out[:, v_at % 4, :])\
                      .then_inc(v_stored[v_at % 4], 16)
                    v_at += 1
            for i in range(4):
                sp.wait_ge(v_stored[i], 64)
            sp.wait_ge(proj_done, len(GROUPS))
            for g in range(4):
                for j in range(4):
                    for lo_b, hi_b in ((0, 3), (1, 2)):
                        row = (4 * g + j) * GRID_W + COL_BASE[lo_b]
                        gap = COL_BASE[hi_b] - COL_BASE[lo_b]
                        src = bass.AP(v_dram.tensor, row * DM, [[DM, KC], [gap * DM, 2], [1, DM]])
                        dst = vk[32 * j:32 * j + 32, 4 * g + lo_b:4 * g + hi_b + 1:hi_b - lo_b, :]
                        sp.dma_start(dst, src).then_inc(vk_in, 16)
            sp.wait_ge(rpb_mid, 48)
            for i in range(QR):
                src = bass.AP(rpb_dram, RPB_PAD + Z0 - RPB_C * i - (QC - 1), [[1, QC], [1, G_LEN]])
                sp.dma_start(bias_g[QC * i:QC * i + QC, :], src).then_inc(bias_in, 16)
            sp.dma_start(mask[:].rearrange("p a b -> p (a b)"), io["c_mask"]).then_inc(bias_in, 16)
            sp.wait_ge(f_rs, 1)
            def load_wo(i):
                n, c = i // KD, i % KD
                if i >= 3:
                    sp.wait_ge(wo_lo_set, i - 2)
                sp.dma_start(wo_raw[:, i % 3, :], w_out[:, c, 512 * n:512 * n + 512]).then_inc(wo_loaded[i % 3], 16)

            def load_xr(i):
                n, t = i // NT, i % NT
                if i >= 4:
                    sp.wait_ge(h_part, i - 3)
                sp.dma_start(x_res[:, i % 4, :], x_rows[:, t, 512 * n:512 * n + 512]).then_inc(xr_loaded[i % 4], 16)

            for i in range(KD + 3):
                load_wo(i)
            for i in range(4):
                load_xr(i)
            for i in range(KD + 3, 2 * KD):
                load_xr(i - KD + 1)
                load_wo(i)
            sp.wait_ge(m_lo_set, NT)
            sp.dma_start(g_moe[:], io["norm_moe"].partition_broadcast(P).rearrange("p o n -> p (o n)")).then_inc(gmoe_in, 16)
            sp.dma_start(w_r[:, :, 0:NG], io["w_router_coarse"].rearrange("o (k p) n -> p (o k) n", p=P)).then_inc(router_in, 16)
            sp.dma_start(w_r[:, :, NG:], io["w_router_fine"].rearrange("o (k p) n -> p (o k) n", p=P)).then_inc(router_in, 16)
            sp.dma_start(b_r[:, 0:NG], io["b_router_coarse"].partition_broadcast(P).rearrange("p o n -> p (o n)")).then_inc(router_in, 16)
            sp.dma_start(b_r[:, NG:], io["b_router_fine"].partition_broadcast(P).rearrange("p o n -> p (o n)")).then_inc(router_in, 16)
            def store_hn(t):
                sp.wait_ge(hn_set, t + 1)
                sp.dma_start(hn_rows[:, t, :], hn[:, t % 2, :]).then_inc(hn_stored[t % 2], 16)

            for i in range(9, 2 * NT):
                load_xr(i)
                if i == 9:
                    sp.wait_ge(fill_set, 1)
                    sp.dma_start(slot_dram.rearrange("(p a) b -> p (a b)", p=P), fill[:]).then_inc(filled, 16)
                if i >= 12:
                    store_hn(i - 12)
            for t in range(4, NT):
                store_hn(t)
            sp.wait_ge(wo_done, 4 * NT)

            def load_gu(n, e, p, reuse):
                if reuse:
                    sp.wait_ge(gu_hi_set, 2 * (n - 1))
                    sp.wait_ge(gu_lo_set, 2 * (n - 1))
                sp.dma_start(gu_raw[:, p, :, 0, :], w_gate[:, e, :, :]).then_inc(gu_loaded[p], 16)
                sp.dma_start(gu_raw[:, p, :, 1, :], w_up[:, e, :, :]).then_inc(gu_loaded[p], 16)

            def load_dn(n, e, p, reuse):
                if reuse:
                    sp.wait_ge(dn_hi_set, n - 1)
                    sp.wait_ge(dn_lo_set, n - 1)
                sp.dma_start(dn_raw[:, p, :, :], w_down[:, e, :, :]).then_inc(dn_loaded[p], 16)

            def one(e):
                return bass.ds(e, 1)

            def load_expert(n, e, p, reuse):
                if isinstance(e, int):
                    load_gu(n, e, p, reuse)
                    load_dn(n, e, p, reuse)
                    return
                if reuse:
                    sp.wait_ge(gu_hi_set, 2 * (n - 1))
                    sp.wait_ge(gu_lo_set, 2 * (n - 1))
                sp.dma_start(gu_raw[:, p, :, 0, :], w_gate[:, one(e), :, :].rearrange("p o k n -> p (o k) n")).then_inc(gu_loaded[p], 16)
                sp.dma_start(gu_raw[:, p, :, 1, :], w_up[:, one(e), :, :].rearrange("p o k n -> p (o k) n")).then_inc(gu_loaded[p], 16)
                if reuse:
                    sp.wait_ge(dn_hi_set, n - 1)
                    sp.wait_ge(dn_lo_set, n - 1)
                sp.dma_start(dn_raw[:, p, :, :], w_down[:, one(e), :, :].rearrange("p o k n -> p (o k) n")).then_inc(dn_loaded[p], 16)

            load_expert(0, 0, 0, False)
            load_expert(1, 1, 1, False)
            sp.dma_start(g_fin[:], io["norm_final"].rearrange("(o n) -> o n", o=1).partition_broadcast(P).rearrange("p o n -> p (o n)")).then_inc(gfin_in, 16)
            with sp.Fori(1, NF // 2) as i:
                for p in range(2):
                    load_expert(2 * i + p, 2 * i + p, p, True)
            sp.wait_ge(most_set, 1)
            over = sp.value_load(most_i[0:1, 0:1])
            with sp.If(over > CAP):
                sp.wait_ge(slots_scattered, 16 * 2 * NT)
                with sp.Fori(1, BLOCKS) as b:
                    sp.wait_ge(idxx_set, NF * b)
                    sp.wait_ge(idxy_set, NF * b)
                    sp.dma_start(slot_all[:], slot_dram[bass.ds(b * NF * CAP, NF * CAP), :].rearrange("(e s) b -> s e b", s=CAP))\
                      .then_inc(slots_loaded, 16)
                    with sp.Fori(0, NF // 2) as i:
                        for p in range(2):
                            load_expert(NF * b + 2 * i + p, 2 * i + p, p, True)
                sp.wait_ge(y_out[0], 16 * NF // 2 * BLOCKS)
                sp.wait_ge(y_out[1], 16 * NF // 2 * BLOCKS)
            with sp.Else():
                sp.wait_ge(y_out[0], 16 * NF // 2)
                sp.wait_ge(y_out[1], 16 * NF // 2)
            for t in range(NT):
                sp.dma_start(y_pair[:, t, :, :], y_rows[:, t, :, :]).then_inc(yp_loaded[t], 16)
            for t in range(NT):
                sp.wait_ge(e_set, t + 1)
                sp.dma_start(out_rows[:, t, :], o_fin[:, t % 4, :]).then_inc(out_stored[t % 4], 16)
            for i in range(4):
                sp.wait_ge(out_stored[i], 32)
            for i in range(2):
                sp.wait_ge(hn_stored[i], 64)
            sp.wait_ge(filled, 16)

        @block.scalar
        def _(act):
            def split_w_hi(w):
                act.wait_ge(w_gained, w + 1)
                if w >= 2:
                    act.wait_ge(proj_done, CHUNK_END[w - 2])
                act.activation(w_hi[:, w % 2, :, :], w_raw[:, w % 2, :, :], ACT.Copy).then_inc(w_hi_set, 1)

            def x_square(t):
                act.wait_ge(x_loaded[t], 16)
                if t:
                    act.wait_ge(x_sq, t)
                act.activation(junk_x[:],
                               x_in[:, t, :], ACT.Square, accum_out=ss_x[:, t:t + 1]).then_inc(x_sq, 1)

            act.wait_ge(consts_in, 80)
            x_square(0)
            x_square(1)
            for t in range(NT):
                if t + 2 < NT:
                    x_square(t + 2)
                for j in range(2):
                    act.wait_ge(x_tr, 2 * t + j + 1)
                    act.activation(xT_hi[:, 4 * j:4 * j + 4, t * P:(t + 1) * P], x_bank(t, j)[:, :].rearrange("p (k n) -> p k n", n=P),
                                   ACT.Copy).then_inc(x_hi, 1)
                if t == 3:
                    split_w_hi(0)
            split_w_hi(1)
            for g, (w, kind, s, half) in enumerate(GROUPS):
                if g in BY_ACT:
                    act.wait_ge(proj_done, g + 1)
                    src = bank[g % 4][:, :]
                    c = 2 * (w % 2) + (s or 0)
                    if kind == "u":
                        if c >= 2:
                            wait_evacuated(act, u_group(c - 2, 0))
                        act.activation(u_top[:, c % 2, :], src, ACT.Copy).then_inc(evac_act, 1)
                    elif kind == "q":
                        dst = qT[:, c, 512 * half:512 * half + 512].rearrange("p (b i w) -> p i b w", b=4, i=QR)[:, :, :, ::-1]
                        act.activation(dst, src.rearrange("p (i b w) -> p i b w", i=QR, b=4), ACT.Copy, scale=-DH ** -0.5).then_inc(evac_act, 1)
                    else:
                        act.activation(kT[:, c, 512 * half:512 * half + 512], src, ACT.Copy).then_inc(evac_act, 1)
                last_of_chunk = g + 1 == len(GROUPS) or GROUPS[g + 1][0] != w
                if last_of_chunk and w + 2 < len(CHUNKS):
                    split_w_hi(w + 2)
                if g == 8:
                    act.wait_ge(m_done, 2)
                    for i in range(2):
                        act.activation(m_chan[:, i, :, :].rearrange("p c n -> p (c n)"), bank[6 + i][:, :], ACT.Copy).then_inc(m_set, 1)
            for i in range(4):
                act.wait_ge(f1_done, i + 1)
                act.activation(a_even[:, i, :], bank[4 + i][:, :], ACT.Copy).then_inc(f1_act, 1)
            act.wait_ge(amid_done, 1)
            act.activation(a_mid[:], bank[0][0:1, :], ACT.Copy).then_inc(amid_set, 1)
            def y_square(c):
                act.wait_ge(f2_dve, c + 1)
                act.activation(y_sq[:, c, :], yT[:, c, :], ACT.Square).then_inc(y_squared, 1)

            for c in range(NC):
                act.wait_ge(f2_done, 2 * c + 1)
                if c >= 2:
                    act.wait_ge(f2_dve, c - 1)
                act.activation(y_tmp[:, c % 2, :], bank[2 * (c % 2)][:, :], ACT.Identity, bias=b_four[:, c:c + 1]).then_inc(f2_tmp, 1)
                if c == 0:
                    act.wait_ge(f_mid_set, 1)
                else:
                    y_square(c - 1)

            def o_square(q):
                act.wait_ge(o_normed, q + 1)
                if q:
                    act.wait_ge(o_scaled, q)
                act.activation(junk_o[:], o_sb[:, q % 2, :], ACT.Square, accum_out=ss_o[:, q:q + 1]).then_inc(o_sq, 1)

            def o_scale(q):
                act.wait_ge(o_rs, q + 1)
                act.wait_ge(o_sq, q + 1)
                act.activation(o_sb[:, q % 2, :], o_sb[:, q % 2, :], ACT.Copy, scale=ss_o[:, q:q + 1]).then_inc(o_scaled, 1)

            def o_place(q):
                a, b = QT[q]
                act.wait_ge(o_tr, q + 1)
                dst = oT[:].rearrange("p c (r w) -> p c r w", w=GRID_W)[:, :, QR * a:QR * a + QR, QC * b:QC * b + QC]
                act.activation(dst, bank[7][:, :].rearrange("p (c r w) -> p c r w", c=NC, w=QC)[:, :, :, ::-1], ACT.Copy).then_inc(oT_set, 1)

            def split_wo_hi(i):
                n, c = i // KD, i % KD
                act.wait_ge(wo_gained, i + 1)
                act.activation(wo_hi[n][:, c, :], wo_raw[:, i % 3, :], ACT.Copy).then_inc(wo_hi_set, 1)

            def pT_copy(m):
                act.wait_ge(p_tr, m + 1)
                if m >= 2:
                    act.wait_ge(pv_done, m - 1)
                act.activation(pT[:, m % 2, :], bank[3 + m % 2][:, 0:NK], ACT.Copy).then_inc(pT_act, 1)

            for m in range(M):
                q, hd = m // HEADS, m % HEADS
                act.wait_ge(s_shift, m + 1)
                if m >= 2:
                    act.wait_ge(p_tr, m - 1)
                if q >= 2 and hd == 0:
                    act.wait_ge(o_inv, q - 1)
                act.activation(p_sb[:, m % 2, :], s_sb[:, m % 2, :], ACT.Exp, bias=s_min[:, m % 4:m % 4 + 1], scale=-1.0,
                               accum_out=r_sum[:, q % 2, hd:hd + 1]).then_inc(p_set, 1)
                if m >= 1 and (m - 1) % 2 == 0:
                    pT_copy(m - 1)
                if m == 1:
                    y_square(NC - 1)
                if q:
                    if hd == 3:
                        o_square(q - 1)
                    if hd == 4:
                        o_scale(q - 1)
                    if hd == 7:
                        o_place(q - 1)
                if m >= 14 and m % 6 == 2 and (m - 14) // 6 < KD:
                    split_wo_hi((m - 14) // 6)
            o_square(7)
            o_scale(7)
            o_place(7)
            for t in range(NT):
                for j, src in ((0, oT), (1, yT)):
                    act.wait_ge(oT_set, 8)
                    act.activation(mT_hi[:, 4 * j:4 * j + 4, t * P:(t + 1) * P], src[:, :, t * P:(t + 1) * P], ACT.Copy).then_inc(m_hi_set, 1)
            for i in range(KD, 2 * KD):
                split_wo_hi(i)
            for t in range(NT + 1):
                if t < NT:
                    act.wait_ge(h_set, NT + t + 1)
                    act.activation(junk_h[:], h[:, t, :], ACT.Square, accum_out=ss_h[:, t:t + 1]).then_inc(h_sq, 1)
                if t >= 1:
                    u = t - 1
                    act.wait_ge(h_tr, 2 * u + 1)
                    if u >= 2:
                        act.wait_ge(r_done, u - 1)
                    act.activation(hT[:, u % 2, 0:4, :].rearrange("p k n -> p (k n)"), bank[4][:, :], ACT.Copy).then_inc(hT_set_act, 1)

            def gu_hi_half(n1, p1, k1, j):
                act.activation(gu_hi[:, 4 * j:4 * j + 4, :], gu_raw[:, p1, 4 * j:4 * j + 4, :, :].rearrange("p k a n -> p k (a n)"),
                               ACT.Copy).then_inc(gu_hi_set, 1)

            def dn_high(n1, p1, k1):
                act.wait_ge(dn_loaded[p1], 16 * (k1 + 1))
                ge(act, dn_done, n1 - 1)
                act.activation(dn_hi[:, p1, :, :], dn_raw[:, p1, :, :], ACT.Copy).then_inc(dn_hi_set, 1)

            def first_splits(n1, p1, k1):
                act.wait_ge(gu_loaded[p1], 32 * (k1 + 1))
                ge(act, gu_done, n1)
                gu_hi_half(n1, p1, k1, 0)
                gu_hi_half(n1, p1, k1, 1)
                dn_high(n1, p1, k1)

            def xgT_high(n1):
                act.wait_ge(xg_tr, n1 + 1)
                act.wait_ge(gu_done, n1) if not isinstance(n1, int) or n1 > 0 else None
                act.activation(xgT_hi[:, 0:4, :].rearrange("p k n -> p (k n)"), bank[2][:, :], ACT.Copy).then_inc(xgT_hi_set, 1)
                act.activation(xgT_hi[:, 4:8, :].rearrange("p k n -> p (k n)"), bank[3][:, :], ACT.Copy).then_inc(xgT_hi_set, 1)

            def step(l, e, n, k, p):
                if l == 0:
                    if not isinstance(n, int):
                        first_splits(n, p, k)
                    xgT_high(n)
                if l != 0:
                    pp, kp = slot(p, k, -1)
                    act.wait_ge(gu_done, n)
                    ge(act, hid_set, n - 1)
                    act.activation(act_g[:], bank[pp][:, 0:FE], ACT.Silu).then_inc(silu_set, 1)
                if l != 0 and (l is None or l < NF):
                    dn_high(n, p, k)
                if l != 0:
                    act.wait_ge(hid_tr, n)
                    act.activation(hidT_hi[:].rearrange("p k n -> p (k n)"), bank[4][:, 0:2 * P], ACT.Copy).then_inc(hidT_hi_set, 1)
                if l is None or l < NF - 1:
                    pn, kn = slot(p, k, 1)
                    act.wait_ge(gu_loaded[pn], 32 * (kn + 1))
                    act.wait_ge(gu_half, n + 1)
                    gu_hi_half(n + 1, pn, kn, 0)
                    xgT_high(n + 1)
                    gu_hi_half(n + 1, pn, kn, 1)

            act.wait_ge(wo_done, 4 * NT)
            first_splits(0, 0, 0)
            act.wait_ge(c_sub, 1)
            act.activation(c_e[:], c_d[:], ACT.Exp).then_inc(c_exp, 1)
            act.wait_ge(d_sub, 1)
            act.activation(r8[:, 6, :], r8[:, 5, :], ACT.Exp).then_inc(d_exp, 1)
            all_blocks(act, step)
            for t in range(NT):
                act.wait_ge(e_two, t + 1)
                if t:
                    act.wait_ge(e_sq, t)
                act.activation(junk_f[:], fin[:, t % 3, :], ACT.Square, accum_out=ss_e[:, t:t + 1]).then_inc(e_sq, 1)

        @block.vector
        def _(dve):
            def split_w_lo(w):
                dve.wait_ge(w_hi_set, w + 1)
                dve.tensor_tensor(w_lo[:, w % 2, :, :], w_raw[:, w % 2, :, :], w_hi[:, w % 2, :, :].bitcast(f32), ALU.subtract)\
                   .then_inc(w_lo_set, 1)

            dve.memset(half_neg[:], -0.5).then_inc(init_set, 1)
            dve.memset(ones_col[:], 1.0).then_inc(init_set, 1)
            dve.memset(w_bd[:], 0.0).then_inc(init_set, 1)
            dve.memset(zeros[:], 0).then_inc(init_set, 1)
            dve.memset(u_odd[:, :, 0:1], 0.0).then_inc(init_set, 1)
            dve.wait_ge(consts_in, 80)
            dve.tensor_copy(tri_ones[:, 0, :], small[:, C_TRI:C_TRI + P]).then_inc(init_set, 1)
            dve.memset(tri_ones[:, 1, :], 1.0).then_inc(init_set, 1)
            dve.wait_ge(cols_tr, 1)
            dve.tensor_copy(cols[:], bank[7][:, 0:20]).then_inc(cols_set, 1)
            for t in range(NT + 1):
                if t < NT:
                    dve.wait_ge(x_rs, t + 1)
                    dve.tensor_scalar(x_in[:, t, :], x_in[:, t, :], ss_x[:, t:t + 1], None, ALU.mult).then_inc(x_scaled, 1)
                if t == 5:
                    split_w_lo(0)
                if t:
                    u = t - 1
                    for j in range(2):
                        dve.wait_ge(x_hi, 2 * u + j + 1)
                        part = (slice(None), slice(4 * j, 4 * j + 4), slice(u * P, (u + 1) * P))
                        dve.tensor_tensor(xT_lo[part], x_bank(u, j)[:, :].rearrange("p (k n) -> p k n", n=P), xT_hi[part].bitcast(f32),
                                          ALU.subtract).then_inc(x_lo, 1)
            split_w_lo(1)
            for g, (w, kind, s, half) in enumerate(GROUPS):
                if g in BY_DVE:
                    dve.wait_ge(proj_done, g + 1)
                    src = bank[g % 4][:, :]
                    if kind == "u":
                        c = 2 * (w % 2) + s
                        wait_evacuated(dve, u_group(c, 1))
                        top = u_top[:, c % 2, :]
                        rev = u_top[:, c % 2, HALF - 1:0:-1]
                        dve.tensor_copy(u_even[:, c, 0:1], src[:, 0:1])
                        dve.tensor_copy(u_even[:, c, HALF:HALF + 1], top[:, 0:1])
                        dve.tensor_tensor(u_even[:, c, 1:HALF], src[:, 1:HALF], rev, ALU.add)
                        dve.tensor_tensor(u_odd[:, c, 1:HALF], src[:, 1:HALF], rev, ALU.subtract).then_inc(evac_dve, 1)
                    else:
                        i = g - 24
                        if i >= 4:
                            dve.wait_ge(v_stored[i % 4], 16 * (i // 4))
                        dve.tensor_copy(v_out[:, i % 4, :], src[:, 0:256]).then_inc(evac_dve, 1)
                last_of_chunk = g + 1 == len(GROUPS) or GROUPS[g + 1][0] != w
                if last_of_chunk and w + 2 < len(CHUNKS):
                    split_w_lo(w + 2)
            for i in range(4):
                dve.wait_ge(f1_done, 5 + i)
                dve.tensor_copy(b_odd[:, i, :], bank[4 + i][:, :]).then_inc(f1_dve, 1)
            dve.wait_ge(f_mid, 1)
            dve.tensor_tensor(yT[:, :, HALF:HALF + 1].rearrange("p c o -> p (c o)"), bank[4][:, 0:NC], b_four, ALU.add).then_inc(f_mid_set, 1)
            def sum_squares(c):
                dve.wait_ge(y_squared, c + 1)
                ge(dve, y_summed, c - 1)
                dve.tensor_tensor(y_sq[:, 0, :], y_sq[:, 0, :], y_sq[:, c, :], ALU.add).then_inc(y_summed, 1)

            for c in range(NC):
                if c >= 2:
                    sum_squares(c - 1)
                dve.wait_ge(f2_tmp, c + 1)
                dve.wait_ge(f2_done, 2 * c + 2)
                yo = bank[2 * (c % 2) + 1]
                dve.tensor_tensor(yT[:, c, 0:HALF], y_tmp[:, c % 2, :], yo[:, :], ALU.subtract)
                dve.tensor_tensor(yT[:, c, T - 1:HALF:-1], y_tmp[:, c % 2, 1:HALF], yo[:, 1:HALF], ALU.add).then_inc(f2_dve, 1)

            def score(m):
                dve.wait_ge(s_done, m + 1)
                dve.wait_ge(bm_set, m + 1)
                if m >= 2:
                    dve.wait_ge(p_set, m - 1)
                dve.tensor_tensor_reduce(out=s_sb[:, m % 2, :], in0=bank[m % 3][:, 0:NK], in1=bm[:, m % 3, :], scale=1.0, scalar=3e38,
                                         op0=ALU.add, op1=ALU.min, accum_out=s_min[:, m % 4:m % 4 + 1]).then_inc(s_shift, 1)

            def pT_copy(m):
                dve.wait_ge(p_tr, m + 1)
                if m >= 2:
                    dve.wait_ge(pv_done, m - 1)
                dve.tensor_copy(pT[:, m % 2, :], bank[3 + m % 2][:, 0:NK]).then_inc(pT_dve, 1)

            def o_norm(q):
                dve.wait_ge(p_set, 8 * (q + 1))
                dve.reciprocal(r_inv[:, q % 2, :], r_sum[:, q % 2, :]).then_inc(o_inv, 1)
                dve.wait_ge(o_inv, q + 1)
                dve.wait_ge(pv_done, 8 * (q + 1))
                if q >= 2:
                    dve.wait_ge(o_tr, q - 1)
                dve.tensor_tensor(o_sb[:, q % 2, :].rearrange("p (h d) -> p h d", d=DH), bank[5 + q % 2][:, :].rearrange("p (h d) -> p h d", d=DH),
                                  r_inv[:, q % 2, :].unsqueeze(2).broadcast_to([P, HEADS, DH]), ALU.mult).then_inc(o_normed, 1)

            def split_wo_lo(i):
                n, c = i // KD, i % KD
                dve.wait_ge(wo_hi_set, i + 1)
                dve.tensor_tensor(wo_lo[n][:, c, :], wo_raw[:, i % 3, :], wo_hi[n][:, c, :].bitcast(f32), ALU.subtract).then_inc(wo_lo_set, 1)

            for m in range(M + 2):
                if m < M:
                    score(m)
                if m >= 2 and m % 2 == 1:
                    pT_copy(m - 2)
                if m == 2:
                    sum_squares(NC - 1)
                if m == 4:
                    dve.wait_ge(f_ssum, 1)
                    dve.tensor_copy(ss_f[:], bank[7][:, 0:NT]).then_inc(f_moved, 1)
                if m >= 8 and m % 8 == 2 and m // 8 - 1 < 7:
                    o_norm(m // 8 - 1)
                if m >= 16 and m % 6 == 4 and (m - 16) // 6 < KD:
                    split_wo_lo((m - 16) // 6)
            o_norm(7)

            def m_low(t):
                for j, src in ((0, oT), (1, yT)):
                    dve.wait_ge(m_hi_set, 2 * t + j + 1)
                    part = (slice(None), slice(4 * j, 4 * j + 4), slice(t * P, (t + 1) * P))
                    last = dve.tensor_tensor(mT_lo[part], src[:, :, t * P:(t + 1) * P], mT_hi[part].bitcast(f32), ALU.subtract)
                last.then_inc(m_lo_set, 1)

            def h_rows(i):
                n, t = i // NT, i % NT
                part = h[:, t, 512 * n:512 * n + 512]
                dve.wait_ge(wo_done, 2 * i + 2)
                dve.wait_ge(xr_loaded[i % 4], 16 * (i // 4 + 1))
                dve.scalar_tensor_tensor(part, bank[2 * (i % 2) + 1][:, :], ss_f[:, t:t + 1], x_res[:, i % 4, :], ALU.mult, ALU.add).then_inc(h_part, 1)
                dve.wait_ge(h_part, i + 1)
                dve.tensor_tensor(part, bank[2 * (i % 2)][:, :], part, ALU.add).then_inc(h_set, 1)

            for t in range(4):
                m_low(t)
            dve.wait_ge(f_rs, 1)
            h_rows(0)
            m_low(4)
            m_low(5)
            h_rows(1)
            m_low(6)
            m_low(7)
            for i in range(2, NT):
                split_wo_lo(KD + i - 2)
                h_rows(i)
            split_wo_lo(2 * KD - 2)
            split_wo_lo(2 * KD - 1)
            dve.wait_ge(gmoe_in, 16)

            dve.memset(fill[:], SKIP).then_inc(fill_set, 1)
            for t in range(NT + 1):
                if t < NT:
                    h_rows(NT + t)
                    dve.wait_ge(h_rs, t + 1)
                    if t >= 2:
                        dve.wait_ge(hn_stored[t % 2], 16 * (t // 2))
                        dve.wait_ge(h_tr, 2 * (t - 1))
                    dve.scalar_tensor_tensor(hn[:, t % 2, :], h[:, t, :], ss_h[:, t:t + 1], g_moe[:], ALU.mult, ALU.mult).then_inc(hn_set, 1)
                if t:
                    u = t - 1
                    dve.wait_ge(h_tr, 2 * u + 2)
                    if u >= 2:
                        dve.wait_ge(r_done, u - 1)
                    dve.tensor_copy(hT[:, u % 2, 4:8, :].rearrange("p k n -> p (k n)"), bank[5][:, :]).then_inc(hT_set, 1)
            dve.memset(xg[:].rearrange("p a n -> p (a n)"), 0.0).then_inc(xg_zero, 1)

            links = [0]

            def link(instruction):
                links[0] += 1
                instruction.then_inc(rt, 1)
                dve.wait_ge(rt, links[0])

            def over_tiles(ap, n):
                return ap.unsqueeze(1).broadcast_to([P, NT, n])

            def over_last(ap, n):
                return ap.unsqueeze(2).broadcast_to([P, NT, n])

            iota, iotam, grp = (small[:, c:c + NF] for c in (C_IOTA, C_IOTAM, C_GRP))
            c_max, gi, m1, e1, m2, dm, ex, gsum, den, den_r, tmp, e2 = (r8[:, i, :] for i in range(12))
            dve.wait_ge(r_done, NT)
            dve.wait_ge(router_in, 64)
            link(dve.tensor_tensor(lg[:], bank[6][:, 0:NT * (NG + NF)].rearrange("p (t n) -> p t n", n=NG + NF),
                                   over_tiles(b_r[:], NG + NF), ALU.add))
            link(dve.tensor_reduce(c_max, lg[:, :, 0:NG], AX.X, ALU.max))
            dve.tensor_tensor(c_d[:], lg[:, :, 0:NG], over_last(c_max, NG), ALU.subtract).then_inc(c_sub, 1)
            dve.wait_ge(c_sub, 1)
            link(dve.tensor_scalar(c_eq[:], c_d[:], 0.0, None, ALU.is_equal))
            link(dve.scalar_tensor_tensor(c_cand[:], c_eq[:], -100.0, over_tiles(small[:, C_IOTA4:C_IOTA4 + NG], NG), ALU.mult, ALU.add))
            link(dve.tensor_reduce(gi, c_cand[:], AX.X, ALU.min))
            link(dve.tensor_tensor(f_eq[:], over_tiles(grp, NF), over_last(gi, NF), ALU.is_equal))
            link(dve.tensor_scalar(f_eq[:], f_eq[:], -1.0, BIG, ALU.add, ALU.mult))
            link(dve.tensor_tensor(f_m[:], lg[:, :, NG:], f_eq[:], ALU.add))

            def best(value, index, one_hot):
                link(dve.tensor_reduce(value, f_m[:], AX.X, ALU.max))
                link(dve.tensor_tensor(f_eq[:], f_m[:], over_last(value, NF), ALU.is_equal))
                link(dve.scalar_tensor_tensor(f_cand[:], f_eq[:], -100.0, over_tiles(iota, NF), ALU.mult, ALU.add))
                link(dve.tensor_reduce(index, f_cand[:], AX.X, ALU.min))
                link(dve.tensor_tensor(one_hot, over_tiles(iotam, NF), over_last(index, NF), ALU.is_equal))

            best(m1, e1, oh1[:])
            link(dve.scalar_tensor_tensor(f_m[:], oh1[:], -2 * BIG, f_m[:], ALU.mult, ALU.add))
            best(m2, e2, oh2[:])
            dve.tensor_tensor(oh[:], oh1[:], oh2[:], ALU.add).then_inc(oh_set, 1)
            dve.tensor_tensor(dm, m2, m1, ALU.subtract).then_inc(d_sub, 1)
            dve.wait_ge(rank_done, 1)
            ranks = bank[7][:, 0:NT * NF].rearrange("p (t n) -> p t n", n=NF)
            dve.tensor_tensor(pick[:, 0, :, :], ranks, oh1[:], ALU.mult)
            link(dve.tensor_tensor(pick[:, 1, :, :], ranks, oh2[:], ALU.mult))
            link(dve.tensor_reduce(r8[:, 10:12, :].rearrange("p c t -> p (c t)"), pick[:].rearrange("p c t n -> p (c t) n"), AX.X, ALU.add))
            dve.wait_ge(slotc_in, 16)
            for c in range(2):
                dve.tensor_tensor(in_slot[:, c, :, :], slot_c[:, S_SLOT:S_SLOT + P].unsqueeze(1).broadcast_to([P, NT, P]),
                                  over_last(r8[:, 10 + c, :], P), ALU.is_equal).then_inc(in_slot_set, 1)
            row, empty, y_row, wrap = (table[:, i, :] for i in range(4))
            dve.wait_ge(table_done, 1)
            link(dve.tensor_reduce(row, bank[6][:, 0:2 * NF].rearrange("p (a e) -> p e a", a=2), AX.X, ALU.add))
            dve.tensor_scalar(wrap, row, T + 0.5, float(-T), ALU.is_gt, ALU.mult)
            link(dve.tensor_scalar(empty, row, 0.0, float(SKIP + 1), ALU.is_equal, ALU.mult))
            link(dve.scalar_tensor_tensor(y_row, row, -1.0, empty, ALU.add, ALU.add))
            link(dve.tensor_tensor(wrap, y_row, wrap, ALU.add))
            dve.tensor_copy(slot_all[:, :, 0], wrap).then_inc(table_set, 1)
            dve.tensor_copy(slot_all[:, :, 1], y_row).then_inc(table_set, 1)
            link(dve.tensor_reduce(most[:, 0:1], bank[7][:, NT * NF:(NT + 1) * NF], AX.X, ALU.max))
            dve.tensor_copy(most_i[:, 0:1], most[:, 0:1]).then_inc(most_set, 1)
            dve.wait_ge(c_exp, 1)
            link(dve.tensor_reduce(gsum, c_e[:], AX.X, ALU.add))
            dve.wait_ge(d_exp, 1)
            link(dve.tensor_scalar(den, ex, 1.0, None, ALU.add))
            link(dve.tensor_tensor(den, den, gsum, ALU.mult))
            link(dve.reciprocal(mix_w[:, 0, :], den))
            link(dve.tensor_tensor(mix_w[:, 1, :], mix_w[:, 0, :], ex, ALU.mult))

            def place_all():
                link(dve.tensor_copy(rank_i[:], ranks))
                link(dve.tensor_single_scalar(rank_i[:], rank_i[:], 7, ALU.arith_shift_right))
                link(dve.tensor_copy(rank_b[:], rank_i[:]))
                link(dve.scalar_tensor_tensor(rank[:], rank_b[:], float(NF * CAP - CAP), ranks, ALU.mult, ALU.add))
                link(dve.tensor_tensor(rank[:], rank[:], over_tiles(small[:, C_SLOT:C_SLOT + NF], NF), ALU.add))
                dve.tensor_tensor(pick[:, 0, :, :], rank[:], oh1[:], ALU.mult)
                link(dve.tensor_tensor(pick[:, 1, :, :], rank[:], oh2[:], ALU.mult))
                link(dve.tensor_reduce(slot_f[:].rearrange("p c t -> p (c t)"), pick[:].rearrange("p c t n -> p (c t) n"), AX.X, ALU.add))
                dve.tensor_copy(slot_of[:], slot_f[:]).then_inc(slots_set, 1)

            def gu_lo_half(p1, j, n1):
                dve.wait_ge(gu_hi_set, 2 * n1 + j + 1)
                dve.tensor_tensor(gu_lo[:, 4 * j:4 * j + 4, :], gu_raw[:, p1, 4 * j:4 * j + 4, :, :].rearrange("p k a n -> p k (a n)"),
                                  gu_hi[:, 4 * j:4 * j + 4, :].bitcast(f32), ALU.subtract).then_inc(gu_lo_set, 1)

            def xgT_low(n1):
                for j in range(2):
                    dve.wait_ge(xgT_hi_set, 2 * n1 + j + 1)
                    dve.tensor_tensor(xgT_lo[:, 4 * j:4 * j + 4, :].rearrange("p k n -> p (k n)"), bank[2 + j][:, :],
                                      xgT_hi[:, 4 * j:4 * j + 4, :].rearrange("p k n -> p (k n)").bitcast(f32), ALU.subtract).then_inc(xgT_lo_set, 1)

            def y_rows_out(n2, p2, k2):
                dve.wait_ge(dn_done, n2 + 1)
                ge(dve, y_out[p2], 16 * k2)
                dve.tensor_copy(y_sb[:, p2, 0:512], bank[5][:, :])
                dve.tensor_copy(y_sb[:, p2, 512:], bank[6][:, :]).then_inc(y_set, 1)

            def step(l, e, n, k, p):
                if l == 0:
                    if not isinstance(n, int):
                        gu_lo_half(p, 0, n)
                        gu_lo_half(p, 1, n)
                    xgT_low(n)
                if l != 0:
                    pp, kp = slot(p, k, -1)
                    dve.wait_ge(silu_set, n)
                    ge(dve, hid_tr, n - 1)
                    dve.tensor_tensor(hid[:], act_g[:], bank[pp][:, FE:2 * FE], ALU.mult).then_inc(hid_set, 1)
                if l is None or l >= 2:
                    y_rows_out(n - 2, p, k - 1)
                if l != 0:
                    dve.wait_ge(hidT_hi_set, n)
                    dve.tensor_tensor(hidT_lo[:].rearrange("p k n -> p (k n)"), bank[4][:, 0:2 * P],
                                      hidT_hi[:].rearrange("p k n -> p (k n)").bitcast(f32), ALU.subtract).then_inc(hidT_lo_set, 1)
                if l is None or l < NF - 1:
                    gu_lo_half(slot(p, k, 1)[0], 0, n + 1)
                if l is None or l < NF - 1:
                    xgT_low(n + 1)
                    gu_lo_half(slot(p, k, 1)[0], 1, n + 1)
                if l == NF:
                    pp, kp = slot(p, k, -1)
                    y_rows_out(n - 1, pp, kp)

            all_blocks(dve, step, place_all)
            dve.wait_ge(gfin_in, 16)
            for t in range(NT + 2):
                if t < NT:
                    if t >= 3:
                        dve.wait_ge(e_set, t - 2)
                    dve.wait_ge(yp_loaded[t], 32)
                    dve.scalar_tensor_tensor(fin[:, t % 3, :], y_pair[:, t, 0, :], mix_w[:, 0, t:t + 1], h[:, t, :], ALU.mult, ALU.add).then_inc(e_one, 1)
                    dve.wait_ge(e_one, t + 1)
                    dve.scalar_tensor_tensor(fin[:, t % 3, :], y_pair[:, t, 1, :], mix_w[:, 1, t:t + 1], fin[:, t % 3, :], ALU.mult, ALU.add).then_inc(e_two, 1)
                if t >= 2:
                    u = t - 2
                    dve.wait_ge(e_rs, u + 1)
                    if u >= 4:
                        dve.wait_ge(out_stored[u % 4], 16 * (u // 4))
                    dve.scalar_tensor_tensor(o_fin[:, u % 4, :], fin[:, u % 3, :], ss_e[:, u:u + 1], g_fin[:], ALU.mult, ALU.mult).then_inc(e_set, 1)

        @block.gpsimd
        def _(pool):
            rms_count = [0]

            def rms(ss, ready, value, done, n):
                pool.wait_ge(ready, value)
                pool.tensor_scalar(ss, ss, 1.0 / n, EPS, ALU.mult, ALU.add).then_inc(rms_mid, 1)
                rms_count[0] += 1
                pool.wait_ge(rms_mid, rms_count[0])
                e = half_neg[:, 0:1] if ss.shape[1] == 1 else half_neg[:, 0:1].broadcast_to(list(ss.shape))
                pool.tensor_tensor(ss, ss, e, ALU.pow).then_inc(done, 1)

            def gain_w(w):
                pool.wait_ge(w_loaded[w % 2], 16 * (w // 2 + 1))
                pool.tensor_tensor(w_raw[:, w % 2, :, :], w_raw[:, w % 2, :, :], g_mix.unsqueeze(2).broadcast_to([P, KD, 256]), ALU.mult)\
                    .then_inc(w_gained, 1)

            def gain_first(j):
                pool.wait_ge(w_loaded[0], 16)
                rows = slice(4 * j, 4 * j + 4)
                last = pool.tensor_tensor(w_raw[:, 0, rows, :], w_raw[:, 0, rows, :], g_mix[:, rows].unsqueeze(2).broadcast_to([P, 4, 256]), ALU.mult)
                if j == 1:
                    last.then_inc(w_gained, 1)

            pool.wait_ge(init_set, HALVES)
            for t in range(NT):
                rms(ss_x[:, t:t + 1], x_sq, t + 1, x_rs, D)
                if t == 2:
                    pool.wait_ge(cols_set, 1)
                if t in (2, 3):
                    gain_first(t - 2)
            for w in range(1, len(CHUNKS)):
                gain_w(w)

            def gain_wo(i):
                n, c = i // KD, i % KD
                pool.wait_ge(wo_loaded[i % 3], 16 * (i // 3 + 1))
                pool.tensor_scalar(wo_raw[:, i % 3, :], wo_raw[:, i % 3, :], g_merged[:, c:c + 1], None, ALU.mult).then_inc(wo_gained, 1)

            pool.wait_ge(bias_in, 16 * (QR + 1))
            for m in range(M):
                q, hd = m // HEADS, m % HEADS
                a, b = QT[q]
                if m >= 3:
                    pool.wait_ge(s_shift, m - 2)
                z = hd * RPB_R * RPB_C + (RPB_R // 2 - 4 * a) * RPB_C + (COL_BASE[b] - QC * b) + RPB_C // 2 - Z0
                view = bass.AP(bias_g, z, [[G_LEN, P], [RPB_C, KR], [1, KC]])
                pool.tensor_tensor(bm[:, m % 3, :].rearrange("p (r w) -> p r w", w=KC), mask[:, q, :].rearrange("p (r w) -> p r w", w=KC),
                                   view, ALU.subtract).then_inc(bm_set, 1)
                if m == 6:
                    rms(ss_f[:], f_moved, 1, f_rs, DM)
                if q and hd == 6:
                    rms(ss_o[:, q - 1:q], o_sq, q, o_rs, DM)
                if m >= 12 and m % 6 == 0 and (m - 12) // 6 < KD:
                    gain_wo((m - 12) // 6)
            rms(ss_o[:, 7:8], o_sq, 8, o_rs, DM)
            for i in range(KD, 2 * KD):
                gain_wo(i)
            pool.wait_ge(wo_done, 2 * NT)
            pool.memset(zero_i[:], 0).then_inc(vals_set, 1)
            pool.iota(slot_val[:, :, :, 0], pattern=[[P, NT], [0, 2]], base=0, channel_multiplier=1).then_inc(vals_set, 1)
            pool.iota(slot_val[:, :, :, 1], pattern=[[P, NT], [T, 2]], base=0, channel_multiplier=1).then_inc(vals_set, 1)
            for t in range(NT):
                rms(ss_h[:, t:t + 1], h_sq, t + 1, h_rs, D)
            for j in range(2):
                pool.wait_ge(gu_hi_set, j + 1)
                pool.tensor_tensor(gu_lo[:, 4 * j:4 * j + 4, :], gu_raw[:, 0, 4 * j:4 * j + 4, :, :].rearrange("p k a n -> p k (a n)"),
                                   gu_hi[:, 4 * j:4 * j + 4, :].bitcast(f32), ALU.subtract).then_inc(gu_lo_set, 1)
            pool.wait_ge(slotc_in, 16)
            pool.wait_ge(oh_set, 1)
            for c, one_hot in enumerate((oh1, oh2)):
                pool.tensor_scalar(sel[:, c, :, 0, :], one_hot[:], slot_c[:, S_ROW:S_ROW + 1], None, ALU.mult).then_inc(sel_set, 1)
                tiles = slot_c[:, S_TILE + c * NT:S_TILE + (c + 1) * NT].unsqueeze(2).broadcast_to([P, NT, NF])
                pool.tensor_tensor(sel[:, c, :, 1, :], one_hot[:], tiles, ALU.mult).then_inc(sel_set, 1)

            def scatter_slots():
                pool.wait_ge(filled, 16)
                pool.wait_ge(slots_set, 1)
                pool.wait_ge(vals_set, 3)
                for t in range(NT):
                    for c in range(2):
                        pool.indirect_dma_start(slot_dram, bass.IndirectOffsetOnAxis(ap=slot_of[:, c, t:t + 1], axis=0), slot_val[:, t, c, :], None)\
                            .then_inc(slots_scattered, 16)

            def gather(e2, n2, p2, k2):
                pool.tensor_tensor(idx_x[:, p2, :], slot_all[:, e2, 0:1], zero_i[:], ALU.add).then_inc(idxx_set, 1)
                pool.wait_ge(idxx_set, n2 + 1)
                pool.sem_inc(idx_seen, 1)
                pool.indirect_dma_start(xg[:, p2, :], None, hn_dram, bass.IndirectOffsetOnAxis(ap=idx_x[:, p2, :], axis=0),
                                        bounds_check=T - 1, oob_is_err=False).then_inc(xg_in[p2], 16)

            def scatter(e2, n2, p2, k2):
                pool.wait_ge(y_set, n2 + 1)
                ge(pool, y_out[p2], 16 * k2)
                pool.tensor_tensor(idx_y[:, p2, :], slot_all[:, e2, 1:2], zero_i[:], ALU.add).then_inc(idxy_set, 1)
                pool.wait_ge(idxy_set, n2 + 1)
                pool.sem_inc(idx_seen, 1)
                pool.indirect_dma_start(y_dram, bass.IndirectOffsetOnAxis(ap=idx_y[:, p2, :], axis=0), y_sb[:, p2, :], None,
                                        bounds_check=2 * T - 1, oob_is_err=False).then_inc(y_out[p2], 16)

            def step(l, e, n, k, p):
                if l == 0:
                    if isinstance(n, int):
                        pool.wait_ge(table_set, 2)
                        pool.wait_ge(vals_set, 1)
                    else:
                        pool.wait_ge(slots_loaded, n // NF * 16)
                    gather(e, n, p, k)
                    pn, kn = slot(p, k, 1)
                    gather(e + 1, n + 1, pn, kn)
                if l is None or l + 2 < NF:
                    pool.wait_ge(xg_tr, n + 1)
                    gather(e + 2, n + 2, p, k + 1)
                if l is None or l >= 2:
                    scatter(e - 2, n - 2, p, k - 1)
                if l is None or l < NF:
                    pool.wait_ge(dn_hi_set, n + 1)
                    pool.tensor_tensor(dn_lo[:, p, :, :], dn_raw[:, p, :, :], dn_hi[:, p, :, :].bitcast(f32), ALU.subtract).then_inc(dn_lo_set, 1)
                if l == NF:
                    pp, kp = slot(p, k, -1)
                    scatter(e - 1, n - 1, pp, kp)

            pool.wait_ge(xg_zero, 1)
            for i in range(2):
                pool.wait_ge(hn_stored[i], 64)
            all_blocks(pool, step, scatter_slots)
            for t in range(NT):
                rms(ss_e[:, t:t + 1], e_sq, t + 1, e_rs, D)

        @block.tensor
        def _(pe):
            pe.wait_ge(consts_in, 80)
            pe.transpose(bank[7][:, 0:20], rows20[:], ident[0:20, 0:20]).then_inc(cols_tr, 1)
            def x_T(t):
                pe.wait_ge(x_scaled, t + 1)
                for j in range(2):
                    if t >= 2:
                        pe.wait_ge(x_lo, 2 * (t - 2) + j + 1)
                    for k in range(4):
                        d = 4 * j + k
                        last = pe.transpose(x_bank(t, j)[:, k * P:(k + 1) * P], x_in[:, t, d * P:(d + 1) * P], ident)
                    last.then_inc(x_tr, 1)

            for t in range(6):
                x_T(t)
            pe.wait_ge(x_lo, 8)
            seen = -1
            for g, (w, kind, s, half) in enumerate(GROUPS):
                if g == 1:
                    x_T(6)
                    x_T(7)
                if g == 2:
                    pe.wait_ge(x_lo, 2 * NT)
                if g == 8:
                    pe.wait_ge(wbd_in, 16 * FG)
                    for i, c in enumerate((C_CC, C_SC)):
                        pe.matmul(bank[6 + i][:, :], small[:, c:c + P], w_bd[:].rearrange("p c n -> p (c n)"), start=True, stop=True).then_inc(m_done, 1)
                if w != seen:
                    pe.wait_ge(w_lo_set, w + 1)
                    seen = w
                if g >= 4:
                    wait_evacuated(pe, g - 4)
                for k in range(KD):
                    first, last = k == 0, k == KD - 1
                    if kind == "v":
                        tok = slice(half * P, (half + 1) * P)
                        done = three(pe, bank[g % 4][:, 0:256], xT_hi[:, k, tok], xT_lo[:, k, tok],
                                     w_hi[:, w % 2, k, :], w_lo[:, w % 2, k, :], first, last)
                    else:
                        tok, col = slice(512 * half, 512 * half + 512), slice(P * s, P * s + P)
                        done = three(pe, bank[g % 4][:, :], w_hi[:, w % 2, k, col], w_lo[:, w % 2, k, col],
                                     xT_hi[:, k, tok], xT_lo[:, k, tok], first, last)
                done.then_inc(proj_done, 1)
            pe.wait_ge(m_set, 2)
            pe.wait_ge(init_set, ODD_ZERO)
            wait_evacuated(pe, 7)
            for i in range(8):
                odd, r = i // 4, i % 4
                if odd:
                    pe.wait_ge(f1_act, r + 1)
                src = u_odd if odd else u_even
                for c in range(NC):
                    last = pe.matmul(bank[4 + r][:, c * P:(c + 1) * P], src[:, c, r * P:(r + 1) * P], m_chan[:, odd, c, :], start=True, stop=True)
                last.then_inc(f1_done, 1)
            wait_evacuated(pe, 36)
            for c in range(NC):
                last = pe.matmul(bank[0][0:1, c * P:(c + 1) * P], u_even[:, c, HALF:HALF + 1], m_chan[:, 0, c, :], start=True, stop=True)
            last.then_inc(amid_done, 1)
            pe.wait_ge(dft_in, 32)
            pe.wait_ge(amid_set, 1)
            for g in (37, 38, 39):
                wait_evacuated(pe, g)
            pe.wait_ge(f1_act, 4)
            pe.wait_ge(f1_dve, 1)
            for c in range(NC):
                col = slice(c * P, (c + 1) * P)
                for i in range(4):
                    pe.matmul(bank[4][:, c:c + 1], a_even[:, i, col], small[:, C_ALT:C_ALT + 1], start=(i == 0), stop=False)
                last = pe.matmul(bank[4][:, c:c + 1], a_mid[0:1, col], altrow[0:1, 0:1], start=False, stop=True)
            last.then_inc(f_mid, 1)
            for c in range(NC):
                col = slice(c * P, (c + 1) * P)
                if c >= 2:
                    pe.wait_ge(f2_tmp, c - 1)
                for i in range(4):
                    pe.matmul(bank[2 * (c % 2)][:, :], a_even[:, i, col], dft[:, 0, i, :], start=(i == 0), stop=False)
                pe.matmul(bank[2 * (c % 2)][:, :], a_mid[0:1, col], altrow[:], start=False, stop=True).then_inc(f2_done, 1)
                pe.wait_ge(f1_dve, 4)
                if c >= 2:
                    pe.wait_ge(f2_dve, c - 1)
                for i in range(4):
                    last = pe.matmul(bank[2 * (c % 2) + 1][:, :], b_odd[:, i, col], dft[:, 1, i, :], start=(i == 0), stop=(i == 3))
                last.then_inc(f2_done, 1)
            def scores(m):
                q, hd = m // HEADS, m % HEADS
                a, b = QT[q]
                rows = slice(DH * (hd % 2), DH * (hd % 2) + DH)
                if m >= 3:
                    pe.wait_ge(s_shift, m - 2)
                grid_k = kT[rows, hd // 2, :].rearrange("p (r w) -> p r w", w=GRID_W)
                pe.matmul(bank[m % 3][:, 0:NK].rearrange("p (r w) -> p r w", w=KC), qT[rows, hd // 2, q * P:(q + 1) * P],
                          grid_k[:, 4 * a:4 * a + KR, COL_BASE[b]:COL_BASE[b] + KC], start=True, stop=True).then_inc(s_done, 1)

            def probs_T(m):
                pe.wait_ge(p_set, m + 1)
                if m >= 2:
                    wait_pT(pe, m - 2)
                for j in range(3):
                    last = pe.transpose(bank[3 + m % 2][:, j * P:(j + 1) * P], p_sb[:, m % 2, j * P:(j + 1) * P], ident)
                last.then_inc(p_tr, 1)

            def values(m):
                q, hd = m // HEADS, m % HEADS
                a, b = QT[q]
                if m == 0:
                    pe.wait_ge(vk_in, 16 * 32)
                if q >= 2 and hd == 0:
                    pe.wait_ge(o_normed, q - 1)
                wait_pT(pe, m)
                part = slice(hd * DH, min((hd + 2) * DH, DM))
                for j in range(3):
                    last = pe.matmul(bank[5 + q % 2][:, part], pT[:, m % 2, j * P:(j + 1) * P],
                                     vk[:, 4 * (a + j) + b, part], start=(j == 0), stop=(j == 2))
                last.then_inc(pv_done, 1)

            def o_T(q):
                pe.wait_ge(o_scaled, q + 1)
                if q:
                    pe.wait_ge(oT_set, q)
                for c in range(NC):
                    last = pe.transpose(bank[7][:, c * P:(c + 1) * P], o_sb[:, q % 2, c * P:(c + 1) * P], ident)
                last.then_inc(o_tr, 1)

            pe.wait_ge(f2_tmp, NC)
            pe.wait_ge(f2_dve, NC)
            for m in range(-2, M + 1):
                if m + 2 < M:
                    scores(m + 2)
                if 0 <= m < M:
                    probs_T(m)
                if m >= 1:
                    values(m - 1)
                if m == 3:
                    pe.wait_ge(y_summed, NC - 1)
                    pe.wait_ge(init_set, ONES)
                    for t in range(NT):
                        last = pe.matmul(bank[7][:, t:t + 1], y_sq[:, 0, t * P:(t + 1) * P], ones_col[:], start=True, stop=True)
                    last.then_inc(f_ssum, 1)
                if m >= 8 and m % 8 == 7 and m < M:
                    o_T(m // 8 - 1)
            o_T(7)
            for i in range(2 * NT):
                n, t = i // NT, i % NT
                tok = slice(t * P, (t + 1) * P)
                if n == 0:
                    pe.wait_ge(m_lo_set, t + 1)
                if i >= 2:
                    pe.wait_ge(h_set, i - 1)
                for part in range(2):
                    for k in range(4):
                        c = 4 * part + k
                        if t == 0:
                            pe.wait_ge(wo_lo_set, KD * n + c + 1)
                        last = three(pe, bank[2 * (i % 2) + part][:, :], mT_hi[:, c, tok], mT_lo[:, c, tok],
                                     wo_hi[n][:, c, :], wo_lo[n][:, c, :], k == 0, k == 3)
                    last.then_inc(wo_done, 1)

                def hn_T(u):
                    pe.wait_ge(hn_set, u + 1)
                    for j in range(2):
                        if u and j == 0:
                            pe.wait_ge(hT_set_act, u)
                        if u and j == 1:
                            pe.wait_ge(hT_set, u)
                        for k in range(4):
                            d = 4 * j + k
                            last = pe.transpose(bank[4 + j][:, k * P:(k + 1) * P], hn[:, u % 2, d * P:(d + 1) * P], ident)
                        last.then_inc(h_tr, 1)

                def route(u):
                    pe.wait_ge(hT_set_act, u + 1)
                    pe.wait_ge(hT_set, u + 1)
                    pe.wait_ge(router_in, 64)
                    for k in range(KD):
                        last = pe.matmul(bank[6][:, u * (NG + NF):(u + 1) * (NG + NF)], hT[:, u % 2, k, :], w_r[:, k, :],
                                         start=(k == 0), stop=(k == KD - 1))
                    last.then_inc(r_done, 1)

                if n == 1 and t >= 1:
                    hn_T(t - 1)
                if n == 1 and t >= 2:
                    route(t - 2)
            route(NT - 2)
            hn_T(NT - 1)
            route(NT - 1)
            pe.wait_ge(oh_set, 1)
            pe.wait_ge(init_set, TRI)
            for t in range(NT + 1):
                dst = bank[7][:, t * NF:(t + 1) * NF]
                for u in range(min(t + 1, NT)):
                    last = pe.matmul(dst, tri_ones[:, 0 if u == t else 1, :], oh[:, u, :], start=(u == 0), stop=(u == min(t, NT - 1)))
            last.then_inc(rank_done, 1)
            pe.wait_ge(sel_set, 4)
            for c in range(2):
                pe.wait_ge(in_slot_set, c + 1)
                for t in range(NT):
                    last = pe.matmul(bank[6][:, 0:2 * NF], in_slot[:, c, t, :], sel[:, c, t, :, :].rearrange("p a e -> p (a e)"),
                                     start=(c == 0 and t == 0), stop=(c == 1 and t == NT - 1))
            last.then_inc(table_done, 1)

            def x_T(n1, p1, k1):
                pe.wait_ge(xg_in[p1], 16 * (k1 + 1))
                ge(pe, xgT_lo_set, 2 * n1)
                for d in range(KD):
                    last = pe.transpose(bank[2 + d // 4][:, d % 4 * P:(d % 4 + 1) * P], xg[:, p1, d * P:(d + 1) * P], ident)
                last.then_inc(xg_tr, 1)

            def gate_up(n, p, j):
                pe.wait_ge(gu_lo_set, 2 * n + j + 1)
                for k in range(4):
                    d = 4 * j + k
                    last = three(pe, bank[p][:, :], xgT_hi[:, d, :], xgT_lo[:, d, :], gu_hi[:, d, :], gu_lo[:, d, :], d == 0, d == KD - 1)
                last.then_inc(gu_done if j else gu_half, 1)

            def step(l, e, n, k, p):
                if l == 0:
                    x_T(n, p, k)
                more = l is None or l < NF
                if more:
                    pe.wait_ge(xgT_lo_set, 2 * n + 2)
                    ge(pe, hid_set, n - 1)
                    gate_up(n, p, 0)
                if l != 0:
                    pe.wait_ge(hid_set, n)
                    ge(pe, hidT_lo_set, n - 1)
                    for c in range(2):
                        last = pe.transpose(bank[4][:, c * P:(c + 1) * P], hid[:, c * P:(c + 1) * P], ident)
                    last.then_inc(hid_tr, 1)
                if more:
                    gate_up(n, p, 1)
                if l is None or l < NF - 1:
                    pn, kn = slot(p, k, 1)
                    x_T(n + 1, pn, kn)
                if l != 0:
                    pe.wait_ge(hidT_lo_set, n)
                    pe.wait_ge(dn_lo_set, n)
                    ge(pe, y_set, n - 1)
                    pp = (p + 1) % 2
                    for c in range(2):
                        for half in range(2):
                            cols_ = slice(512 * half, 512 * half + 512)
                            last = three(pe, bank[5 + half][:, :], hidT_hi[:, c, :], hidT_lo[:, c, :],
                                         dn_hi[:, pp, c, cols_], dn_lo[:, pp, c, cols_], c == 0, c == 1)
                    last.then_inc(dn_done, 1)

            all_blocks(pe, step)


_INPUTS = ("x", "norm_mix", "w_in", "rpb", "w_four", "b_four", "g_attn_out", "g_four_out", "w_out", "norm_moe",
           "w_router_coarse", "b_router_coarse", "w_router_fine", "b_router_fine", "w_gate", "w_up", "w_down", "norm_final")


def kernel(**inputs):
    import concourse.bacc as bacc
    from concourse.bass_utils import run_bass_kernel_spmd

    nc = bacc.Bacc("TRN2", target_bir_lowering=False, num_devices=1)
    arrays = {name: np.ascontiguousarray(inputs[name]) for name in _INPUTS}
    arrays.update(constants())
    io = {name: nc.dram_tensor(name, a.shape, mybir.dt.float32, kind="ExternalInput").ap() for name, a in arrays.items()}
    out = nc.dram_tensor("out", (1, T, D), mybir.dt.float32, kind="ExternalOutput").ap()
    build(nc, io, out)
    result = run_bass_kernel_spmd(nc, [arrays], core_ids=[0])
    return result.results[0]["out"]
```

```python
import concourse.bass as bass
import concourse.mybir as mybir
import numpy as np
from contextlib import ExitStack

P = 128
T, D = 1024, 1024
NT, KD = T // P, D // P
GRID_W, ROWS = 64, 16
HEADS, DH = 8, 64
WIN_H, WIN_W = 8, 16
DM = 512
NC = DM // P
QR, QC = 8, 16
KR, KC = 12, 32
NK = KR * KC
COL_BASE = (0, 8, 24, 32)
RPB_R, RPB_C = 2 * WIN_H - 1, 2 * WIN_W - 1
FG = 8
HALF, QUARTER = T // 2, T // 4
NG, NF = 4, 32
EPG = NF // NG
FE = 256
CAP = P
BLOCKS = T // CAP
SLOTS = BLOCKS * NF * CAP
RING = 3
USES = [(NF - r + RING - 1) // RING for r in range(RING)]
SKIP = 1 << 20
EPS = 1e-6
BIG = 1e30

RPB_PAD = 160
RPB_N = HEADS * RPB_R * RPB_C
Z0 = (RPB_R // 2 - 4) * RPB_C - 1
G_LEN = (HEADS - 1) * RPB_R * RPB_C + (KR - 1 + RPB_R // 2) * RPB_C + (KC - 1) + RPB_C // 2 - Z0 + 1

C_ID, C_TRI, C_CC, C_SC = 0, 128, 256, 384
C_IOTA, C_IOTAM, C_GRP, C_SLOT, C_IOTA4, C_ALT = 512, 544, 576, 608, 640, 644
C_N = 648
S_SLOT, S_ROW, S_TILE = 0, P, P + 1
S_N = P + 1 + 2 * NT


def constants():
    ang = 2 * np.pi * ((np.arange(QUARTER)[:, None] * np.arange(HALF)[None, :]) % T) / T
    dft = np.stack([np.cos(ang), np.sin(ang)], 0).reshape(2, 2, P, QUARTER, 2).transpose(2, 0, 4, 1, 3)
    c = np.arange(FG * 8)
    small = np.zeros((P, C_N))
    small[:, C_ID:C_ID + P] = np.eye(P)
    small[:, C_TRI:C_TRI + P] = np.arange(P)[:, None] < np.arange(P)[None, :]
    a2 = 2 * np.pi * ((c[:, None] * c[None, :]) % 64) / 64
    for i in range(2):
        s = slice(64 * i, 64 * i + 64)
        small[s, C_CC + 64 * i:C_CC + 64 * i + 64] = np.cos(a2) / 256
        small[s, C_SC + 64 * i:C_SC + 64 * i + 64] = np.sin(a2) / 256
    e = np.arange(NF)
    small[:, C_IOTA:C_IOTA + NF] = e
    small[:, C_IOTAM:C_IOTAM + NF] = e - 100
    small[:, C_GRP:C_GRP + NF] = e // EPG - 100
    small[:, C_SLOT:C_SLOT + NF] = e * CAP
    small[:, C_IOTA4:C_IOTA4 + NG] = np.arange(NG)
    small[:, C_ALT] = 1 - 2 * (np.arange(P) % 2)
    slots = np.zeros((P, S_N))
    slots[:, S_SLOT:S_SLOT + P] = np.arange(P)
    slots[:, S_ROW] = np.arange(P) + 1
    slots[:, S_TILE:] = P * np.arange(2 * NT)
    altrow = (1 - 2 * (np.arange(HALF) % 2))[None]
    mask = np.full((P, 8, KR, KC), BIG)
    for a in range(2):
        for b in range(4):
            for i in range(QR):
                for cc in range(QC):
                    r, col = QR * a + i, QC * b + cc
                    rs = min(max(r - WIN_H // 2, 0), ROWS - WIN_H)
                    cs = min(max(col - WIN_W // 2, 0), GRID_W - WIN_W)
                    j0, k0 = rs - 4 * a, cs - COL_BASE[b]
                    mask[QC * i + QC - 1 - cc, 4 * a + b, j0:j0 + WIN_H, k0:k0 + WIN_W] = 0
    f = np.float32
    return {"c_dft": np.ascontiguousarray(dft.reshape(P, -1)).astype(f), "c_small": small.astype(f), "c_slots": slots.astype(f),
            "c_alt": altrow.astype(f), "c_mask": mask.reshape(P, -1).astype(f)}


def build(nc, io, out):
    f32, f32r, bf16 = mybir.dt.float32, mybir.dt.float32r, mybir.dt.bfloat16
    i32, u32 = mybir.dt.int32, mybir.dt.uint32
    ALU, ACT, AX = mybir.AluOpType, mybir.ActivationFunctionType, mybir.AxisListType

    v_dram = nc.dram_tensor("v_rows", (T, DM), f32).ap()
    rpb_dram = nc.dram_tensor("rpb_padded", (1, RPB_N + 2 * RPB_PAD), f32)
    hn_dram = nc.dram_tensor("hn_rows", (T, D), f32).ap()
    slot_dram = nc.dram_tensor("slot_table", (SLOTS, 2), u32).ap()
    y_dram = nc.dram_tensor("y_rows", (2 * T, D), f32).ap()

    w_in = io["w_in"].rearrange("o (k p) n -> p (o k) n", p=P)
    w_out = io["w_out"].rearrange("o (k p) n -> p (o k) n", p=P)
    w_gate = io["w_gate"].rearrange("o e (k p) n -> p (o e) k n", p=P)
    w_up = io["w_up"].rearrange("o e (k p) n -> p (o e) k n", p=P)
    w_down = io["w_down"].rearrange("o e (k p) n -> p (o e) k n", p=P)
    x_rows = io["x"].rearrange("o (t p) n -> p (o t) n", p=P)
    out_rows = out.rearrange("o (t p) n -> p (o t) n", p=P)
    hn_rows = hn_dram.rearrange("(t p) n -> p t n", p=P)
    y_rows = y_dram.rearrange("(k t p) n -> p t k n", p=P, k=2)

    ctx = ExitStack()
    BASE = 16512

    def at(name, kb, shape, dtype=f32):
        return nc.alloc_sbuf_tensor_at(name, shape, dtype, offset=BASE + int(kb * 32) * 32)

    def sem(name):
        return ctx.enter_context(nc.semaphore(name))

    with ctx:
        small = at("small", 0, [P, C_N])
        ident = small[:, C_ID:C_ID + P]
        tri_ones = at("tri_ones", 2.6, [P, 2, P], bf16)
        rows20 = at("rows20", 3.15, [20, P])
        cols = at("cols", 3.7, [P, 20])
        g_mix, g_merged, b_four = cols[:, 0:8], cols[:, 8:16], cols[:, 16:20]
        half_neg = at("half_neg", 3.8, [P, 1])
        ss_x = at("ss_x", 3.82, [P, 8])
        ss_h = at("ss_h", 3.86, [P, 8])
        ss_f = at("ss_f", 3.9, [P, 8])
        xT_hi = at("xT_hi", 4, [P, KD, T], f32r)
        xT_lo = at("xT_lo", 36, [P, KD, T], f32r)
        x_in = at("x_in", 68, [P, NT, D])
        qT = at("qT", 68, [P, NC, T])
        kT = at("kT", 84, [P, NC, T])
        w_raw = at("w_raw", 100, [P, 2, KD, 256])
        w_hi = at("w_hi", 116, [P, 2, KD, 256], f32r)
        w_lo = at("w_lo", 132, [P, 2, KD, 256], f32r)
        u_even = at("u_even", 148, [P, NC, HALF + 1])
        u_odd = at("u_odd", 156.5, [P, NC, HALF])
        u_ee = at("u_ee", 169, [P, NC, QUARTER])
        u_oe = at("u_oe", 173, [P, NC, QUARTER])
        u_top = at("u_top", 165, [P, 2, HALF])
        v_out = at("v_out", 177, [P, 4, 256])
        dft = at("dft", 181, [P, 2, 2, 2, QUARTER])
        m_chan = at("m_chan", 197, [P, 2, NC, P])
        w_bd = at("w_bd", 201, [P, NC, P])
        altrow = at("altrow", 203, [1, HALF])
        zeros = at("zeros", 205, [P, 512], u32)
        junk_x = at("junk_x", 165, [P, D])
        slot_c = at("slot_c", 207, [P, S_N])
        ones_col = at("ones_col", 3.98, [P, 1])
        a_even = at("a_even", 128, [P, 4, DM])
        b_odd = at("b_odd", 136, [P, 4, DM])
        a_mid = at("a_mid", 144, [1, 2, DM])
        y_tmp = at("y_tmp", 165, [P, 2, HALF])
        y_sq = at("y_sq", 148, [P, NC, T])
        yT = at("yT", 52, [P, NC, T])
        vk = at("vk", 4, [P, 16, DM])
        bias_g = at("bias_g", 100, [P, G_LEN])
        mask = at("mask", 116, [P, 8, NK])
        bm = at("bm", 36, [P, 3, NK])
        s_sb = at("s_sb", 40.5, [P, 2, NK])
        p_sb = at("p_sb", 43.5, [P, 2, NK])
        pT = at("pT", 46.5, [P, 2, NK])
        s_min = at("s_min", 49.5, [P, 4])
        r_sum = at("r_sum", 49.6, [P, 2, 8])
        r_inv = at("r_inv", 49.7, [P, 2, 8])
        ss_o = at("ss_o", 49.8, [P, 8])
        junk_o = at("junk_o", 50, [P, DM])
        oT = at("oT", 148, [P, NC, T])
        o_sb = at("o_sb", 197, [P, 2, DM])
        wo_raw = at("wo_raw", 201, [P, 3, 512])
        wo_hi = [at("wo_hi0", 181, [P, KD, 512], f32r), at("wo_hi1", 4, [P, KD, 512], f32r)]
        wo_lo = [at("wo_lo0", 165, [P, KD, 512], f32r), at("wo_lo1", 20, [P, KD, 512], f32r)]
        mT_hi = at("mT_hi", 68, [P, KD, T], f32r)
        mT_lo = at("mT_lo", 100, [P, KD, T], f32r)
        h = at("h", 36, [P, NT, D])
        x_res = at("x_res", 132, [P, 4, 512])
        hn = at("hn", 140, [P, 2, D])
        junk_h = at("junk_h", 148, [P, D])
        g_moe = at("g_moe", 152, [P, D])
        w_r = at("w_r", 156, [P, KD, NG + NF])
        b_r = at("b_r", 207.6, [P, NG + NF])
        fill = at("fill", 158, [P, 512], u32)
        hT = at("hT", 187, [P, 2, KD, P])
        lg = at("lg", 80, [P, NT, NG + NF])
        c_d = at("c_d", 81.2, [P, NT, NG])
        c_e = at("c_e", 81.4, [P, NT, NG])
        c_eq = at("c_eq", 81.6, [P, NT, NG])
        c_cand = at("c_cand", 81.8, [P, NT, NG])
        r8 = at("r8", 82, [P, 12, NT])
        f_m = at("f_m", 76, [P, NT, NF])
        f_eq = at("f_eq", 77, [P, NT, NF])
        f_cand = at("f_cand", 78, [P, NT, NF])
        oh1 = at("oh1", 197, [P, NT, NF])
        oh2 = at("oh2", 198, [P, NT, NF])
        oh = at("oh", 79, [P, NT, NF], bf16)
        rank = at("rank", 150, [P, NT, NF])
        rank_i = at("rank_i", 196, [P, NT, NF], i32)
        rank_b = at("rank_b", 151, [P, NT, NF])
        pick = at("pick", 148, [P, 2, NT, NF])
        sel = at("sel", 72, [P, 2, NT, 2, NF], bf16)
        in_slot = at("in_slot", 68, [P, 2, NT, P], bf16)
        table = at("table", 74, [P, 4, NF])
        gu_raw = [at(f"gu_raw{i}", kb, [P, KD, 2, FE]) for i, kb in enumerate((168, 84, 152))]
        dn_raw = [at(f"dn_raw{i}", kb, [P, 2, D]) for i, kb in enumerate((199, 100, 108))]
        gu_hi = at("gu_hi", 4, [P, KD, 2 * FE], f32r)
        gu_lo = at("gu_lo", 20, [P, KD, 2 * FE], f32r)
        dn_hi = at("dn_hi", 116, [P, 2, 2, D], f32r)
        dn_lo = at("dn_lo", 68, [P, 2, 2, D], f32r)
        xg = at("xg", 132, [P, 2, D])
        xgT_hi = at("xgT_hi", 140, [P, KD, P], f32r)
        xgT_lo = at("xgT_lo", 144, [P, KD, P], f32r)
        act_g = at("act_g", 148, [P, FE])
        hid = at("hid", 149, [P, FE])
        hidT_hi = at("hidT_hi", 150, [P, 2, P], f32r)
        hidT_lo = at("hidT_lo", 151, [P, 2, P], f32r)
        y_sb = at("y_sb", 187, [P, 2, D])
        slot_all = at("slot_all", 195, [P, NF, 2], u32)
        slot_val = at("slot_val", 195.3, [P, NT, 2, 2], u32)
        slot_f = at("slot_f", 186.75, [P, 2, NT])
        slot_of = at("slot_of", 195.5, [P, 2, NT], u32)
        mix_w = at("mix_w", 195.6, [P, 2, NT])
        idx_x = at("idx_x", 195.7, [P, 2, 1], u32)
        idx_y = at("idx_y", 195.72, [P, 2, 1], u32)
        zero_i = at("zero_i", 195.75, [P, 1], u32)
        most = at("most", 195.8, [P, 2], f32)
        most_i = at("most_i", 195.9, [P, 2], i32)
        y_pair = at("y_pair", 68, [P, NT, 2, D])
        g_fin = at("g_fin", 132, [P, D])
        fin = at("fin", 4, [P, 3, D])
        o_fin = at("o_fin", 148, [P, NT, D])
        junk_f = at("junk_f", 32, [P, D])
        ss_e = at("ss_e", 136, [P, 8])

        bank = [ctx.enter_context(nc.psum_tensor(f"bank{i}", [P, 512], f32)) for i in range(8)]

        consts_in, wbd_in, dft_in = (sem(n) for n in ("consts_in", "wbd_in", "dft_in"))
        x_loaded = [sem(f"x_loaded{t}") for t in range(NT)]
        w_loaded = [sem(f"w_loaded{i}") for i in range(2)]
        init_set, fill_set, rms_mid = (sem(n) for n in ("init_set", "fill_set", "rms_mid"))
        HALVES, ONES, WBD_ZERO, ZEROS, ODD_ZERO, TRI = 1, 2, 3, 4, 5, 7
        cols_tr, cols_set, m_done, m_set = (sem(n) for n in ("cols_tr", "cols_set", "m_done", "m_set"))
        x_sq, x_rs, x_scaled, x_tr, x_hi, x_lo = (sem(n) for n in ("x_sq", "x_rs", "x_scaled", "x_tr", "x_hi", "x_lo"))
        w_gained, w_hi_set, w_lo_set, proj_done, evac_act, evac_dve = (
            sem(n) for n in ("w_gained", "w_hi_set", "w_lo_set", "proj_done", "evac_act", "evac_dve"))
        v_stored = [sem(f"v_stored{i}") for i in range(4)]
        vk_in, rpb_mid, bias_in = (sem(n) for n in ("vk_in", "rpb_mid", "bias_in"))
        f1_done, f1_act, f1_dve, f2_done, f2_tmp, f2_dve, f_mid, f_mid_set, y_squared, y_summed, f_moved, f_rs = (
            sem(n) for n in ("f1_done", "f1_act", "f1_dve", "f2_done", "f2_tmp", "f2_dve", "f_mid", "f_mid_set", "y_squared", "y_summed", "f_moved", "f_rs"))
        bm_set, s_done, s_shift, p_set, p_tr, pT_act, pT_dve, pv_done = (
            sem(n) for n in ("bm_set", "s_done", "s_shift", "p_set", "p_tr", "pT_act", "pT_dve", "pv_done"))
        o_inv, o_normed, o_sq, o_rs, o_scaled, o_tr, oT_set = (
            sem(n) for n in ("o_inv", "o_normed", "o_sq", "o_rs", "o_scaled", "o_tr", "oT_set"))
        wo_loaded = [sem(f"wo_loaded{i}") for i in range(3)]
        wo_gained, wo_hi_set, wo_lo_set, m_hi_set, m_lo_set, wo_done, h_part, h_set = (
            sem(n) for n in ("wo_gained", "wo_hi_set", "wo_lo_set", "m_hi_set", "m_lo_set", "wo_done", "h_part", "h_set"))
        xr_loaded = [sem(f"xr_loaded{i}") for i in range(4)]
        gmoe_in, router_in, filled = (sem(n) for n in ("gmoe_in", "router_in", "filled"))
        h_sq, h_rs, hn_set, h_tr, hT_set, r_done = (sem(n) for n in ("h_sq", "h_rs", "hn_set", "h_tr", "hT_set", "r_done"))
        hn_stored = [sem(f"hn_stored{i}") for i in range(2)]
        rt, c_sub, c_exp, d_sub, d_exp, oh_set, rank_done, slots_set, vals_set, slots_scattered = (
            sem(n) for n in ("rt", "c_sub", "c_exp", "d_sub", "d_exp", "oh_set", "rank_done", "slots_set", "vals_set", "slots_scattered"))
        slots_loaded, xg_zero, most_set, gu_half, amid_done, amid_set = (
            sem(n) for n in ("slots_loaded", "xg_zero", "most_set", "gu_half", "amid_done", "amid_set"))
        folded = sem("folded")
        f_ssum, hT_set_act = (sem(n) for n in ("f_ssum", "hT_set_act"))
        slotc_in, sel_set, in_slot_set, table_done, table_set = (
            sem(n) for n in ("slotc_in", "sel_set", "in_slot_set", "table_done", "table_set"))
        gu_loaded = [sem(f"gu_loaded{i}") for i in range(RING)]
        dn_loaded = [sem(f"dn_loaded{i}") for i in range(RING)]
        gu_hi_set, gu_lo_set, dn_hi_set, dn_lo_set = (sem(n) for n in ("gu_hi_set", "gu_lo_set", "dn_hi_set", "dn_lo_set"))
        idxx_set, idxy_set, idx_seen = sem("idxx_set"), sem("idxy_set"), sem("idx_seen")
        xg_in = [sem(f"xg_in{i}") for i in range(2)]
        y_out = [sem(f"y_out{i}") for i in range(2)]
        xg_tr, xgT_hi_set, xgT_lo_set, gu_done, silu_set, hid_set, hid_tr, hidT_hi_set, hidT_lo_set, dn_done, y_set = (
            sem(n) for n in ("xg_tr", "xgT_hi_set", "xgT_lo_set", "gu_done", "silu_set", "hid_set", "hid_tr",
                             "hidT_hi_set", "hidT_lo_set", "dn_done", "y_set"))
        yp_loaded = x_loaded
        gfin_in, e_one, e_two, e_sq, e_rs, e_set = (sem(n) for n in ("gfin_in", "e_one", "e_two", "e_sq", "e_rs", "e_set"))
        e_scaled, e_pool = sem("e_scaled"), sem("e_pool")
        out_stored = sem("out_stored")

        block = ctx.enter_context(nc.Block())

        CHUNKS = [("u", 3 * DM), ("u", 3 * DM + 256), ("q", 0), ("q", 256), ("k", DM), ("k", DM + 256),
                  ("v", 2 * DM), ("v", 2 * DM + 256)]
        GROUPS = []
        for w, (kind, _) in enumerate(CHUNKS):
            if kind == "v":
                GROUPS += [(w, kind, None, t) for t in range(NT)]
            elif w == 0:
                GROUPS += [(w, kind, s, half) for half in (0, 1) for s in range(2)]
            else:
                GROUPS += [(w, kind, s, half) for s in range(2) for half in (1, 0)]
        CHUNK_END = [sum(x[0] <= w for x in GROUPS) for w in range(len(CHUNKS))]
        BY_ACT = [g for g, (_, kind, _, half) in enumerate(GROUPS) if kind in "qk" or (kind == "u" and half == 1)]
        BY_DVE = [g for g in range(len(GROUPS)) if g not in BY_ACT]

        def u_group(c, half):
            return GROUPS.index((c // 2, "u", c % 2, half))

        def x_bank(t, j):
            return bank[4 + 2 * (t % 2) + j]

        def wait_evacuated(eng, g):
            if g in BY_ACT:
                eng.wait_ge(evac_act, BY_ACT.index(g) + 1)
            else:
                eng.wait_ge(evac_dve, BY_DVE.index(g) + 1)

        QT = [(a, b) for a in range(2) for b in range(4)]
        M = len(QT) * HEADS

        BY_POOL = [0, 2, 4]

        def wait_finished(eng, t):
            if t in BY_POOL:
                eng.wait_ge(e_pool, BY_POOL.index(t) + 1)
            else:
                eng.wait_ge(e_set, t + 1 - sum(u < t for u in BY_POOL))

        def wait_pT(eng, m):
            eng.wait_ge(pT_dve if m % 2 else pT_act, m // 2 + 1)

        def three(pe, dst, hi, lo, rhi, rlo, first, last):
            pe.matmul(dst, hi, rhi, start=first, stop=False)
            pe.matmul(dst, hi, rlo, start=False, stop=False)
            return pe.matmul(dst, lo, rhi, start=False, stop=last)

        def chunk_c(w):
            return CHUNKS[w][1]

        def slot(p, k, d):
            return (p + d) % 2, k + (p + d) // 2

        def ge(eng, which, value):
            if not isinstance(value, int) or value > 0:
                eng.wait_ge(which, value)

        def ring_at(l, b):
            return l % RING, USES[l % RING] * b + l // RING

        def expert_pass(eng, step, b):
            def peeled(l):
                step(l, l, NF * b + l, NF // 2 * b + l // 2, l % 2, lambda d: ring_at(l + d, b))
            for l in range(4):
                peeled(l)
            with eng.Fori(0, 4) as i:
                for u in range(6):
                    def ring(d):
                        place, uses = ring_at(4 + u + d, b)
                        return place, uses + 2 * i
                    step(None, 6 * i + 4 + u, NF * b + 6 * i + 4 + u, NF // 2 * b + 3 * i + (4 + u) // 2, u % 2, ring)
            for l in range(28, NF + 1):
                peeled(l)

        def all_blocks(eng, step, before=None):
            expert_pass(eng, step, 0)
            eng.wait_ge(most_set, 1)
            over = eng.value_load(most_i[0:1, 0:1])
            with eng.If(over > CAP):
                if before:
                    before()
                with eng.Fori(1, BLOCKS) as b:
                    expert_pass(eng, step, b)
            with eng.Else():
                eng.nop()
            eng.nop()

        @block.sync
        def _(sp):
            sp.dma_start(small[:], io["c_small"]).then_inc(consts_in, 16)
            sp.dma_start(slot_c[:], io["c_slots"]).then_inc(slotc_in, 16)
            for t in range(NT):
                sp.dma_start(x_in[:, t, :], x_rows[:, t, :]).then_inc(x_loaded[t], 16)
                if t in (2, 5):
                    w = 0 if t == 2 else 1
                    sp.dma_start(w_raw[:, w, :, :], w_in[:, :, chunk_c(w):chunk_c(w) + 256]).then_inc(w_loaded[w], 16)
                if t == 0:
                    for k, name in ((0, "norm_mix"), (8, "g_attn_out"), (12, "g_four_out"), (16, "b_four")):
                        src = io[name].rearrange("o (k p) -> (o k) p", p=P)
                        sp.dma_start(rows20[k:k + src.shape[0], :], src).then_inc(consts_in, 16)
            sp.wait_ge(init_set, WBD_ZERO)
            for g in range(FG):
                o = 64 * (g % 2)
                sp.dma_start(w_bd[o:o + 64, g // 2, o:o + 64], io["w_four"][0, g]).then_inc(wbd_in, 16)
            sp.dma_start(dft[:].rearrange("p a b c d -> p (a b c d)"), io["c_dft"]).then_inc(dft_in, 16)
            sp.dma_start(altrow[:], io["c_alt"]).then_inc(dft_in, 16)
            sp.wait_ge(init_set, ZEROS)
            rp = rpb_dram.ap()
            sp.dma_start(rp[:, RPB_PAD:RPB_PAD + RPB_N], io["rpb"].rearrange("o h a b -> o (h a b)")).then_inc(rpb_mid, 16)
            for o in (0, RPB_PAD + RPB_N):
                sp.dma_start(rp[:, o:o + RPB_PAD], zeros[0:1, 0:RPB_PAD].bitcast(f32)).then_inc(rpb_mid, 16)
            for w in range(2, len(CHUNKS)):
                sp.wait_ge(w_lo_set, w - 1)
                sp.dma_start(w_raw[:, w % 2, :, :], w_in[:, :, chunk_c(w):chunk_c(w) + 256]).then_inc(w_loaded[w % 2], 16)
            v_at = 0
            for w in (6, 7):
                for t in range(NT):
                    g = 24 + v_at
                    wait_evacuated(sp, g)
                    sp.dma_start(v_dram[t * P:(t + 1) * P, 256 * (w - 6):256 * (w - 5)], v_out[:, v_at % 4, :])\
                      .then_inc(v_stored[v_at % 4], 16)
                    v_at += 1
            for i in range(4):
                sp.wait_ge(v_stored[i], 64)
            sp.wait_ge(proj_done, len(GROUPS))
            for g in range(4):
                for j in range(4):
                    for lo_b, hi_b in ((0, 3), (1, 2)):
                        row = (4 * g + j) * GRID_W + COL_BASE[lo_b]
                        gap = COL_BASE[hi_b] - COL_BASE[lo_b]
                        src = bass.AP(v_dram.tensor, row * DM, [[DM, KC], [gap * DM, 2], [1, DM]])
                        dst = vk[32 * j:32 * j + 32, 4 * g + lo_b:4 * g + hi_b + 1:hi_b - lo_b, :]
                        sp.dma_start(dst, src).then_inc(vk_in, 16)
            sp.wait_ge(rpb_mid, 48)
            for i in range(QR):
                src = bass.AP(rpb_dram, RPB_PAD + Z0 - RPB_C * i - (QC - 1), [[1, QC], [1, G_LEN]])
                sp.dma_start(bias_g[QC * i:QC * i + QC, :], src).then_inc(bias_in, 16)
            sp.dma_start(mask[:].rearrange("p a b -> p (a b)"), io["c_mask"]).then_inc(bias_in, 16)
            sp.wait_ge(f_rs, 1)
            def load_wo(i):
                n, c = i // KD, i % KD
                if i >= 3:
                    sp.wait_ge(wo_lo_set, i - 2)
                sp.dma_start(wo_raw[:, i % 3, :], w_out[:, c, 512 * n:512 * n + 512]).then_inc(wo_loaded[i % 3], 16)

            def load_xr(i):
                n, t = i // NT, i % NT
                if i >= 4:
                    sp.wait_ge(h_part, i - 3)
                sp.dma_start(x_res[:, i % 4, :], x_rows[:, t, 512 * n:512 * n + 512]).then_inc(xr_loaded[i % 4], 16)

            for i in range(KD + 3):
                load_wo(i)
            for i in range(4):
                load_xr(i)
            for i in range(KD + 3, 2 * KD):
                load_xr(i - KD + 1)
                load_wo(i)
            sp.wait_ge(m_lo_set, NT)
            sp.dma_start(g_moe[:], io["norm_moe"].partition_broadcast(P).rearrange("p o n -> p (o n)")).then_inc(gmoe_in, 16)
            sp.dma_start(w_r[:, :, 0:NG], io["w_router_coarse"].rearrange("o (k p) n -> p (o k) n", p=P)).then_inc(router_in, 16)
            sp.dma_start(w_r[:, :, NG:], io["w_router_fine"].rearrange("o (k p) n -> p (o k) n", p=P)).then_inc(router_in, 16)
            sp.dma_start(b_r[:, 0:NG], io["b_router_coarse"].partition_broadcast(P).rearrange("p o n -> p (o n)")).then_inc(router_in, 16)
            sp.dma_start(b_r[:, NG:], io["b_router_fine"].partition_broadcast(P).rearrange("p o n -> p (o n)")).then_inc(router_in, 16)
            def store_hn(t):
                sp.wait_ge(hn_set, t + 1)
                sp.dma_start(hn_rows[:, t, :], hn[:, t % 2, :]).then_inc(hn_stored[t % 2], 16)

            def one(ap, e):
                return ap[:, bass.ds(e, 1), :, :].rearrange("p o k n -> p (o k) n")

            def load_gate(e, r):
                sp.dma_start(gu_raw[r][:, :, 0, :], one(w_gate, e)).then_inc(gu_loaded[r], 16)

            def load_up(e, r):
                sp.dma_start(gu_raw[r][:, :, 1, :], one(w_up, e)).then_inc(gu_loaded[r], 16)

            def load_down(e, r):
                sp.dma_start(dn_raw[r][:], one(w_down, e)).then_inc(dn_loaded[r], 16)

            def load_expert(e, r, split):
                sp.wait_ge(gu_hi_set, 2 * split)
                sp.wait_ge(gu_lo_set, 2 * split)
                load_gate(e, r)
                load_up(e, r)
                sp.wait_ge(dn_hi_set, split)
                sp.wait_ge(dn_lo_set, split)
                load_down(e, r)

            for i in range(9, 2 * NT):
                load_xr(i)
                if i == 10:
                    sp.wait_ge(wo_done, 2 * NT)
                    sp.wait_ge(wo_lo_set, 2 * KD)
                    load_gate(0, 0)
                if i == 12:
                    load_up(0, 0)
                if i == 14:
                    load_down(0, 0)
                if i == 9:
                    sp.wait_ge(fill_set, 1)
                    sp.dma_start(slot_dram.rearrange("(p a) b -> p (a b)", p=P), fill[:]).then_inc(filled, 16)
                if i >= 12:
                    store_hn(i - 12)
            for t in range(4, NT):
                store_hn(t)
            sp.wait_ge(wo_done, 4 * NT)

            def load_rest(b):
                with sp.Fori(1, NF // RING) as i:
                    for r in range(RING):
                        load_expert(RING * i + r, r, NF * b + RING * i + r - RING + 1)
                for l in range(NF // RING * RING, NF):
                    load_expert(l, l % RING, NF * b + l - RING + 1)

            load_gate(1, 1)
            load_up(1, 1)
            load_down(1, 1)
            sp.wait_ge(r_done, NT)
            sp.wait_ge(filled, 16)
            load_gate(2, 2)
            load_up(2, 2)
            sp.wait_ge(idxx_set, 2)
            load_down(2, 2)
            load_rest(0)
            sp.wait_ge(most_set, 1)
            over = sp.value_load(most_i[0:1, 0:1])
            with sp.If(over > CAP):
                sp.wait_ge(slots_scattered, 16 * 2 * NT)
                with sp.Fori(1, BLOCKS) as b:
                    sp.wait_ge(idxx_set, NF * b)
                    sp.wait_ge(idxy_set, NF * b)
                    sp.dma_start(slot_all[:], slot_dram[bass.ds(b * NF * CAP, NF * CAP), :].rearrange("(e s) b -> s e b", s=CAP))\
                      .then_inc(slots_loaded, 16)
                    for r in range(RING):
                        load_expert(r, r, NF * b)
                    load_rest(b)
                sp.wait_ge(y_out[0], 16 * NF // 2 * BLOCKS)
                sp.wait_ge(y_out[1], 16 * NF // 2 * BLOCKS)
            with sp.Else():
                sp.wait_ge(y_out[0], 16 * NF // 2)
                sp.wait_ge(y_out[1], 16 * NF // 2)
            for t in range(NT):
                sp.dma_start(y_pair[:, t, :, :], y_rows[:, t, :, :]).then_inc(yp_loaded[t], 16)
                if t == 1:
                    sp.dma_start(g_fin[:], io["norm_final"].rearrange("(o n) -> o n", o=1).partition_broadcast(P).rearrange("p o n -> p (o n)")).then_inc(gfin_in, 16)
            for t in range(NT):
                wait_finished(sp, t)
                sp.dma_start(out_rows[:, t, :], o_fin[:, t, :]).then_inc(out_stored, 16)
            sp.wait_ge(out_stored, 16 * NT)
            for i in range(2):
                sp.wait_ge(hn_stored[i], 64)
            sp.wait_ge(filled, 16)

        @block.scalar
        def _(act):
            def split_w_hi(w):
                act.wait_ge(w_gained, w + 1)
                if w >= 2:
                    act.wait_ge(proj_done, CHUNK_END[w - 2])
                act.activation(w_hi[:, w % 2, :, :], w_raw[:, w % 2, :, :], ACT.Copy).then_inc(w_hi_set, 1)

            def x_square(t):
                act.wait_ge(x_loaded[t], 16)
                if t:
                    act.wait_ge(x_sq, t)
                act.activation(junk_x[:],
                               x_in[:, t, :], ACT.Square, accum_out=ss_x[:, t:t + 1]).then_inc(x_sq, 1)

            act.wait_ge(consts_in, 80)
            x_square(0)
            x_square(1)
            for t in range(NT):
                if t + 2 < NT:
                    x_square(t + 2)
                for j in range(2):
                    act.wait_ge(x_tr, 2 * t + j + 1)
                    act.activation(xT_hi[:, 4 * j:4 * j + 4, t * P:(t + 1) * P], x_bank(t, j)[:, :].rearrange("p (k n) -> p k n", n=P),
                                   ACT.Copy).then_inc(x_hi, 1)
                if t == 3:
                    split_w_hi(0)
            split_w_hi(1)
            for g, (w, kind, s, half) in enumerate(GROUPS):
                if g in BY_ACT:
                    act.wait_ge(proj_done, g + 1)
                    src = bank[g % 4][:, :]
                    c = 2 * (w % 2) + (s or 0)
                    if kind == "u":
                        if c >= 2:
                            wait_evacuated(act, u_group(c - 2, 0))
                        act.activation(u_top[:, c % 2, :], src, ACT.Copy).then_inc(evac_act, 1)
                    elif kind == "q":
                        dst = qT[:, c, 512 * half:512 * half + 512].rearrange("p (b i w) -> p i b w", b=4, i=QR)[:, :, :, ::-1]
                        act.activation(dst, src.rearrange("p (i b w) -> p i b w", i=QR, b=4), ACT.Copy, scale=-DH ** -0.5).then_inc(evac_act, 1)
                    else:
                        act.activation(kT[:, c, 512 * half:512 * half + 512], src, ACT.Copy).then_inc(evac_act, 1)
                last_of_chunk = g + 1 == len(GROUPS) or GROUPS[g + 1][0] != w
                if last_of_chunk and w + 2 < len(CHUNKS):
                    split_w_hi(w + 2)
                if g == 8:
                    act.wait_ge(m_done, 2)
                    for i in range(2):
                        act.activation(m_chan[:, i, :, :].rearrange("p c n -> p (c n)"), bank[6 + i][:, :], ACT.Copy).then_inc(m_set, 1)
            for i in range(4):
                act.wait_ge(f1_done, i + 1)
                act.activation(a_even[:, i, :], bank[4 + i][:, :], ACT.Copy).then_inc(f1_act, 1)
            for i in range(2):
                act.wait_ge(amid_done, i + 1)
                act.activation(a_mid[:, i, :], bank[i][0:1, :], ACT.Copy).then_inc(amid_set, 1)
            def y_square(c):
                act.wait_ge(f2_dve, c + 1)
                act.activation(y_sq[:, c, :], yT[:, c, :], ACT.Square).then_inc(y_squared, 1)

            for c in range(NC):
                act.wait_ge(f2_done, 2 * c + 1)
                if c >= 2:
                    act.wait_ge(f2_dve, c - 1)
                act.activation(y_tmp[:, c % 2, :], bank[2 * (c % 2)][:, :], ACT.Identity, bias=b_four[:, c:c + 1]).then_inc(f2_tmp, 1)
                if c == 0:
                    act.wait_ge(f_mid_set, 1)
                else:
                    y_square(c - 1)

            def o_square(q):
                act.wait_ge(o_normed, q + 1)
                if q:
                    act.wait_ge(o_scaled, q)
                act.activation(junk_o[:], o_sb[:, q % 2, :], ACT.Square, accum_out=ss_o[:, q:q + 1]).then_inc(o_sq, 1)

            def o_scale(q):
                act.wait_ge(o_rs, q + 1)
                act.wait_ge(o_sq, q + 1)
                act.activation(o_sb[:, q % 2, :], o_sb[:, q % 2, :], ACT.Copy, scale=ss_o[:, q:q + 1]).then_inc(o_scaled, 1)

            def o_place(q):
                a, b = QT[q]
                act.wait_ge(o_tr, q + 1)
                dst = oT[:].rearrange("p c (r w) -> p c r w", w=GRID_W)[:, :, QR * a:QR * a + QR, QC * b:QC * b + QC]
                act.activation(dst, bank[7][:, :].rearrange("p (c r w) -> p c r w", c=NC, w=QC)[:, :, :, ::-1], ACT.Copy).then_inc(oT_set, 1)

            def split_wo_hi(i):
                n, c = i // KD, i % KD
                act.wait_ge(wo_gained, i + 1)
                act.activation(wo_hi[n][:, c, :], wo_raw[:, i % 3, :], ACT.Copy).then_inc(wo_hi_set, 1)

            def pT_copy(m):
                act.wait_ge(p_tr, m + 1)
                if m >= 2:
                    act.wait_ge(pv_done, m - 1)
                act.activation(pT[:, m % 2, :], bank[3 + m % 2][:, 0:NK], ACT.Copy).then_inc(pT_act, 1)

            for m in range(M):
                q, hd = m // HEADS, m % HEADS
                act.wait_ge(s_shift, m + 1)
                if m >= 2:
                    act.wait_ge(p_tr, m - 1)
                if q >= 2 and hd == 0:
                    act.wait_ge(o_inv, q - 1)
                act.activation(p_sb[:, m % 2, :], s_sb[:, m % 2, :], ACT.Exp, bias=s_min[:, m % 4:m % 4 + 1], scale=-1.0,
                               accum_out=r_sum[:, q % 2, hd:hd + 1]).then_inc(p_set, 1)
                if m >= 1 and (m - 1) % 2 == 0:
                    pT_copy(m - 1)
                if m == 1:
                    y_square(NC - 1)
                if q:
                    if hd == 3:
                        o_square(q - 1)
                    if hd == 4:
                        o_scale(q - 1)
                    if hd == 7:
                        o_place(q - 1)
                if m >= 14 and m % 6 == 2 and (m - 14) // 6 < KD:
                    split_wo_hi((m - 14) // 6)
            def split_m_hi(t):
                act.wait_ge(s_done, M)
                for j, src in ((0, oT), (1, yT)):
                    act.wait_ge(oT_set, 4 if t < NT // 2 else 8)
                    act.activation(mT_hi[:, 4 * j:4 * j + 4, t * P:(t + 1) * P], src[:, :, t * P:(t + 1) * P], ACT.Copy).then_inc(m_hi_set, 1)

            split_m_hi(0)
            o_square(7)
            split_m_hi(1)
            o_scale(7)
            split_m_hi(2)
            o_place(7)
            for t in range(3, NT):
                split_m_hi(t)
            for i in range(KD, 2 * KD):
                split_wo_hi(i)
            for t in range(NT + 1):
                if t >= 1:
                    u = t - 1
                    act.wait_ge(h_tr, 2 * u + 1)
                    if u >= 2:
                        act.wait_ge(r_done, u - 1)
                    act.activation(hT[:, u % 2, 0:4, :].rearrange("p k n -> p (k n)"), bank[4][:, :], ACT.Copy).then_inc(hT_set_act, 1)
                if t < NT:
                    act.wait_ge(h_set, NT + t + 1)
                    act.activation(junk_h[:], h[:, t, :], ACT.Square, accum_out=ss_h[:, t:t + 1]).then_inc(h_sq, 1)

            def gu_hi_half(r, j):
                act.activation(gu_hi[:, 4 * j:4 * j + 4, :], gu_raw[r][:, 4 * j:4 * j + 4, :, :].rearrange("p k a n -> p k (a n)"),
                               ACT.Copy).then_inc(gu_hi_set, 1)

            def dn_high(n1, p1, r, uses):
                act.wait_ge(dn_loaded[r], 16 * (uses + 1))
                ge(act, dn_done, n1 - 1)
                act.activation(dn_hi[:, p1, :, :], dn_raw[r][:], ACT.Copy).then_inc(dn_hi_set, 1)

            def first_splits(n1, r, uses):
                act.wait_ge(gu_loaded[r], 32 * (uses + 1))
                ge(act, gu_done, n1)
                gu_hi_half(r, 0)
                gu_hi_half(r, 1)
                dn_high(n1, 0, r, uses)

            def xgT_high(n1):
                act.wait_ge(xg_tr, n1 + 1)
                act.wait_ge(gu_done, n1) if not isinstance(n1, int) or n1 > 0 else None
                act.activation(xgT_hi[:, 0:4, :].rearrange("p k n -> p (k n)"), bank[2][:, :], ACT.Copy).then_inc(xgT_hi_set, 1)
                act.activation(xgT_hi[:, 4:8, :].rearrange("p k n -> p (k n)"), bank[3][:, :], ACT.Copy).then_inc(xgT_hi_set, 1)

            def step(l, e, n, k, p, ring):
                if l == 0:
                    if not isinstance(n, int):
                        first_splits(n, *ring(0))
                    xgT_high(n)
                if l != 0:
                    pp, kp = slot(p, k, -1)
                    act.wait_ge(gu_done, n)
                    ge(act, hid_set, n - 1)
                    act.activation(act_g[:], bank[pp][:, 0:FE], ACT.Silu).then_inc(silu_set, 1)
                if l != 0 and (l is None or l < NF):
                    dn_high(n, p, *ring(0))
                if l != 0:
                    act.wait_ge(hid_tr, n)
                    act.activation(hidT_hi[:].rearrange("p k n -> p (k n)"), bank[4][:, 0:2 * P], ACT.Copy).then_inc(hidT_hi_set, 1)
                if l is None or l < NF - 1:
                    r, uses = ring(1)
                    act.wait_ge(gu_loaded[r], 32 * (uses + 1))
                    act.wait_ge(gu_half, n + 1)
                    gu_hi_half(r, 0)
                    xgT_high(n + 1)
                    gu_hi_half(r, 1)

            act.wait_ge(wo_done, 4 * NT)
            first_splits(0, *ring_at(0, 0))
            act.wait_ge(c_sub, 1)
            act.activation(c_e[:], c_d[:], ACT.Exp).then_inc(c_exp, 1)
            act.wait_ge(d_sub, 1)
            act.activation(r8[:, 6, :], r8[:, 5, :], ACT.Exp).then_inc(d_exp, 1)
            all_blocks(act, step)
            def e_scale(t):
                act.wait_ge(e_rs, t + 1)
                act.activation(o_fin[:, t, :], fin[:, t % 3, :], ACT.Copy, scale=ss_e[:, t:t + 1]).then_inc(e_scaled, 1)

            for t in range(NT):
                act.wait_ge(e_two, t + 1)
                if t:
                    act.wait_ge(e_sq, t)
                act.activation(junk_f[:], fin[:, t % 3, :], ACT.Square, accum_out=ss_e[:, t:t + 1]).then_inc(e_sq, 1)
                if t - 1 in BY_POOL:
                    e_scale(t - 1)

        @block.vector
        def _(dve):
            def split_w_lo(w):
                dve.wait_ge(w_hi_set, w + 1)
                dve.tensor_tensor(w_lo[:, w % 2, :, :], w_raw[:, w % 2, :, :], w_hi[:, w % 2, :, :].bitcast(f32), ALU.subtract)\
                   .then_inc(w_lo_set, 1)

            dve.memset(half_neg[:], -0.5).then_inc(init_set, 1)
            dve.memset(ones_col[:], 1.0).then_inc(init_set, 1)
            dve.memset(w_bd[:], 0.0).then_inc(init_set, 1)
            dve.memset(zeros[:], 0).then_inc(init_set, 1)
            dve.memset(u_odd[:, :, 0:1], 0.0)
            dve.memset(u_oe[:, :, 0:1], 0.0).then_inc(init_set, 1)
            dve.wait_ge(consts_in, 80)
            dve.tensor_copy(tri_ones[:, 0, :], small[:, C_TRI:C_TRI + P]).then_inc(init_set, 1)
            dve.memset(tri_ones[:, 1, :], 1.0).then_inc(init_set, 1)
            dve.wait_ge(cols_tr, 1)
            dve.tensor_copy(cols[:], bank[7][:, 0:20]).then_inc(cols_set, 1)
            for t in range(NT + 1):
                if t < NT:
                    dve.wait_ge(x_rs, t + 1)
                    dve.tensor_scalar(x_in[:, t, :], x_in[:, t, :], ss_x[:, t:t + 1], None, ALU.mult).then_inc(x_scaled, 1)
                if t == 5:
                    split_w_lo(0)
                if t:
                    u = t - 1
                    for j in range(2):
                        dve.wait_ge(x_hi, 2 * u + j + 1)
                        part = (slice(None), slice(4 * j, 4 * j + 4), slice(u * P, (u + 1) * P))
                        dve.tensor_tensor(xT_lo[part], x_bank(u, j)[:, :].rearrange("p (k n) -> p k n", n=P), xT_hi[part].bitcast(f32),
                                          ALU.subtract).then_inc(x_lo, 1)
            split_w_lo(1)
            for g, (w, kind, s, half) in enumerate(GROUPS):
                if g in BY_DVE:
                    dve.wait_ge(proj_done, g + 1)
                    src = bank[g % 4][:, :]
                    if kind == "u":
                        c = 2 * (w % 2) + s
                        wait_evacuated(dve, u_group(c, 1))
                        top = u_top[:, c % 2, :]
                        rev = u_top[:, c % 2, HALF - 1:0:-1]
                        dve.tensor_copy(u_even[:, c, 0:1], src[:, 0:1])
                        dve.tensor_copy(u_even[:, c, HALF:HALF + 1], top[:, 0:1])
                        dve.tensor_tensor(u_even[:, c, 1:HALF], src[:, 1:HALF], rev, ALU.add)
                        dve.tensor_tensor(u_odd[:, c, 1:HALF], src[:, 1:HALF], rev, ALU.subtract).then_inc(evac_dve, 1)
                        wait_evacuated(dve, g)
                        e_low, e_rev = u_even[:, c, 0:QUARTER], u_even[:, c, HALF:QUARTER:-1]
                        o_low, o_rev = u_odd[:, c, 1:QUARTER], u_odd[:, c, HALF - 1:QUARTER:-1]
                        dve.tensor_tensor(u_ee[:, c, :], e_low, e_rev, ALU.add)
                        dve.tensor_tensor(u_oe[:, c, 1:QUARTER], o_low, o_rev, ALU.subtract).then_inc(folded, 1)
                        dve.wait_ge(folded, 2 * c + 1)
                        dve.tensor_tensor(e_low, e_low, e_rev, ALU.subtract)
                        dve.tensor_tensor(o_low, o_low, o_rev, ALU.add).then_inc(folded, 1)
                    else:
                        i = g - 24
                        if i >= 4:
                            dve.wait_ge(v_stored[i % 4], 16 * (i // 4))
                        dve.tensor_copy(v_out[:, i % 4, :], src[:, 0:256]).then_inc(evac_dve, 1)
                last_of_chunk = g + 1 == len(GROUPS) or GROUPS[g + 1][0] != w
                if last_of_chunk and w + 2 < len(CHUNKS):
                    split_w_lo(w + 2)
            for i in range(4):
                dve.wait_ge(f1_done, 5 + i)
                dve.tensor_copy(b_odd[:, i, :], bank[4 + i][:, :]).then_inc(f1_dve, 1)
            dve.wait_ge(f_mid, 1)
            dve.tensor_tensor(yT[:, :, HALF:HALF + 1].rearrange("p c o -> p (c o)"), bank[4][:, 0:NC], b_four, ALU.add).then_inc(f_mid_set, 1)
            def sum_squares(c):
                dve.wait_ge(y_squared, c + 1)
                ge(dve, y_summed, c - 1)
                dve.tensor_tensor(y_sq[:, 0, :], y_sq[:, 0, :], y_sq[:, c, :], ALU.add).then_inc(y_summed, 1)

            for c in range(NC):
                if c >= 2:
                    sum_squares(c - 1)
                dve.wait_ge(f2_tmp, c + 1)
                dve.wait_ge(f2_done, 2 * c + 2)
                yo = bank[2 * (c % 2) + 1]
                dve.tensor_tensor(yT[:, c, 0:HALF].rearrange("p (m q) -> p q m", q=2), y_tmp[:, c % 2, :].rearrange("p (q m) -> p q m", q=2),
                                  yo[:, :].rearrange("p (q m) -> p q m", q=2), ALU.subtract)
                dve.tensor_tensor(yT[:, c, T - 2:HALF:-2], y_tmp[:, c % 2, 1:QUARTER], yo[:, 1:QUARTER], ALU.add)
                dve.tensor_tensor(yT[:, c, T - 1:HALF:-2], y_tmp[:, c % 2, QUARTER:], yo[:, QUARTER:], ALU.add).then_inc(f2_dve, 1)

            def score(m):
                dve.wait_ge(s_done, m + 1)
                dve.wait_ge(bm_set, m + 1)
                if m >= 2:
                    dve.wait_ge(p_set, m - 1)
                dve.tensor_tensor_reduce(out=s_sb[:, m % 2, :], in0=bank[m % 3][:, 0:NK], in1=bm[:, m % 3, :], scale=1.0, scalar=3e38,
                                         op0=ALU.add, op1=ALU.min, accum_out=s_min[:, m % 4:m % 4 + 1]).then_inc(s_shift, 1)

            def pT_copy(m):
                dve.wait_ge(p_tr, m + 1)
                if m >= 2:
                    dve.wait_ge(pv_done, m - 1)
                dve.tensor_copy(pT[:, m % 2, :], bank[3 + m % 2][:, 0:NK]).then_inc(pT_dve, 1)

            def o_norm(q):
                dve.wait_ge(p_set, 8 * (q + 1))
                dve.reciprocal(r_inv[:, q % 2, :], r_sum[:, q % 2, :]).then_inc(o_inv, 1)
                dve.wait_ge(o_inv, q + 1)
                dve.wait_ge(pv_done, 8 * (q + 1))
                if q >= 2:
                    dve.wait_ge(o_tr, q - 1)
                dve.tensor_tensor(o_sb[:, q % 2, :].rearrange("p (h d) -> p h d", d=DH), bank[5 + q % 2][:, :].rearrange("p (h d) -> p h d", d=DH),
                                  r_inv[:, q % 2, :].unsqueeze(2).broadcast_to([P, HEADS, DH]), ALU.mult).then_inc(o_normed, 1)

            def split_wo_lo(i):
                n, c = i // KD, i % KD
                dve.wait_ge(wo_hi_set, i + 1)
                dve.tensor_tensor(wo_lo[n][:, c, :], wo_raw[:, i % 3, :], wo_hi[n][:, c, :].bitcast(f32), ALU.subtract).then_inc(wo_lo_set, 1)

            for m in range(M + 2):
                if m < M:
                    score(m)
                if m >= 2 and m % 2 == 1:
                    pT_copy(m - 2)
                if m == 2:
                    sum_squares(NC - 1)
                if m == 4:
                    dve.wait_ge(f_ssum, 1)
                    dve.tensor_copy(ss_f[:], bank[7][:, 0:NT]).then_inc(f_moved, 1)
                if m >= 8 and m % 8 == 2 and m // 8 - 1 < 7:
                    o_norm(m // 8 - 1)
                if m >= 16 and m % 6 == 4 and (m - 16) // 6 < KD:
                    split_wo_lo((m - 16) // 6)

            def m_low(t):
                for j, src in ((0, oT), (1, yT)):
                    dve.wait_ge(m_hi_set, 2 * t + j + 1)
                    part = (slice(None), slice(4 * j, 4 * j + 4), slice(t * P, (t + 1) * P))
                    last = dve.tensor_tensor(mT_lo[part], src[:, :, t * P:(t + 1) * P], mT_hi[part].bitcast(f32), ALU.subtract)
                last.then_inc(m_lo_set, 1)

            def h_rows(i):
                n, t = i // NT, i % NT
                part = h[:, t, 512 * n:512 * n + 512]
                dve.wait_ge(wo_done, 2 * i + 2)
                dve.wait_ge(xr_loaded[i % 4], 16 * (i // 4 + 1))
                dve.scalar_tensor_tensor(part, bank[2 * (i % 2) + 1][:, :], ss_f[:, t:t + 1], x_res[:, i % 4, :], ALU.mult, ALU.add).then_inc(h_part, 1)
                dve.wait_ge(h_part, i + 1)
                dve.tensor_tensor(part, bank[2 * (i % 2)][:, :], part, ALU.add).then_inc(h_set, 1)

            m_low(0)
            o_norm(7)
            for t in range(1, 4):
                m_low(t)
            dve.wait_ge(f_rs, 1)
            h_rows(0)
            m_low(4)
            m_low(5)
            h_rows(1)
            m_low(6)
            m_low(7)
            for i in range(2, NT):
                split_wo_lo(KD + i - 2)
                h_rows(i)
            split_wo_lo(2 * KD - 2)
            split_wo_lo(2 * KD - 1)
            dve.wait_ge(gmoe_in, 16)

            dve.memset(fill[:], SKIP).then_inc(fill_set, 1)
            for t in range(NT + 1):
                if t < NT:
                    h_rows(NT + t)
                if t:
                    u = t - 1
                    dve.wait_ge(h_tr, 2 * u + 2)
                    if u >= 2:
                        dve.wait_ge(r_done, u - 1)
                    dve.tensor_copy(hT[:, u % 2, 4:8, :].rearrange("p k n -> p (k n)"), bank[5][:, :]).then_inc(hT_set, 1)
                if t < NT:
                    dve.wait_ge(h_rs, t + 1)
                    if t >= 2:
                        dve.wait_ge(hn_stored[t % 2], 16 * (t // 2))
                        dve.wait_ge(h_tr, 2 * (t - 1))
                    dve.scalar_tensor_tensor(hn[:, t % 2, :], h[:, t, :], ss_h[:, t:t + 1], g_moe[:], ALU.mult, ALU.mult).then_inc(hn_set, 1)
            dve.memset(xg[:].rearrange("p a n -> p (a n)"), 0.0).then_inc(xg_zero, 1)

            links = [0]

            def link(instruction):
                links[0] += 1
                instruction.then_inc(rt, 1)
                dve.wait_ge(rt, links[0])

            def over_tiles(ap, n):
                return ap.unsqueeze(1).broadcast_to([P, NT, n])

            def over_last(ap, n):
                return ap.unsqueeze(2).broadcast_to([P, NT, n])

            iota, iotam, grp = (small[:, c:c + NF] for c in (C_IOTA, C_IOTAM, C_GRP))
            c_max, gi, m1, e1, m2, dm, ex, gsum, den, den_r, tmp, e2 = (r8[:, i, :] for i in range(12))
            dve.wait_ge(r_done, NT)
            dve.wait_ge(router_in, 64)
            link(dve.tensor_tensor(lg[:], bank[6][:, 0:NT * (NG + NF)].rearrange("p (t n) -> p t n", n=NG + NF),
                                   over_tiles(b_r[:], NG + NF), ALU.add))
            link(dve.tensor_reduce(c_max, lg[:, :, 0:NG], AX.X, ALU.max))
            dve.tensor_tensor(c_d[:], lg[:, :, 0:NG], over_last(c_max, NG), ALU.subtract).then_inc(c_sub, 1)
            dve.wait_ge(c_sub, 1)
            link(dve.tensor_scalar(c_eq[:], c_d[:], 0.0, None, ALU.is_equal))
            link(dve.scalar_tensor_tensor(c_cand[:], c_eq[:], -100.0, over_tiles(small[:, C_IOTA4:C_IOTA4 + NG], NG), ALU.mult, ALU.add))
            link(dve.tensor_reduce(gi, c_cand[:], AX.X, ALU.min))
            link(dve.tensor_tensor(f_eq[:], over_tiles(grp, NF), over_last(gi, NF), ALU.not_equal))
            link(dve.scalar_tensor_tensor(f_m[:], f_eq[:], -BIG, lg[:, :, NG:], ALU.mult, ALU.add))

            def best(value, index, one_hot):
                link(dve.tensor_reduce(value, f_m[:], AX.X, ALU.max))
                link(dve.tensor_tensor(f_eq[:], f_m[:], over_last(value, NF), ALU.is_equal))
                link(dve.scalar_tensor_tensor(f_cand[:], f_eq[:], -100.0, over_tiles(iota, NF), ALU.mult, ALU.add))
                link(dve.tensor_reduce(index, f_cand[:], AX.X, ALU.min))
                link(dve.tensor_tensor(one_hot, over_tiles(iotam, NF), over_last(index, NF), ALU.is_equal))

            best(m1, e1, oh1[:])
            link(dve.scalar_tensor_tensor(f_m[:], oh1[:], -2 * BIG, f_m[:], ALU.mult, ALU.add))
            best(m2, e2, oh2[:])
            dve.tensor_tensor(oh[:], oh1[:], oh2[:], ALU.add).then_inc(oh_set, 1)
            dve.tensor_tensor(dm, m2, m1, ALU.subtract).then_inc(d_sub, 1)
            dve.wait_ge(rank_done, 1)
            ranks = bank[7][:, 0:NT * NF].rearrange("p (t n) -> p t n", n=NF)
            dve.tensor_tensor(pick[:, 0, :, :], ranks, oh1[:], ALU.mult)
            link(dve.tensor_tensor(pick[:, 1, :, :], ranks, oh2[:], ALU.mult))
            link(dve.tensor_reduce(r8[:, 10:12, :].rearrange("p c t -> p (c t)"), pick[:].rearrange("p c t n -> p (c t) n"), AX.X, ALU.add))
            dve.wait_ge(slotc_in, 16)
            for c in range(2):
                dve.tensor_tensor(in_slot[:, c, :, :], slot_c[:, S_SLOT:S_SLOT + P].unsqueeze(1).broadcast_to([P, NT, P]),
                                  over_last(r8[:, 10 + c, :], P), ALU.is_equal).then_inc(in_slot_set, 1)
            row, empty, y_row, wrap = (table[:, i, :] for i in range(4))
            dve.wait_ge(table_done, 1)
            link(dve.tensor_reduce(row, bank[6][:, 0:2 * NF].rearrange("p (a e) -> p e a", a=2), AX.X, ALU.add))
            dve.tensor_scalar(wrap, row, T + 0.5, float(-T), ALU.is_gt, ALU.mult)
            link(dve.tensor_scalar(empty, row, 0.0, float(SKIP + 1), ALU.is_equal, ALU.mult))
            link(dve.scalar_tensor_tensor(y_row, row, -1.0, empty, ALU.add, ALU.add))
            link(dve.tensor_tensor(wrap, y_row, wrap, ALU.add))
            dve.tensor_copy(slot_all[:, :, 0], wrap).then_inc(table_set, 1)
            dve.tensor_copy(slot_all[:, :, 1], y_row).then_inc(table_set, 1)
            link(dve.tensor_reduce(most[:, 0:1], bank[7][:, NT * NF:(NT + 1) * NF], AX.X, ALU.max))
            dve.tensor_copy(most_i[:, 0:1], most[:, 0:1]).then_inc(most_set, 1)
            dve.wait_ge(c_exp, 1)
            link(dve.tensor_reduce(gsum, c_e[:], AX.X, ALU.add))
            dve.wait_ge(d_exp, 1)
            link(dve.tensor_scalar(den, ex, 1.0, None, ALU.add))
            link(dve.tensor_tensor(den, den, gsum, ALU.mult))
            link(dve.reciprocal(mix_w[:, 0, :], den))
            link(dve.tensor_tensor(mix_w[:, 1, :], mix_w[:, 0, :], ex, ALU.mult))

            def place_all():
                link(dve.tensor_copy(rank_i[:], ranks))
                link(dve.tensor_single_scalar(rank_i[:], rank_i[:], 7, ALU.arith_shift_right))
                link(dve.tensor_copy(rank_b[:], rank_i[:]))
                link(dve.scalar_tensor_tensor(rank[:], rank_b[:], float(NF * CAP - CAP), ranks, ALU.mult, ALU.add))
                link(dve.tensor_tensor(rank[:], rank[:], over_tiles(small[:, C_SLOT:C_SLOT + NF], NF), ALU.add))
                dve.tensor_tensor(pick[:, 0, :, :], rank[:], oh1[:], ALU.mult)
                link(dve.tensor_tensor(pick[:, 1, :, :], rank[:], oh2[:], ALU.mult))
                link(dve.tensor_reduce(slot_f[:].rearrange("p c t -> p (c t)"), pick[:].rearrange("p c t n -> p (c t) n"), AX.X, ALU.add))
                dve.tensor_copy(slot_of[:], slot_f[:]).then_inc(slots_set, 1)

            def gu_lo_half(r, j, n1):
                dve.wait_ge(gu_hi_set, 2 * n1 + j + 1)
                dve.tensor_tensor(gu_lo[:, 4 * j:4 * j + 4, :], gu_raw[r][:, 4 * j:4 * j + 4, :, :].rearrange("p k a n -> p k (a n)"),
                                  gu_hi[:, 4 * j:4 * j + 4, :].bitcast(f32), ALU.subtract).then_inc(gu_lo_set, 1)

            def xgT_low(n1):
                for j in range(2):
                    dve.wait_ge(xgT_hi_set, 2 * n1 + j + 1)
                    dve.tensor_tensor(xgT_lo[:, 4 * j:4 * j + 4, :].rearrange("p k n -> p (k n)"), bank[2 + j][:, :],
                                      xgT_hi[:, 4 * j:4 * j + 4, :].rearrange("p k n -> p (k n)").bitcast(f32), ALU.subtract).then_inc(xgT_lo_set, 1)

            def y_rows_out(n2, p2, k2):
                dve.wait_ge(dn_done, n2 + 1)
                ge(dve, y_out[p2], 16 * k2)
                dve.tensor_copy(y_sb[:, p2, 0:512], bank[5][:, :])
                dve.tensor_copy(y_sb[:, p2, 512:], bank[6][:, :]).then_inc(y_set, 1)

            def step(l, e, n, k, p, ring):
                if l == 0:
                    gu_lo_half(ring(0)[0], 0, n)
                    gu_lo_half(ring(0)[0], 1, n)
                    xgT_low(n)
                if l != 0:
                    pp, kp = slot(p, k, -1)
                    dve.wait_ge(silu_set, n)
                    ge(dve, hid_tr, n - 1)
                    dve.tensor_tensor(hid[:], act_g[:], bank[pp][:, FE:2 * FE], ALU.mult).then_inc(hid_set, 1)
                if l is None or l >= 2:
                    y_rows_out(n - 2, p, k - 1)
                if l != 0:
                    dve.wait_ge(hidT_hi_set, n)
                    dve.tensor_tensor(hidT_lo[:].rearrange("p k n -> p (k n)"), bank[4][:, 0:2 * P],
                                      hidT_hi[:].rearrange("p k n -> p (k n)").bitcast(f32), ALU.subtract).then_inc(hidT_lo_set, 1)
                if l is None or l < NF - 1:
                    gu_lo_half(ring(1)[0], 0, n + 1)
                if l is None or l < NF - 1:
                    xgT_low(n + 1)
                    gu_lo_half(ring(1)[0], 1, n + 1)
                if l == NF:
                    pp, kp = slot(p, k, -1)
                    y_rows_out(n - 1, pp, kp)

            all_blocks(dve, step, place_all)
            for t in range(NT + 2):
                if t < NT:
                    if t - 3 in BY_POOL:
                        dve.wait_ge(e_scaled, BY_POOL.index(t - 3) + 1)
                    elif t >= 3:
                        wait_finished(dve, t - 3)
                    dve.wait_ge(yp_loaded[t], 32)
                    dve.scalar_tensor_tensor(fin[:, t % 3, :], y_pair[:, t, 0, :], mix_w[:, 0, t:t + 1], h[:, t, :], ALU.mult, ALU.add).then_inc(e_one, 1)
                    dve.wait_ge(e_one, t + 1)
                    dve.scalar_tensor_tensor(fin[:, t % 3, :], y_pair[:, t, 1, :], mix_w[:, 1, t:t + 1], fin[:, t % 3, :], ALU.mult, ALU.add).then_inc(e_two, 1)
                if t >= 2 and t - 2 not in BY_POOL:
                    u = t - 2
                    dve.wait_ge(e_rs, u + 1)
                    if u == 1:
                        dve.wait_ge(gfin_in, 16)
                    dve.scalar_tensor_tensor(o_fin[:, u, :], fin[:, u % 3, :], ss_e[:, u:u + 1], g_fin[:], ALU.mult, ALU.mult).then_inc(e_set, 1)

        @block.gpsimd
        def _(pool):
            rms_count = [0]

            def rms(ss, ready, value, done, n):
                pool.wait_ge(ready, value)
                pool.tensor_scalar(ss, ss, 1.0 / n, EPS, ALU.mult, ALU.add).then_inc(rms_mid, 1)
                rms_count[0] += 1
                pool.wait_ge(rms_mid, rms_count[0])
                e = half_neg[:, 0:1] if ss.shape[1] == 1 else half_neg[:, 0:1].broadcast_to(list(ss.shape))
                pool.tensor_tensor(ss, ss, e, ALU.pow).then_inc(done, 1)

            def gain_w(w):
                pool.wait_ge(w_loaded[w % 2], 16 * (w // 2 + 1))
                pool.tensor_tensor(w_raw[:, w % 2, :, :], w_raw[:, w % 2, :, :], g_mix.unsqueeze(2).broadcast_to([P, KD, 256]), ALU.mult)\
                    .then_inc(w_gained, 1)

            def gain_first(j):
                pool.wait_ge(w_loaded[0], 16)
                rows = slice(4 * j, 4 * j + 4)
                last = pool.tensor_tensor(w_raw[:, 0, rows, :], w_raw[:, 0, rows, :], g_mix[:, rows].unsqueeze(2).broadcast_to([P, 4, 256]), ALU.mult)
                if j == 1:
                    last.then_inc(w_gained, 1)

            pool.wait_ge(init_set, HALVES)
            for t in range(NT):
                rms(ss_x[:, t:t + 1], x_sq, t + 1, x_rs, D)
                if t == 2:
                    pool.wait_ge(cols_set, 1)
                if t in (2, 3):
                    gain_first(t - 2)
            for w in range(1, len(CHUNKS)):
                gain_w(w)

            def gain_wo(i):
                n, c = i // KD, i % KD
                pool.wait_ge(wo_loaded[i % 3], 16 * (i // 3 + 1))
                pool.tensor_scalar(wo_raw[:, i % 3, :], wo_raw[:, i % 3, :], g_merged[:, c:c + 1], None, ALU.mult).then_inc(wo_gained, 1)

            pool.wait_ge(bias_in, 16 * (QR + 1))
            for m in range(M):
                q, hd = m // HEADS, m % HEADS
                a, b = QT[q]
                if m >= 3:
                    pool.wait_ge(s_shift, m - 2)
                z = hd * RPB_R * RPB_C + (RPB_R // 2 - 4 * a) * RPB_C + (COL_BASE[b] - QC * b) + RPB_C // 2 - Z0
                view = bass.AP(bias_g, z, [[G_LEN, P], [RPB_C, KR], [1, KC]])
                pool.tensor_tensor(bm[:, m % 3, :].rearrange("p (r w) -> p r w", w=KC), mask[:, q, :].rearrange("p (r w) -> p r w", w=KC),
                                   view, ALU.subtract).then_inc(bm_set, 1)
                if m == 6:
                    rms(ss_f[:], f_moved, 1, f_rs, DM)
                if q and hd == 6:
                    rms(ss_o[:, q - 1:q], o_sq, q, o_rs, DM)
                if m >= 12 and m % 6 == 0 and (m - 12) // 6 < KD:
                    gain_wo((m - 12) // 6)
            rms(ss_o[:, 7:8], o_sq, 8, o_rs, DM)
            for i in range(KD, 2 * KD):
                gain_wo(i)
            pool.wait_ge(wo_done, 2 * NT)
            pool.memset(zero_i[:], 0).then_inc(vals_set, 1)
            pool.iota(slot_val[:, :, :, 0], pattern=[[P, NT], [0, 2]], base=0, channel_multiplier=1).then_inc(vals_set, 1)
            pool.iota(slot_val[:, :, :, 1], pattern=[[P, NT], [T, 2]], base=0, channel_multiplier=1).then_inc(vals_set, 1)
            for t in range(NT):
                rms(ss_h[:, t:t + 1], h_sq, t + 1, h_rs, D)
            pool.wait_ge(slotc_in, 16)
            pool.wait_ge(oh_set, 1)
            for c, one_hot in enumerate((oh1, oh2)):
                pool.tensor_scalar(sel[:, c, :, 0, :], one_hot[:], slot_c[:, S_ROW:S_ROW + 1], None, ALU.mult).then_inc(sel_set, 1)
                tiles = slot_c[:, S_TILE + c * NT:S_TILE + (c + 1) * NT].unsqueeze(2).broadcast_to([P, NT, NF])
                pool.tensor_tensor(sel[:, c, :, 1, :], one_hot[:], tiles, ALU.mult).then_inc(sel_set, 1)

            def scatter_slots():
                pool.wait_ge(filled, 16)
                pool.wait_ge(slots_set, 1)
                pool.wait_ge(vals_set, 3)
                for t in range(NT):
                    for c in range(2):
                        pool.indirect_dma_start(slot_dram, bass.IndirectOffsetOnAxis(ap=slot_of[:, c, t:t + 1], axis=0), slot_val[:, t, c, :], None)\
                            .then_inc(slots_scattered, 16)

            def gather(e2, n2, p2, k2):
                pool.tensor_tensor(idx_x[:, p2, :], slot_all[:, e2, 0:1], zero_i[:], ALU.add).then_inc(idxx_set, 1)
                pool.wait_ge(idxx_set, n2 + 1)
                pool.sem_inc(idx_seen, 1)
                pool.indirect_dma_start(xg[:, p2, :], None, hn_dram, bass.IndirectOffsetOnAxis(ap=idx_x[:, p2, :], axis=0),
                                        bounds_check=T - 1, oob_is_err=False).then_inc(xg_in[p2], 16)

            def scatter(e2, n2, p2, k2):
                pool.wait_ge(y_set, n2 + 1)
                ge(pool, y_out[p2], 16 * k2)
                pool.tensor_tensor(idx_y[:, p2, :], slot_all[:, e2, 1:2], zero_i[:], ALU.add).then_inc(idxy_set, 1)
                pool.wait_ge(idxy_set, n2 + 1)
                pool.sem_inc(idx_seen, 1)
                pool.indirect_dma_start(y_dram, bass.IndirectOffsetOnAxis(ap=idx_y[:, p2, :], axis=0), y_sb[:, p2, :], None,
                                        bounds_check=2 * T - 1, oob_is_err=False).then_inc(y_out[p2], 16)

            def dn_low(n1, p1, r):
                pool.wait_ge(dn_hi_set, n1 + 1)
                pool.tensor_tensor(dn_lo[:, p1, :, :], dn_raw[r][:], dn_hi[:, p1, :, :].bitcast(f32), ALU.subtract).then_inc(dn_lo_set, 1)

            def step(l, e, n, k, p, ring):
                if l == 0:
                    if isinstance(n, int):
                        pool.wait_ge(table_set, 2)
                        pool.wait_ge(vals_set, 1)
                    else:
                        pool.wait_ge(slots_loaded, n // NF * 16)
                    gather(e, n, p, k)
                    pn, kn = slot(p, k, 1)
                    gather(e + 1, n + 1, pn, kn)
                if l == 0:
                    dn_low(n, p, ring(0)[0])
                if l is None or l + 2 < NF:
                    pool.wait_ge(xg_tr, n + 1)
                    gather(e + 2, n + 2, p, k + 1)
                if l is None or l >= 2:
                    scatter(e - 2, n - 2, p, k - 1)
                if l != 0 and (l is None or l < NF):
                    dn_low(n, p, ring(0)[0])
                if l == NF:
                    pp, kp = slot(p, k, -1)
                    scatter(e - 1, n - 1, pp, kp)

            pool.wait_ge(xg_zero, 1)
            for i in range(2):
                pool.wait_ge(hn_stored[i], 64)
            all_blocks(pool, step, scatter_slots)
            for t in range(NT):
                rms(ss_e[:, t:t + 1], e_sq, t + 1, e_rs, D)
                if t - 1 in BY_POOL:
                    if t == 1:
                        pool.wait_ge(gfin_in, 16)
                    pool.wait_ge(e_scaled, BY_POOL.index(t - 1) + 1)
                    pool.tensor_tensor(o_fin[:, t - 1, :], o_fin[:, t - 1, :], g_fin[:], ALU.mult).then_inc(e_pool, 1)

        @block.tensor
        def _(pe):
            pe.wait_ge(consts_in, 80)
            pe.transpose(bank[7][:, 0:20], rows20[:], ident[0:20, 0:20]).then_inc(cols_tr, 1)
            def x_T(t):
                pe.wait_ge(x_scaled, t + 1)
                for j in range(2):
                    if t >= 2:
                        pe.wait_ge(x_lo, 2 * (t - 2) + j + 1)
                    for k in range(4):
                        d = 4 * j + k
                        last = pe.transpose(x_bank(t, j)[:, k * P:(k + 1) * P], x_in[:, t, d * P:(d + 1) * P], ident)
                    last.then_inc(x_tr, 1)

            for t in range(6):
                x_T(t)
            pe.wait_ge(x_lo, 8)
            seen = -1
            for g, (w, kind, s, half) in enumerate(GROUPS):
                if g == 1:
                    x_T(6)
                    x_T(7)
                if g == 2:
                    pe.wait_ge(x_lo, 2 * NT)
                if g == 8:
                    pe.wait_ge(wbd_in, 16 * FG)
                    for i, c in enumerate((C_CC, C_SC)):
                        pe.matmul(bank[6 + i][:, :], small[:, c:c + P], w_bd[:].rearrange("p c n -> p (c n)"), start=True, stop=True).then_inc(m_done, 1)
                if w != seen:
                    pe.wait_ge(w_lo_set, w + 1)
                    seen = w
                if g >= 4:
                    wait_evacuated(pe, g - 4)
                for k in range(KD):
                    first, last = k == 0, k == KD - 1
                    if kind == "v":
                        tok = slice(half * P, (half + 1) * P)
                        done = three(pe, bank[g % 4][:, 0:256], xT_hi[:, k, tok], xT_lo[:, k, tok],
                                     w_hi[:, w % 2, k, :], w_lo[:, w % 2, k, :], first, last)
                    else:
                        tok, col = slice(512 * half, 512 * half + 512), slice(P * s, P * s + P)
                        done = three(pe, bank[g % 4][:, :], w_hi[:, w % 2, k, col], w_lo[:, w % 2, k, col],
                                     xT_hi[:, k, tok], xT_lo[:, k, tok], first, last)
                done.then_inc(proj_done, 1)
            pe.wait_ge(m_set, 2)
            pe.wait_ge(init_set, ODD_ZERO)
            pe.wait_ge(folded, 2 * NC)
            for i in range(8):
                odd, r = i // 4, i % 4
                if odd:
                    pe.wait_ge(f1_act, r + 1)
                src = ((u_ee, u_even), (u_oe, u_odd))[odd][r // 2]
                tok = slice(r % 2 * P, (r % 2 + 1) * P)
                for c in range(NC):
                    last = pe.matmul(bank[4 + r][:, c * P:(c + 1) * P], src[:, c, tok], m_chan[:, odd, c, :], start=True, stop=True)
                last.then_inc(f1_done, 1)
            for i, src in enumerate((u_even, u_odd)):
                wait_evacuated(pe, 36 + i)
                for c in range(NC):
                    last = pe.matmul(bank[i][0:1, c * P:(c + 1) * P], src[:, c, QUARTER:QUARTER + 1], m_chan[:, i, c, :], start=True, stop=True)
                last.then_inc(amid_done, 1)
            pe.wait_ge(dft_in, 32)
            pe.wait_ge(amid_set, 2)
            for g in (38, 39):
                wait_evacuated(pe, g)
            pe.wait_ge(f1_act, 4)
            pe.wait_ge(f1_dve, 1)
            for c in range(NC):
                col = slice(c * P, (c + 1) * P)
                for i in range(2):
                    pe.matmul(bank[4][:, c:c + 1], a_even[:, i, col], small[:, C_ALT:C_ALT + 1], start=(i == 0), stop=False)
                last = pe.matmul(bank[4][:, c:c + 1], a_mid[0:1, 0, col], altrow[0:1, 0:1], start=False, stop=True)
            last.then_inc(f_mid, 1)

            def positions(dst, rows, odd, col):
                for q in range(2):
                    part = dst[:, q * QUARTER:(q + 1) * QUARTER]
                    for i in range(2):
                        last = pe.matmul(part, rows[:, 2 * q + i, col], dft[:, odd, q, i, :], start=(i == 0), stop=(i == 1 and q != odd))
                    if q == odd:
                        last = pe.matmul(part, a_mid[0:1, odd, col], altrow[0:1, 0:QUARTER], start=False, stop=True)
                last.then_inc(f2_done, 1)

            for c in range(NC):
                col = slice(c * P, (c + 1) * P)
                if c >= 2:
                    pe.wait_ge(f2_tmp, c - 1)
                positions(bank[2 * (c % 2)], a_even, 0, col)
                pe.wait_ge(f1_dve, 4)
                if c >= 2:
                    pe.wait_ge(f2_dve, c - 1)
                positions(bank[2 * (c % 2) + 1], b_odd, 1, col)

            def scores(m):
                q, hd = m // HEADS, m % HEADS
                a, b = QT[q]
                rows = slice(DH * (hd % 2), DH * (hd % 2) + DH)
                if m >= 3:
                    pe.wait_ge(s_shift, m - 2)
                grid_k = kT[rows, hd // 2, :].rearrange("p (r w) -> p r w", w=GRID_W)
                pe.matmul(bank[m % 3][:, 0:NK].rearrange("p (r w) -> p r w", w=KC), qT[rows, hd // 2, q * P:(q + 1) * P],
                          grid_k[:, 4 * a:4 * a + KR, COL_BASE[b]:COL_BASE[b] + KC], start=True, stop=True).then_inc(s_done, 1)

            def probs_T(m):
                pe.wait_ge(p_set, m + 1)
                if m >= 2:
                    wait_pT(pe, m - 2)
                for j in range(3):
                    last = pe.transpose(bank[3 + m % 2][:, j * P:(j + 1) * P], p_sb[:, m % 2, j * P:(j + 1) * P], ident)
                last.then_inc(p_tr, 1)

            def values(m):
                q, hd = m // HEADS, m % HEADS
                a, b = QT[q]
                if m == 0:
                    pe.wait_ge(vk_in, 16 * 32)
                if q >= 2 and hd == 0:
                    pe.wait_ge(o_normed, q - 1)
                wait_pT(pe, m)
                part = slice(hd * DH, min((hd + 2) * DH, DM))
                for j in range(3):
                    last = pe.matmul(bank[5 + q % 2][:, part], pT[:, m % 2, j * P:(j + 1) * P],
                                     vk[:, 4 * (a + j) + b, part], start=(j == 0), stop=(j == 2))
                last.then_inc(pv_done, 1)

            def o_T(q):
                pe.wait_ge(o_scaled, q + 1)
                if q:
                    pe.wait_ge(oT_set, q)
                for c in range(NC):
                    last = pe.transpose(bank[7][:, c * P:(c + 1) * P], o_sb[:, q % 2, c * P:(c + 1) * P], ident)
                last.then_inc(o_tr, 1)

            for m in range(-2, M + 1):
                if m == -2:
                    pe.wait_ge(f2_tmp, NC - 1)
                if m == -1:
                    pe.wait_ge(f2_dve, NC - 1)
                if m == 0:
                    pe.wait_ge(f2_tmp, NC)
                if m + 2 < M:
                    scores(m + 2)
                if m == 0:
                    pe.wait_ge(f2_dve, NC)
                if 0 <= m < M:
                    probs_T(m)
                if m >= 1:
                    values(m - 1)
                if m == 3:
                    pe.wait_ge(y_summed, NC - 1)
                    pe.wait_ge(init_set, ONES)
                    for t in range(NT):
                        last = pe.matmul(bank[7][:, t:t + 1], y_sq[:, 0, t * P:(t + 1) * P], ones_col[:], start=True, stop=True)
                    last.then_inc(f_ssum, 1)
                if m >= 8 and m % 8 == 7 and m < M:
                    o_T(m // 8 - 1)
            for i in range(2 * NT):
                n, t = i // NT, i % NT
                tok = slice(t * P, (t + 1) * P)
                if n == 0:
                    pe.wait_ge(m_lo_set, t + 1)
                if i >= 2:
                    pe.wait_ge(h_set, i - 1)
                for part in range(2):
                    for k in range(4):
                        c = 4 * part + k
                        if t == 0:
                            pe.wait_ge(wo_lo_set, KD * n + c + 1)
                        last = three(pe, bank[2 * (i % 2) + part][:, :], mT_hi[:, c, tok], mT_lo[:, c, tok],
                                     wo_hi[n][:, c, :], wo_lo[n][:, c, :], k == 0, k == 3)
                    last.then_inc(wo_done, 1)
                if i == 0:
                    o_T(7)

                def hn_T(u):
                    pe.wait_ge(hn_set, u + 1)
                    for j in range(2):
                        if u and j == 0:
                            pe.wait_ge(hT_set_act, u)
                        if u and j == 1:
                            pe.wait_ge(hT_set, u)
                        for k in range(4):
                            d = 4 * j + k
                            last = pe.transpose(bank[4 + j][:, k * P:(k + 1) * P], hn[:, u % 2, d * P:(d + 1) * P], ident)
                        last.then_inc(h_tr, 1)

                def route(u):
                    pe.wait_ge(hT_set_act, u + 1)
                    pe.wait_ge(hT_set, u + 1)
                    pe.wait_ge(router_in, 64)
                    for k in range(KD):
                        last = pe.matmul(bank[6][:, u * (NG + NF):(u + 1) * (NG + NF)], hT[:, u % 2, k, :], w_r[:, k, :],
                                         start=(k == 0), stop=(k == KD - 1))
                    last.then_inc(r_done, 1)

                if n == 1 and t >= 1:
                    hn_T(t - 1)
                if n == 1 and t >= 2:
                    route(t - 2)
            route(NT - 2)
            hn_T(NT - 1)
            route(NT - 1)
            pe.wait_ge(oh_set, 1)
            pe.wait_ge(init_set, TRI)
            for t in range(NT + 1):
                dst = bank[7][:, t * NF:(t + 1) * NF]
                for u in range(min(t + 1, NT)):
                    last = pe.matmul(dst, tri_ones[:, 0 if u == t else 1, :], oh[:, u, :], start=(u == 0), stop=(u == min(t, NT - 1)))
            last.then_inc(rank_done, 1)
            pe.wait_ge(sel_set, 4)
            for c in range(2):
                pe.wait_ge(in_slot_set, c + 1)
                for t in range(NT):
                    last = pe.matmul(bank[6][:, 0:2 * NF], in_slot[:, c, t, :], sel[:, c, t, :, :].rearrange("p a e -> p (a e)"),
                                     start=(c == 0 and t == 0), stop=(c == 1 and t == NT - 1))
            last.then_inc(table_done, 1)

            def x_T(n1, p1, k1):
                pe.wait_ge(xg_in[p1], 16 * (k1 + 1))
                ge(pe, xgT_lo_set, 2 * n1)
                for d in range(KD):
                    last = pe.transpose(bank[2 + d // 4][:, d % 4 * P:(d % 4 + 1) * P], xg[:, p1, d * P:(d + 1) * P], ident)
                last.then_inc(xg_tr, 1)

            def gate_up(n, p, j):
                pe.wait_ge(gu_lo_set, 2 * n + j + 1)
                for k in range(4):
                    d = 4 * j + k
                    last = three(pe, bank[p][:, :], xgT_hi[:, d, :], xgT_lo[:, d, :], gu_hi[:, d, :], gu_lo[:, d, :], d == 0, d == KD - 1)
                last.then_inc(gu_done if j else gu_half, 1)

            def step(l, e, n, k, p, ring):
                if l == 0:
                    x_T(n, p, k)
                more = l is None or l < NF
                if more:
                    pe.wait_ge(xgT_lo_set, 2 * n + 2)
                    ge(pe, hid_set, n - 1)
                    gate_up(n, p, 0)
                if l != 0:
                    pe.wait_ge(hid_set, n)
                    ge(pe, hidT_lo_set, n - 1)
                    for c in range(2):
                        last = pe.transpose(bank[4][:, c * P:(c + 1) * P], hid[:, c * P:(c + 1) * P], ident)
                    last.then_inc(hid_tr, 1)
                if more:
                    gate_up(n, p, 1)
                if l is None or l < NF - 1:
                    pn, kn = slot(p, k, 1)
                    x_T(n + 1, pn, kn)
                if l != 0:
                    pe.wait_ge(hidT_lo_set, n)
                    pe.wait_ge(dn_lo_set, n)
                    ge(pe, y_set, n - 1)
                    pp = (p + 1) % 2
                    for c in range(2):
                        for half in range(2):
                            cols_ = slice(512 * half, 512 * half + 512)
                            last = three(pe, bank[5 + half][:, :], hidT_hi[:, c, :], hidT_lo[:, c, :],
                                         dn_hi[:, pp, c, cols_], dn_lo[:, pp, c, cols_], c == 0, c == 1)
                    last.then_inc(dn_done, 1)

            all_blocks(pe, step)


_INPUTS = ("x", "norm_mix", "w_in", "rpb", "w_four", "b_four", "g_attn_out", "g_four_out", "w_out", "norm_moe",
           "w_router_coarse", "b_router_coarse", "w_router_fine", "b_router_fine", "w_gate", "w_up", "w_down", "norm_final")


def kernel(**inputs):
    import concourse.bacc as bacc
    from concourse.bass_utils import run_bass_kernel_spmd

    nc = bacc.Bacc("TRN2", target_bir_lowering=False, num_devices=1)
    arrays = {name: np.ascontiguousarray(inputs[name]) for name in _INPUTS}
    arrays.update(constants())
    io = {name: nc.dram_tensor(name, a.shape, mybir.dt.float32, kind="ExternalInput").ap() for name, a in arrays.items()}
    out = nc.dram_tensor("out", (1, T, D), mybir.dt.float32, kind="ExternalOutput").ap()
    build(nc, io, out)
    result = run_bass_kernel_spmd(nc, [arrays], core_ids=[0])
    return result.results[0]["out"]
```
